# Optimizing a Trainium2 kernel written in Bass

```python
import jax, jax.numpy as jnp
from jax import lax
import numpy as np

D_MODEL = 1024
BATCH = 1
SEQ = 256
DEPTH = 2

GRID_W = 64
RET_HEADS = 4
RET_DK = 128
RET_DV = 256
NA_HEADS = 16
NA_DH = 64
NA_WIN_ROWS = 8
NA_WIN_COLS = 16
ML_HEADS = 4
ML_DK = 128
ML_DV = 256
ML_CONV_W = 5
CHUNK = 128
D_FF = -(-8 * D_MODEL // (3 * 256)) * 256
ROPE_BASE = 10000.0
EPS = 1e-6
N_BRANCH = 3
RET_QK = RET_HEADS * RET_DK
RET_V = RET_HEADS * RET_DV
NA_W = NA_HEADS * NA_DH
ML_QK = ML_HEADS * ML_DK
ML_V = ML_HEADS * ML_DV
IN_SPLITS = (RET_QK, RET_QK, RET_V, RET_V, NA_W, NA_W, NA_W, ML_QK, ML_QK, ML_V, ML_V, 4 * ML_HEADS, N_BRANCH * D_MODEL)
IN_W = sum(IN_SPLITS)

kernel_name = "hybrid_retention_natten_mlstm_encoder"

def rmsnorm(x, g):
    xf = x.astype(jnp.float32)
    y = xf * lax.rsqrt(jnp.mean(xf * xf, axis=-1, keepdims=True) + EPS)
    return (y * g.astype(jnp.float32)).astype(x.dtype)

def head_layernorm(x):
    xf = x.astype(jnp.float32)
    mu = jnp.mean(xf, axis=-1, keepdims=True)
    xc = xf - mu
    return xc * lax.rsqrt(jnp.mean(xc * xc, axis=-1, keepdims=True) + EPS)

def split_heads(t, heads):
    B, T, _ = t.shape
    return t.reshape(B, T, heads, -1).transpose(0, 2, 1, 3)

def merge_heads(t):
    B, H, T, d = t.shape
    return t.transpose(0, 2, 1, 3).reshape(B, T, H * d)

def rotary(x, cos, sin):
    x1, x2 = jnp.split(x, 2, axis=-1)
    return jnp.concatenate([x1 * cos - x2 * sin, x1 * sin + x2 * cos], axis=-1)

def retention_dir(q, k, v, log_gamma, include_diag):
    B, H, T, dk = q.shape
    dv = v.shape[-1]
    nc = T // CHUNK
    qc = q.reshape(B, H, nc, CHUNK, dk)
    kc = k.reshape(B, H, nc, CHUNK, dk)
    vc = v.reshape(B, H, nc, CHUNK, dv)
    pos = jnp.arange(CHUNK, dtype=jnp.float32)
    diff = pos[:, None] - pos[None, :]
    mask = (diff >= 0) if include_diag else (diff > 0)
    decay = jnp.where(mask, jnp.exp(log_gamma[:, None, None] * jnp.maximum(diff, 0.0)), 0.0)
    s = jnp.einsum('bhcid,bhcjd->bhcij', qc, kc) * decay[:, None]
    o_intra = jnp.einsum('bhcij,bhcje->bhcie', s, vc)
    k_w = kc * jnp.exp(log_gamma[:, None] * (CHUNK - 1 - pos))[:, None, :, None]
    s_chunk = jnp.einsum('bhcjd,bhcje->bhcde', k_w, vc)
    chunk_decay = jnp.exp(log_gamma * CHUNK)[None, :, None, None]

    def step(R, S):
        return chunk_decay * R + S, R

    _, r_prev = lax.scan(step, jnp.zeros((B, H, dk, dv), s_chunk.dtype), jnp.moveaxis(s_chunk, 2, 0))
    r_prev = jnp.moveaxis(r_prev, 0, 2)
    q_w = qc * jnp.exp(log_gamma[:, None] * (pos + 1.0))[:, None, :, None]
    o_inter = jnp.einsum('bhcid,bhcde->bhcie', q_w, r_prev)
    return (o_intra + o_inter).reshape(B, H, T, dv)

def retention_branch(rq, rk, rv, rg, decay_logit, cos, sin):
    B, T, _ = rq.shape
    q = rotary(split_heads(rq, RET_HEADS), cos, sin) * (RET_DK ** -0.5)
    k = rotary(split_heads(rk, RET_HEADS), cos, sin)
    v = split_heads(rv, RET_HEADS)
    lg_f = jax.nn.log_sigmoid(decay_logit[0].astype(jnp.float32))
    lg_b = jax.nn.log_sigmoid(decay_logit[1].astype(jnp.float32))
    fwd = retention_dir(q, k, v, lg_f, True)
    bwd = jnp.flip(retention_dir(jnp.flip(q, 2), jnp.flip(k, 2), jnp.flip(v, 2), lg_b, False), 2)
    y = merge_heads(head_layernorm(fwd + bwd)).astype(rg.dtype)
    return jax.nn.silu(rg) * y

def neighbourhood_attention(q, k, v, rpb):
    B, T, _ = q.shape
    rows = T // GRID_W
    wr = min(NA_WIN_ROWS, rows)
    wc = NA_WIN_COLS

    def grid(t):
        return t.reshape(B, rows, GRID_W, NA_HEADS, NA_DH).transpose(0, 3, 1, 2, 4)

    qg = jnp.moveaxis(grid(q), 2, 0)
    kg, vg = grid(k), grid(v)
    col = jnp.arange(GRID_W)
    col_idx = jnp.clip(col - wc // 2, 0, GRID_W - wc)[:, None] + jnp.arange(wc)[None, :]
    col_rel = col_idx - col[:, None] + (NA_WIN_COLS - 1)
    rpb_cols = rpb[:, :, col_rel]
    scale = NA_DH ** -0.5

    def row_block(args):
        r, q_r = args
        rs = jnp.clip(r - wr // 2, 0, rows - wr)
        k_r = lax.dynamic_slice_in_dim(kg, rs, wr, axis=2)[:, :, :, col_idx]
        v_r = lax.dynamic_slice_in_dim(vg, rs, wr, axis=2)[:, :, :, col_idx]
        row_rel = rs + jnp.arange(wr) - r + (NA_WIN_ROWS - 1)
        bias = rpb_cols[:, row_rel].transpose(0, 2, 1, 3)
        s = jnp.einsum('bhqd,bhrqjd->bhqrj', q_r, k_r).astype(jnp.float32) * scale + bias.astype(jnp.float32)
        p = jax.nn.softmax(s.reshape(B, NA_HEADS, GRID_W, wr * wc), axis=-1)
        p = p.reshape(B, NA_HEADS, GRID_W, wr, wc).astype(v_r.dtype)
        return jnp.einsum('bhqrj,bhrqjd->bhqd', p, v_r)

    out = lax.map(row_block, (jnp.arange(rows), qg))
    return out.transpose(1, 0, 3, 2, 4).reshape(B, T, NA_W)

def centred_depthwise_conv(x, w, b):
    K, C = w.shape
    out = lax.conv_general_dilated(x, w[:, None, :], window_strides=(1,), padding=[(K // 2, K // 2)],
                                   dimension_numbers=('NWC', 'WIO', 'NWC'), feature_group_count=C)
    return out + b

def mlstm_dir(q, k, v, i_pre, log_f):
    B, H, T, dk = q.shape
    dv = v.shape[-1]
    nc = T // CHUNK
    qc = q.reshape(B, H, nc, CHUNK, dk)
    kc = k.reshape(B, H, nc, CHUNK, dk)
    vc = v.reshape(B, H, nc, CHUNK, dv)
    ic = i_pre.reshape(B, H, nc, CHUNK)
    b = jnp.cumsum(log_f.reshape(B, H, nc, CHUNK), axis=-1)
    pos = jnp.arange(CHUNK)
    causal = pos[:, None] >= pos[None, :]
    d_log = jnp.where(causal, b[..., :, None] - b[..., None, :] + ic[..., None, :], -jnp.inf)
    b_last = b[..., -1]
    a = b_last[..., None] - b + ic
    m_loc = jnp.max(a, axis=-1)
    w = jnp.exp(a - m_loc[..., None])
    c_loc = jnp.einsum('bhcj,bhcjd,bhcje->bhcde', w, kc, vc)
    n_loc = jnp.einsum('bhcj,bhcjd->bhcd', w, kc)

    def step(carry, xs):
        C, n, m = carry
        bl, ml, cl, nl = xs
        m_new = jnp.maximum(bl + m, ml)
        s_old = jnp.exp(bl + m - m_new)
        s_new = jnp.exp(ml - m_new)
        C_new = s_old[..., None, None] * C + s_new[..., None, None] * cl
        n_new = s_old[..., None] * n + s_new[..., None] * nl
        return (C_new, n_new, m_new), (C, n, m)

    init = (jnp.zeros((B, H, dk, dv), c_loc.dtype), jnp.zeros((B, H, dk), n_loc.dtype),
            jnp.full((B, H), -jnp.inf, jnp.float32))
    xs = (jnp.moveaxis(b_last, 2, 0), jnp.moveaxis(m_loc, 2, 0), jnp.moveaxis(c_loc, 2, 0), jnp.moveaxis(n_loc, 2, 0))
    _, (c_prev, n_prev, m_prev) = lax.scan(step, init, xs)
    c_prev = jnp.moveaxis(c_prev, 0, 2)
    n_prev = jnp.moveaxis(n_prev, 0, 2)
    m_prev = jnp.moveaxis(m_prev, 0, 2)
    g = b + m_prev[..., None]
    m_t = jnp.maximum(g, jnp.max(d_log, axis=-1))
    s_inter = jnp.exp(g - m_t)
    s = jnp.einsum('bhcid,bhcjd->bhcij', qc, kc) * jnp.exp(d_log - m_t[..., None])
    num = s_inter[..., None] * jnp.einsum('bhcid,bhcde->bhcie', qc, c_prev) + jnp.einsum('bhcij,bhcje->bhcie', s, vc)
    den = s_inter * jnp.einsum('bhcid,bhcd->bhci', qc, n_prev) + jnp.sum(s, axis=-1)
    h = num / jnp.maximum(jnp.abs(den), jnp.exp(-m_t))[..., None]
    return h.reshape(B, H, T, dv)

def mlstm_branch(mq, mk, mv, mo, mgate, conv_w, conv_b, gate_b, norm_g):
    B, T, _ = mq.shape
    qk = jax.nn.silu(centred_depthwise_conv(jnp.concatenate([mq, mk], axis=-1), conv_w, conv_b))
    q_in, k_in = jnp.split(qk, 2, axis=-1)
    q = split_heads(q_in, ML_HEADS) * (ML_DK ** -0.5)
    k = split_heads(k_in, ML_HEADS)
    v = split_heads(mv, ML_HEADS)
    pre = mgate.astype(jnp.float32).reshape(B, T, 2, 2, ML_HEADS) + gate_b.astype(jnp.float32)
    pre = pre.transpose(2, 3, 0, 4, 1)
    fwd = mlstm_dir(q, k, v, pre[0, 0], jax.nn.log_sigmoid(pre[0, 1]))
    bwd = mlstm_dir(jnp.flip(q, 2), jnp.flip(k, 2), jnp.flip(v, 2),
                    jnp.flip(pre[1, 0], -1), jnp.flip(jax.nn.log_sigmoid(pre[1, 1]), -1))
    h = merge_heads(head_layernorm(fwd + jnp.flip(bwd, 2))) * norm_g.astype(jnp.float32)
    return jax.nn.sigmoid(mo) * h.astype(mo.dtype)

def setup_inputs(seed: int = 0) -> dict:
    key = jax.random.key(seed)
    ks = jax.random.split(key, 24)
    f32 = jnp.float32

    def nrm(k, shape, scale):
        return jax.random.normal(k, shape, f32) * scale

    x = nrm(ks[0], (BATCH, SEQ, D_MODEL), 1.0)
    norm1_g = 1.0 + nrm(ks[1], (DEPTH, D_MODEL), 0.02)
    w_in = nrm(ks[2], (DEPTH, D_MODEL, IN_W), D_MODEL ** -0.5)
    gate_b = nrm(ks[3], (DEPTH, N_BRANCH * D_MODEL), 0.02)
    ret_base = jnp.log(2.0 ** (5.0 + jnp.arange(RET_HEADS, dtype=f32)) - 1.0)
    ret_decay_logit = ret_base[None, None, :] + nrm(ks[4], (DEPTH, 2, RET_HEADS), 0.1)
    na_rpb = nrm(ks[5], (DEPTH, NA_HEADS, 2 * NA_WIN_ROWS - 1, 2 * NA_WIN_COLS - 1), 0.02)
    ml_conv_w = nrm(ks[6], (DEPTH, ML_CONV_W, 2 * ML_QK), ML_CONV_W ** -0.5)
    ml_conv_b = nrm(ks[7], (DEPTH, 2 * ML_QK), 0.02)
    i_bias = nrm(ks[8], (DEPTH, 2, 1, ML_HEADS), 0.1)
    f_bias = jnp.linspace(3.0, 6.0, ML_HEADS, dtype=f32)[None, None, None, :] + nrm(ks[9], (DEPTH, 2, 1, ML_HEADS), 0.1)
    ml_gate_b = jnp.concatenate([i_bias, f_bias], axis=2)
    ml_norm_g = 1.0 + nrm(ks[10], (DEPTH, ML_V), 0.02)
    w_ret_o = nrm(ks[11], (DEPTH, RET_V, D_MODEL), RET_V ** -0.5)
    w_na_o = nrm(ks[12], (DEPTH, NA_W, D_MODEL), NA_W ** -0.5)
    w_ml_o = nrm(ks[13], (DEPTH, ML_V, D_MODEL), ML_V ** -0.5)
    w_out = nrm(ks[14], (DEPTH, D_MODEL, D_MODEL), D_MODEL ** -0.5)
    norm2_g = 1.0 + nrm(ks[15], (DEPTH, D_MODEL), 0.02)
    w_ffn_up = nrm(ks[16], (DEPTH, D_MODEL, 2 * D_FF), D_MODEL ** -0.5)
    w_ffn_down = nrm(ks[17], (DEPTH, D_FF, D_MODEL), D_FF ** -0.5)
    final_g = 1.0 + nrm(ks[18], (D_MODEL,), 0.02)
    return {"x": x, "norm1_g": norm1_g, "w_in": w_in, "gate_b": gate_b, "ret_decay_logit": ret_decay_logit,
            "na_rpb": na_rpb, "ml_conv_w": ml_conv_w, "ml_conv_b": ml_conv_b, "ml_gate_b": ml_gate_b,
            "ml_norm_g": ml_norm_g, "w_ret_o": w_ret_o, "w_na_o": w_na_o, "w_ml_o": w_ml_o, "w_out": w_out,
            "norm2_g": norm2_g, "w_ffn_up": w_ffn_up, "w_ffn_down": w_ffn_down, "final_g": final_g}

def reference(x, norm1_g, w_in, gate_b, ret_decay_logit, na_rpb, ml_conv_w, ml_conv_b, ml_gate_b, ml_norm_g,
              w_ret_o, w_na_o, w_ml_o, w_out, norm2_g, w_ffn_up, w_ffn_down, final_g):
    B, T, _ = x.shape
    half = RET_DK // 2
    inv_freq = ROPE_BASE ** (-jnp.arange(half, dtype=jnp.float32) / half)
    ang = jnp.arange(T, dtype=jnp.float32)[:, None] * inv_freq[None, :]
    cos, sin = jnp.cos(ang), jnp.sin(ang)
    split_at = np.cumsum(IN_SPLITS)[:-1]
    for l in range(DEPTH):
        h = rmsnorm(x, norm1_g[l])
        proj = h @ w_in[l]
        (rq, rk, rv, rg, nq, nk, nv, mq, mk, mv, mo, mgate, mix_gate) = jnp.split(proj, split_at, axis=-1)
        y_ret = retention_branch(rq, rk, rv, rg, ret_decay_logit[l], cos, sin)
        y_na = neighbourhood_attention(nq, nk, nv, na_rpb[l])
        y_ml = mlstm_branch(mq, mk, mv, mo, mgate, ml_conv_w[l], ml_conv_b[l], ml_gate_b[l], ml_norm_g[l])
        gates = jax.nn.sigmoid((mix_gate + gate_b[l]).astype(jnp.float32)).astype(x.dtype)
        g_ret, g_na, g_ml = jnp.split(gates, N_BRANCH, axis=-1)
        merged = g_ret * (y_ret @ w_ret_o[l]) + g_na * (y_na @ w_na_o[l]) + g_ml * (y_ml @ w_ml_o[l])
        x = x + merged @ w_out[l]
        h2 = rmsnorm(x, norm2_g[l])
        a, u = jnp.split(h2 @ w_ffn_up[l], 2, axis=-1)
        x = x + (jax.nn.silu(a) * u) @ w_ffn_down[l]
    return rmsnorm(x, final_g)


_drawn_inputs = setup_inputs


def setup_inputs(seed=0):
    import zlib

    import numpy as np

    out = dict(_drawn_inputs(seed))
    spreads = {}
    factors = {'gate_b': 8.0,
     'na_rpb': 35.311,
     'ml_conv_b': 7.303,
     'ml_norm_g': 6.225,
     'norm2_g': 2.674,
     'final_g': 8.469}
    for name, (base, spread) in spreads.items():
        noise = np.random.default_rng([zlib.crc32(name.encode()), seed]).standard_normal(out[name].shape)
        drawn = base * np.exp(spread * noise) if base else spread * noise
        out[name] = __import__('jax').numpy.asarray(drawn.astype(out[name].dtype))
    for name, factor in factors.items():
        out[name] = (out[name] * factor).astype(out[name].dtype)
    return out
```

```python
from contextlib import ExitStack

import numpy as np
import concourse.bass as bass
from concourse import mybir

F32 = mybir.dt.float32
ALU = mybir.AluOpType
ACT = mybir.ActivationFunctionType
AX_X = mybir.AxisListType.X

P = 128
T = 256
NT = T // P
D = 1024
KD = D // P
DEPTH = 2
GRID_W = 64
ROWS = T // GRID_W
WIN_ROWS, WIN_COLS = 8, 16
RET_HEADS, NA_HEADS, ML_HEADS = 4, 16, 4
DK, DV, NA_DH = 128, 256, 64
CONV_W = 5
FF = 2816
KF = FF // P
EPS = 1e-6
QK_SCALE = float(DK) ** -0.5
NA_SCALE = float(NA_DH) ** -0.5
LOWEST = -3.0e38

RQ, RK, RV, RG, NQ, NK, NV, MQ, MK, MV, MO, MGATE, MIX = np.cumsum(
    [0, 512, 512, 1024, 1024, 1024, 1024, 1024, 512, 512, 1024, 1024, 16]).tolist()
IN_W = MIX + 3 * D

N512 = 512
UK = 4
RING = 5

IN_GROUPS = ([("nq", NQ), ("nq", NQ + N512), ("nk", NK), ("nk", NK + N512), ("nv", NV), ("nv", NV + N512),
              ("mq", MQ), ("mk", MK), ("mv", MV), ("mv", MV + N512), ("rq", RQ), ("rk", RK),
              ("rv", RV), ("rv", RV + N512), ("rg", RG), ("rg", RG + N512), ("mo", MO), ("mo", MO + N512)]
             + [("mix", MIX + j * N512) for j in range(6)])
FEATURE_MAJOR = ("nq", "nk", "mq", "mk")
G_MIX = 18
G_PROJ = len(IN_GROUPS)
BRANCHES = ("na", "ml", "ret")
G_OUT = G_PROJ + 2 * len(BRANCHES)
G_UP = G_OUT + 2
N_UP = FF // 256
G_DOWN = G_UP + N_UP
U_DOWN = 2 * G_DOWN
N_DOWN = KF // 2
UNITS = U_DOWN + N_DOWN
GATE_OF = {"ret": 0, "na": 1, "ml": 2}

U_NA = 12
U_ML = U_NA + NA_HEADS + 2
U_RET = U_ML + 9


def mixer_schedule():
    after = {}

    def put(u, *step):
        after.setdefault(u, []).append(step)

    put(3, "gate")
    put(7, "gate_turn")
    for h in range(NA_HEADS):
        put(U_NA + h, "na_scores", h)
    for h in range(NA_HEADS):
        put(U_NA + h + 1, "na_turn", h)
        put(U_NA + h + 2, "na_values", h)
    for h in range(ML_HEADS):
        put(U_ML + 2 * h, "ml_scores", h)
        put(U_ML + 2 * h + 1, "ml_values", h, 0)
        put(U_ML + 2 * h + 2, "ml_values", h, 1)
    put(U_RET, "turn", "rot")
    for h in range(RET_HEADS):
        put(U_RET + 1 + h, "ret_scores", h)
        put(U_RET + 2 + h, "ret_values", h)
    put(2 * G_PROJ - 2, "turn", "na")
    put(2 * G_PROJ + 2, "turn", "ml")
    put(2 * G_PROJ + 4, "turn", "ret")
    put(2 * G_OUT - 1, "turn", "merged")
    put(2 * G_UP - 1, "turn", "norm2")
    for c in range(N_UP):
        put(2 * (G_UP + c) + (2 if c < N_UP - 1 else 3), "up_turn", c)
    for u in after:
        after[u].sort(key=lambda s: s[0] in ("na_scores", "ml_scores", "ret_scores"))
    return after


MIXER = mixer_schedule()


def bank_uses():
    count, uses = [0] * 4, {}

    def use(bank, *name):
        count[bank] += 1
        uses[name] = (bank, count[bank])

    def turn(name):
        for b in range(4):
            use(b, "turn", name, b)

    use(0, "params")
    turn("norm1")
    for u in range(UNITS):
        for step in MIXER.get(u, []):
            what, i = step[0], step[1] if len(step) > 1 else None
            if what == "gate":
                use(0, "gate")
            elif what == "gate_turn":
                use(1, "gate_turn")
            elif what == "na_scores":
                use(0, "na_scores", i)
            elif what == "na_turn":
                use(1, "na_turn", i)
            elif what == "na_values" and i % 8 == 0:
                use(2, "na_values", i // 8, 0)
                use(3, "na_values", i // 8, 1)
            elif what == "ml_scores":
                use(0, "ml_scores", i)
                use(1, "ml_rows", i)
            elif what == "ml_values":
                use(2, "ml_values", i, step[2], 0)
                use(3, "ml_values", i, step[2], 1)
            elif what == "ret_scores":
                use(i % 2, "ret_scores", i)
            elif what == "ret_values":
                use(2 + i % 2, "ret_values", i)
            elif what == "turn":
                turn(i)
            elif what == "up_turn":
                use(i % 4, "up_turn", i)
    return uses


USES = bank_uses()


def trunk(nc, x_in, norm1_g, w_in, gate_b, ret_decay_logit, na_bias, ml_conv_w, ml_conv_b, ml_gate_b,
          ml_norm_g, w_ret_o, w_na_o, w_ml_o, w_out, norm2_g, w_ffn_up, w_ffn_down, final_g,
          c_ident, c_cos, c_sin, c_dist, c_window, out):
    ctx = ExitStack()
    with ctx:
        def sb(name, shape):
            return ctx.enter_context(nc.sbuf_tensor(name, shape, F32))

        names = []

        def sem(name):
            s = ctx.enter_context(nc.semaphore(name))
            names.append((name, s))
            return s

        ring = sb("ring", [P, RING, UK, N512])
        x = sb("x", [P, NT, D])
        turned = sb("turned", [P, 2, KD, T])
        tok = sb("tok", [P, NT, D])
        y_na = sb("y_na", [P, NT, D])
        tmp = sb("tmp", [P, NT, N512])
        region_a = sb("region_a", [P, 24 * 256])
        region_b = sb("region_b", [P, 96 * 64 + 16])
        conv_in = sb("conv_in", [P, 8, T + CONV_W - 1])
        conv_out = sb("conv_out", [P, 8, T])
        mv = sb("mv", [P, NT, ML_HEADS, DV + 1])
        rot = sb("rot", [P, NT, 2, RET_HEADS, DK])
        rot_T = sb("rot_T", [P, 2 * RET_HEADS, T])
        rv = sb("rv", [P, NT, D])
        decay = sb("decay", [P, RET_HEADS, NT, T])
        small = sb("small", [P, 2048])
        tanh_buf = sb("tanh_buf", [P, NT, N512])
        ident = sb("ident", [P, P])
        cos = sb("cos", [P, NT, DK])
        sin = sb("sin", [P, NT, DK])
        window = sb("window", [P, GRID_W])
        rows64 = sb("rows64", [64, P])
        cols64 = sb("cols64", [P, 64])
        gate_w = sb("gate_w", [P, KD, 16])
        gbias = sb("gbias", [64, 2])
        acol = sb("acol", [P, NT, 64])
        emt = sb("emt", [P, NT, 64])
        stat = sb("stat", [P, 160])

        nqT = region_a[:, 0:2048].rearrange("p (k t) -> p k t", k=8)
        nkT = region_a[:, 2048:4096].rearrange("p (k t) -> p k t", k=8)
        nv = region_a[:, 4096:6144].rearrange("p (n c) -> p n c", n=NT)
        mixg = region_a[:, 0:6144].rearrange("p (n c) -> p n c", n=NT)
        ffT = region_a[:, 0:KF * T].rearrange("p (k t) -> p k t", k=KF)
        bias = region_b[:, 0:6144].rearrange("p (h j c) -> p h j c", h=NA_HEADS, j=6)
        rgs = region_b[:, 0:2048].rearrange("p (n c) -> p n c", n=NT)
        mog = region_b[:, 2048:4096].rearrange("p (n c) -> p n c", n=NT)
        norm_g = region_b[:, 4096:5120]
        gate_row = region_b[:, 5120:6144].rearrange("p (s c) -> p s c", s=2)
        dist = tmp[:, :, :]
        h_ml = conv_in[:, :, :].rearrange("p k c -> p (k c)")[:, 0:2048].rearrange("p (n c) -> p n c", n=NT)
        o_ret = rot[:, :, :, :, :].rearrange("p n a h d -> p n (a h d)")
        rot_flat = o_ret
        na_p = small[:, 0:1024].rearrange("p (s n c) -> p s n c", s=2, n=NT)
        na_pT = small[:, 1024:2048].rearrange("p (s n c) -> p s n c", s=2, n=NT)
        ml_e = small[:, 0:1024].rearrange("p (d j t) -> p d j t", d=2, j=NT)
        ml_w = small[:, 1024:2048].rearrange("p (d j t) -> p d j t", d=2, j=NT)
        ret_p = small[:, 0:1024].rearrange("p (s j t) -> p s j t", s=2, j=NT)
        up_s = small[:, 0:512].rearrange("p (n c) -> p n c", n=NT)
        up_v = small[:, 512:1536].rearrange("p (s n c) -> p s n c", s=2, n=NT)
        up_th = tanh_buf[:, :, :].rearrange("p s (n c) -> p s n c", n=NT)
        gw = tok[0:64, :, :].rearrange("p n c -> p (n c)").rearrange("p (s t) -> p s t", s=8)
        g_i, g_f, g_e, g_l, g_b, g_a, g_m, g_mt = (gw[:, i, :] for i in range(8))
        g_nm, g_one = g_e, g_m
        gate_w64 = rv[:, 0, :].rearrange("p (k i r) -> p k i r", k=KD, i=2)
        ss, rstd = stat[:, 0:2], stat[:, 2:4]
        lg = stat[:, 4:12]
        lg_e, lg_l, lg_raw = stat[:, 12:20], stat[:, 20:28], stat[:, 28:36]
        na_max = stat[:, 36:40].rearrange("p (s n) -> p s n", s=2)
        na_sum = stat[:, 40:72].rearrange("p (n h) -> p n h", n=NT)
        den = stat[:, 72:76].rearrange("p (d n) -> p d n", d=2)
        bn = stat[:, 76:124].rearrange("p (g s) -> p g s", g=8)
        mean_var = stat[:, 124:140].rearrange("p (g s) -> p g s", g=8)
        rs8 = stat[:, 140:148]
        half = stat[:, 148:156]
        rden = stat[:, 156:160].rearrange("p (d n) -> p d n", d=2)

        acc = ctx.enter_context(nc.psum_tensor("acc", [P, 4, N512], F32))
        mix = ctx.enter_context(nc.psum_tensor("mix", [P, 4, N512], F32))

        unit_in = [sem(f"unit_in{i}") for i in range(RING)]
        unit_used = sem("unit_used")
        group_done = sem("group_done")
        acc_read = [sem("acc_read0"), sem("acc_read1")]
        filled = [sem(f"filled{b}") for b in range(4)]
        read = [sem(f"read{b}") for b in range(4)]
        params_in = sem("params_in")
        bias_in = sem("bias_in")
        norm_g_in = sem("norm_g_in")
        gate_row_in = [sem("gate_row_in0"), sem("gate_row_in1")]
        sumsq = sem("sumsq")
        rstd_ok = sem("rstd_ok")
        xs_ok = sem("xs_ok")
        gate_w_ok = sem("gate_w_ok")
        lg_a, lg_b, lg_c = sem("lg_abs"), sem("lg_ln"), sem("decay_arg")
        decay_ok = sem("decay_ok")
        g_abs, g_ln, g_rows = sem("g_abs"), sem("g_ln"), sem("g_rows")
        bias_ok = sem("bias_ok")
        na_soft = sem("na_soft")
        na_exp = sem("na_exp")
        na_out = sem("na_out")
        conv_ok, conv_th, conv_silu = sem("conv_ok"), sem("conv_th"), sem("conv_silu")
        rot_ok = sem("rot_ok")
        ml_exp, ml_mask, ml_wt = sem("ml_exp"), sem("ml_mask"), sem("ml_wt")
        bn_ok = sem("bn_ok")
        rs_ok = sem("rs_ok")
        y_ok = sem("y_ok")
        ret_wt = sem("ret_wt")
        rg_th, mo_th = sem("rg_th"), sem("mo_th")
        mix_raw = sem("mix_raw")
        mix_th = sem("mix_th")
        branch_tmp, branch_sum, merged_ok = sem("branch_tmp"), sem("branch_sum"), sem("merged_ok")
        x_ok = sem("x_ok")
        up_tanh, up_v_ok = sem("up_tanh"), sem("up_v_ok")
        dve_step, act_step, pool_step = sem("dve_step"), sem("act_step"), sem("pool_step")
        pad_ok = sem("pad_ok")
        arrived = sem("arrived")
        layer_sems = list(names)
        consts_in, x_in_sem, out_sem = sem("consts_in"), sem("x_in"), sem("out_sem")
        fixed_ok = sem("fixed_ok")
        fin_sq, fin_rs, fin_step, fin_y = sem("fin_sq"), sem("fin_rs"), sem("fin_step"), sem("fin_y")
        final_g_in = sem("final_g_in")
        go = {e: sem(f"go_{e}") for e in ("act", "dve", "pe", "pool")}

        block = ctx.enter_context(nc.Block())

        def wait_group(eng, g):
            eng.wait_ge(group_done, g + 1)

        def wait_group_read(eng, g):
            eng.wait_ge(acc_read[g % 2], g // 2 + 1)

        def wait_unit_used(eng, u):
            if u >= U_DOWN:
                eng.wait_ge(unit_used, G_DOWN + u - U_DOWN + 1)
            elif u % 2:
                wait_group(eng, u // 2)
            else:
                eng.wait_ge(unit_used, u // 2 + 1)

        def wait_filled(eng, *name):
            bank, n = USES[name]
            eng.wait_ge(filled[bank], n)

        def wait_read(eng, *name):
            bank, n = USES[name]
            eng.wait_ge(read[bank], n)

        def pair(g):
            return acc[:, 2 * (g % 2):2 * (g % 2) + 2, :]

        def pair_fm(g):
            return pair(g).rearrange("p b (k t) -> p (b k) t", t=T)

        def layer_end(eng, key):
            eng.drain().then_inc(arrived, 1)
            eng.wait_ge(go[key], 1)
            eng.sem_clear(go[key])

        class Steps:

            def __init__(self, eng, semaphore):
                self.eng, self.semaphore, self.n = eng, semaphore, 0

            def link(self, ins):
                self.n += 1
                ins.then_inc(self.semaphore, 1)
                self.eng.wait_ge(self.semaphore, self.n)

        @block.sync
        def _(sp):
            sp.dma_start(x[:], x_in.rearrange("b (n p) c -> p (b n) c", p=P)).then_inc(x_in_sem, 16)

            def source(l, u):
                if u >= U_DOWN:
                    k = 2 * (u - U_DOWN)
                    return w_ffn_down[bass.ds(l, 1), k * P:(k + 2) * P, :].rearrange(
                        "a (k p) c -> p (a k) c", p=P)
                g, k = u // 2, UK * (u % 2)
                rows = slice(k * P, (k + UK) * P)
                if g < G_PROJ:
                    w, col = w_in, IN_GROUPS[g][1]
                elif g < G_OUT:
                    w = {"na": w_na_o, "ml": w_ml_o, "ret": w_ret_o}[BRANCHES[(g - G_PROJ) // 2]]
                    col = (g - G_PROJ) % 2 * N512
                elif g < G_UP:
                    w, col = w_out, (g - G_OUT) * N512
                else:
                    return [w_ffn_up[bass.ds(l, 1), rows, s:s + 256].rearrange("a (k p) c -> p (a k) c", p=P)
                            for s in ((g - G_UP) * 256, FF + (g - G_UP) * 256)]
                return w[bass.ds(l, 1), rows, col:col + N512].rearrange("a (k p) c -> p (a k) c", p=P)

            with sp.Fori(0, DEPTH) as l:
                for u in range(UNITS):
                    slot = u % RING
                    if u >= RING:
                        wait_unit_used(sp, u - RING)
                    src = source(l, u)
                    if isinstance(src, list):
                        for i, s in enumerate(src):
                            sp.dma_start(ring[:, slot, :, 256 * i:256 * i + 256], s).then_inc(unit_in[slot], 16)
                    elif u >= U_DOWN:
                        sp.dma_start(ring[:, slot, :, :].rearrange("p k c -> p (k c)").rearrange(
                            "p (k c) -> p k c", k=2), src).then_inc(unit_in[slot], 16)
                    else:
                        sp.dma_start(ring[:, slot, :, :], src).then_inc(unit_in[slot], 16)
                sp.wait_ge(arrived, 4)
                for _, s in layer_sems:
                    sp.sem_clear(s)
                for e in go.values():
                    sp.sem_inc(e, 1)
            sp.dma_start(ring[:, 0, 0:2, :], final_g.partition_broadcast(P).rearrange(
                "p (k c) -> p k c", k=2)).then_inc(final_g_in, 16)
            for n in range(NT):
                sp.wait_ge(fin_y, n + 1)
                sp.dma_start(out[0, n * P:(n + 1) * P, :], tok[:, n, :]).then_inc(out_sem, 16)
            sp.wait_ge(out_sem, 16 * NT)

        def unit_in_count(u):
            n = 0
            for v in range(u % RING, u + 1, RING):
                n += 32 if 2 * G_UP <= v < U_DOWN else 16
            return n

        @block.tensor
        def _(pe):
            pe.wait_ge(consts_in, 16 * 4)

            def turn(name, src, dst_free=None):
                for b in range(4):
                    bank, n = USES[("turn", name, b)]
                    if n > 1:
                        pe.wait_ge(read[bank], n - 1)
                    if name == "merged":
                        pe.wait_ge(merged_ok, 1 + b // 2)
                    for j in range(2):
                        for n in range(NT):
                            c = (2 * b + j) * P
                            ins = pe.transpose(mix[:, b, j * T + n * P:j * T + (n + 1) * P],
                                               src[:, n, c:c + P], ident[:])
                    ins.then_inc(filled[b], 1)

            def begin(*name):
                bank, n = USES[name]
                if n > 1:
                    pe.wait_ge(read[bank], n - 1)
                return bank

            def mixer(step):
                what = step[0]
                if what == "gate":
                    b = begin("gate")
                    pe.wait_ge(gate_w_ok, 2)
                    for i in range(2):
                        for k in range(KD):
                            ins = pe.matmul(mix[0:64, b, i * T:(i + 1) * T], gate_w64[:, k, i, :],
                                            turned[:, 0, k, :], start=(k == 0), stop=(k == KD - 1))
                    ins.then_inc(filled[b], 1)
                elif what == "gate_turn":
                    b = begin("gate_turn")
                    pe.wait_ge(g_rows, 1)
                    for i, src in enumerate((g_a, g_mt)):
                        for n in range(NT):
                            o = (i * NT + n) * 64
                            ins = pe.transpose(mix[:, b, o:o + 64], src[:, n * P:(n + 1) * P],
                                               ident[0:64, 0:64])
                    ins.then_inc(filled[b], 1)
                elif what == "na_scores":
                    h = step[1]
                    b = begin("na_scores", h)
                    if h == 0:
                        for g in range(4):
                            wait_group_read(pe, g)
                    r = NA_DH * (h % 2)
                    for n in range(NT):
                        ins = pe.matmul(mix[:, b, n * T:(n + 1) * T],
                                        nqT[r:r + NA_DH, h // 2, n * P:(n + 1) * P],
                                        nkT[r:r + NA_DH, h // 2, :], start=True, stop=True)
                    ins.then_inc(filled[b], 1)
                elif what == "na_turn":
                    h = step[1]
                    b = begin("na_turn", h)
                    pe.wait_ge(na_exp, h + 1)
                    for k in range(NT):
                        for n in range(NT):
                            ins = pe.transpose(mix[:, b, k * T + n * P:k * T + (n + 1) * P],
                                               na_p[:, h % 2, n, k * P:(k + 1) * P], ident[:])
                    ins.then_inc(filled[b], 1)
                elif what == "na_values":
                    h = step[1]
                    banks = [USES[("na_values", h // 8, n)][0] for n in range(NT)]
                    if h % 8 == 0:
                        for n in range(NT):
                            begin("na_values", h // 8, n)
                    if h == 0:
                        wait_group_read(pe, 4)
                        wait_group_read(pe, 5)
                    wait_read(pe, "na_turn", h)
                    for n in range(NT):
                        for k in range(NT):
                            ins = pe.matmul(mix[:, banks[n], (h % 8) * NA_DH:(h % 8 + 1) * NA_DH],
                                            na_pT[:, h % 2, k, n * P:(n + 1) * P],
                                            nv[:, k, h * NA_DH:(h + 1) * NA_DH],
                                            start=(k == 0), stop=(k == NT - 1))
                        if h % 8 == 7:
                            ins.then_inc(filled[banks[n]], 1)
                elif what == "ml_scores":
                    h = step[1]
                    b = begin("ml_scores", h)
                    if h == 0:
                        pe.wait_ge(conv_silu, 8)
                    for j in range(NT):
                        ins = pe.matmul(mix[:, b, j * T:(j + 1) * T],
                                        conv_out[:, ML_HEADS + h, j * P:(j + 1) * P],
                                        conv_out[:, h, :], start=True, stop=True)
                    ins.then_inc(filled[b], 1)
                    b = begin("ml_rows", h)
                    for d in range(2):
                        r = 32 * d + h
                        ins = pe.matmul(mix[:, b, d * T:(d + 1) * T],
                                        ident[0:64, r:r + 1].to_broadcast([64, P]), g_nm,
                                        start=True, stop=True)
                    ins.then_inc(filled[b], 1)
                elif what == "ml_values":
                    h, d = step[1], step[2]
                    if (h, d) == (0, 0):
                        wait_group_read(pe, 8)
                        wait_group_read(pe, 9)
                    pe.wait_ge(ml_wt, 2 * h + d + 1)
                    for n in range(NT):
                        b = begin("ml_values", h, d, n)
                        js = range(0, n + 1) if d == 0 else range(n, NT)
                        for j in js:
                            ins = pe.matmul(mix[:, b, 0:DV + 1], ml_w[:, d, j, n * P:(n + 1) * P],
                                            mv[:, j, h, :], start=(j == js[0]), stop=(j == js[-1]))
                        ins.then_inc(filled[b], 1)
                elif what == "ret_scores":
                    h = step[1]
                    b = begin("ret_scores", h)
                    if h == 0:
                        for i in range(4):
                            wait_read(pe, "turn", "rot", i)
                    for j in range(NT):
                        ins = pe.matmul(mix[:, b, j * T:(j + 1) * T],
                                        rot_T[:, RET_HEADS + h, j * P:(j + 1) * P],
                                        rot_T[:, h, :], start=True, stop=True)
                    ins.then_inc(filled[b], 1)
                elif what == "ret_values":
                    h = step[1]
                    b = begin("ret_values", h)
                    if h == 0:
                        wait_group_read(pe, 12)
                        wait_group_read(pe, 13)
                    pe.wait_ge(ret_wt, h + 1)
                    for n in range(NT):
                        for j in range(NT):
                            ins = pe.matmul(mix[:, b, n * T:(n + 1) * T], ret_p[:, h % 2, j, n * P:(n + 1) * P],
                                            rv[:, j, h * DV:(h + 1) * DV], start=(j == 0), stop=(j == NT - 1))
                    ins.then_inc(filled[b], 1)
                elif what == "turn":
                    name = step[1]
                    if name == "rot":
                        pe.wait_ge(rot_ok, 4)
                    elif name == "na":
                        [wait_read(pe, "na_values", i, n) for i in range(2) for n in range(NT)]
                    elif name == "ml":
                        pe.wait_ge(y_ok, 1)
                    elif name == "ret":
                        pe.wait_ge(y_ok, 2)
                    elif name == "norm2":
                        pe.wait_ge(xs_ok, 4)
                    turn(name, {"rot": rot_flat, "na": y_na, "ml": h_ml, "ret": o_ret, "merged": tok,
                                "norm2": tok}[name])
                elif what == "up_turn":
                    c = step[1]
                    b = begin("up_turn", c)
                    pe.wait_ge(up_v_ok, c + 1)
                    for j in range(2):
                        for n in range(NT):
                            ins = pe.transpose(mix[:, b, j * T + n * P:j * T + (n + 1) * P],
                                               up_v[:, c % 2, n, j * P:(j + 1) * P], ident[:])
                    ins.then_inc(filled[b], 1)

            def left_of(g):
                if g < G_PROJ:
                    return 0, "norm1"
                if g < G_OUT:
                    i = (g - G_PROJ) // 2
                    return (1, 0, 1)[i], BRANCHES[i]
                return (0, "merged") if g < G_UP else (1, "norm2")

            with pe.Fori(0, DEPTH):
                pe.wait_ge(params_in, 16 * 9)
                pe.transpose(mix[:, 0, 0:64], rows64[:], ident[0:64, 0:64]).then_inc(filled[0], 1)
                pe.wait_ge(xs_ok, 2)
                turn("norm1", tok)
                for u in range(UNITS):
                    slot, g = u % RING, u // 2
                    pe.wait_ge(unit_in[slot], unit_in_count(u))
                    if u < U_DOWN:
                        buf, name = left_of(g)
                        if u % 2 == 0 and g >= 2:
                            wait_group_read(pe, g - 2)
                        for k in range(UK):
                            kk = UK * (u % 2) + k
                            if kk % 2 == 0:
                                wait_read(pe, "turn", name, kk // 2)
                            if g >= G_PROJ or IN_GROUPS[g][0] not in FEATURE_MAJOR:
                                for n in range(NT):
                                    ins = pe.matmul(pair(g)[:, n, :], turned[:, buf, kk, n * P:(n + 1) * P],
                                                    ring[:, slot, k, :], start=(kk == 0), stop=(kk == KD - 1))
                            else:
                                for j in range(4):
                                    ins = pe.matmul(pair_fm(g)[:, j, :], ring[:, slot, k, j * P:(j + 1) * P],
                                                    turned[:, buf, kk, :], start=(kk == 0 and j % 2 == 0),
                                                    stop=(kk == KD - 1), skip_group_check=True)
                    else:
                        c = u - U_DOWN
                        if c == 0:
                            wait_group_read(pe, G_DOWN - 1)
                            wait_group_read(pe, G_DOWN - 2)
                        wait_read(pe, "up_turn", c)
                        down = ring[:, slot, :, :].rearrange("p k c -> p (k c)")
                        for k in range(2):
                            for n in range(NT):
                                for j in range(2):
                                    ins = pe.matmul(acc[:, 2 * n + j, :], ffT[:, 2 * c + k, n * P:(n + 1) * P],
                                                    down[:, k * D + j * N512:k * D + (j + 1) * N512],
                                                    start=(c == 0 and k == 0), stop=(c == N_DOWN - 1 and k == 1))
                    ends = u % 2 == 1 if u < U_DOWN else u == UNITS - 1
                    ins.then_inc(group_done if ends else unit_used, 1)
                    for step in MIXER.get(u, []):
                        mixer(step)
                layer_end(pe, "pe")

        @block.scalar
        def _(act):
            steps = Steps(act, act_step)

            def turned_banks(name):
                dst = rot_T if name == "rot" else turned[:, {"norm1": 0, "ml": 0, "merged": 0}.get(name, 1), :, :]
                for b in range(2):
                    wait_filled(act, "turn", name, b)
                    if name in ("norm1", "norm2"):
                        for j in range(2):
                            k = 2 * b + j
                            col = k + (8 if name == "norm2" else 0)
                            ins = act.activation(dst[:, k, :], mix[:, b, j * T:(j + 1) * T], ACT.Copy,
                                                 scale=cols64[:, col:col + 1])
                    else:
                        ins = act.activation(dst[:, 2 * b:2 * b + 2, :], mix[:, b, :].rearrange(
                            "p (k t) -> p k t", k=2), ACT.Copy, scale=0.5 if name == "merged" else 1.0)
                    ins.then_inc(read[b], 1)

            def squares(x_count):
                if x_count:
                    act.wait_ge(x_ok, x_count)
                for n in range(NT):
                    junk = (tanh_buf[:, :, :].rearrange("p s c -> p (s c)"), small[:, 0:D])[n]
                    act.activation(junk, x[:, n, :], ACT.Square, accum_out=ss[:, n:n + 1]).then_inc(sumsq, 1)

            def group(g):
                part = IN_GROUPS[g][0]
                half_of = slice((g % 2) * N512, (g % 2 + 1) * N512)
                if part in ("nq", "nk"):
                    dst = (nqT if part == "nq" else nkT)[:, 4 * (g % 2):4 * (g % 2) + 4, :]
                    wait_group(act, g)
                    act.activation(dst, pair_fm(g), ACT.Copy).then_inc(acc_read[g % 2], 1)
                elif part in ("mq", "mk"):
                    k = 0 if part == "mq" else 4
                    wait_group(act, g)
                    act.wait_ge(pad_ok, 2)
                    act.activation(conv_in[:, k:k + 4, 2:2 + T], pair_fm(g), ACT.Copy).then_inc(acc_read[g % 2], 1)
                elif part in ("nv", "rv"):
                    wait_group(act, g)
                    act.activation((nv if part == "nv" else rv)[:, :, half_of], pair(g),
                                   ACT.Copy).then_inc(acc_read[g % 2], 1)
                elif part == "mv":
                    wait_group(act, g)
                    for n in range(NT):
                        ins = act.activation(mv[:, n, 2 * (g % 2):2 * (g % 2) + 2, 0:DV],
                                             pair(g)[:, n, :].rearrange("p (h d) -> p h d", h=2), ACT.Copy)
                    ins.then_inc(acc_read[g % 2], 1)
                elif part == "rg":
                    wait_group(act, g)
                    if g % 2:
                        wait_group_read(act, g - 1)
                    else:
                        act.wait_ge(conv_silu, 8)
                    act.activation(tanh_buf[:], pair(g), ACT.Tanh, scale=0.5).then_inc(rg_th, 1)
                elif part == "mo":
                    wait_group(act, g)
                    act.activation(mog[:, :, half_of], pair(g), ACT.Tanh, scale=0.5).then_inc(acc_read[g % 2], 1)
                elif part == "mix":
                    j = g - G_MIX
                    wait_group_read(act, g)
                    cols = mixg[:, :, j * N512:(j + 1) * N512]
                    act.activation(cols, cols, ACT.Tanh, scale=0.5).then_inc(mix_th, 1)

            def mixer(step):
                what = step[0]
                if what == "gate":
                    act.wait_ge(g_abs, 1)
                    steps.link(act.activation(g_e, g_e, ACT.Exp, scale=-1.0))
                    act.activation(g_l, g_e, ACT.Ln, bias=1.0).then_inc(g_ln, 1)
                elif what == "gate_turn":
                    wait_filled(act, "gate_turn")
                    b = USES[("gate_turn",)][0]
                    act.activation(acol[:], mix[:, b, 0:2 * 64].rearrange("p (n r) -> p n r", n=NT), ACT.Copy)
                    act.activation(emt[:], mix[:, b, 2 * 64:4 * 64].rearrange("p (n r) -> p n r", n=NT),
                                   ACT.Exp, scale=-1.0).then_inc(read[b], 1)
                elif what == "na_scores":
                    h = step[1]
                    act.wait_ge(na_soft, h + 1)
                    for n in range(NT):
                        ins = act.activation(na_p[:, h % 2, n, :], na_p[:, h % 2, n, :], ACT.Exp,
                                             bias=na_max[:, h % 2, n:n + 1], accum_out=na_sum[:, n, h:h + 1])
                    ins.then_inc(na_exp, 1)
                elif what == "na_turn":
                    h = step[1]
                    wait_filled(act, "na_turn", h)
                    b = USES[("na_turn", h)][0]
                    act.activation(na_pT[:, h % 2, :, :], mix[:, b, :].rearrange("p (k c) -> p k c", k=NT),
                                   ACT.Copy).then_inc(read[b], 1)
                elif what == "ml_scores":
                    h = step[1]
                    wait_filled(act, "ml_rows", h)
                    b = USES[("ml_rows", h)][0]
                    if h == 0:
                        wait_read(act, "gate_turn")
                    else:
                        act.wait_ge(ml_wt, 2 * h)
                    for d, j, t0, t1 in ((0, 0, 0, T), (0, 1, P, T), (1, 0, 0, P), (1, 1, 0, T)):
                        r = 32 * d + h
                        ins = act.activation(ml_e[:, d, j, t0:t1], mix[:, b, d * T + t0:d * T + t1], ACT.Exp,
                                             bias=acol[:, j, r:r + 1])
                        if (d, j) == (1, 1):
                            ins.then_inc(read[b], 1)
                elif what == "ret_values":
                    h = step[1]
                    wait_filled(act, "ret_values", h)
                    b = USES[("ret_values", h)][0]
                    act.activation(o_ret[:, :, h * DV:(h + 1) * DV], mix[:, b, :].rearrange(
                        "p (n c) -> p n c", n=NT), ACT.Copy).then_inc(read[b], 1)
                elif what == "turn":
                    if step[1] == "norm2":
                        squares(2)
                    turned_banks(step[1])
                elif what == "up_turn":
                    c = step[1]
                    wait_filled(act, "up_turn", c)
                    b = USES[("up_turn", c)][0]
                    act.activation(ffT[:, 2 * c:2 * c + 2, :], mix[:, b, :].rearrange("p (k t) -> p k t", k=2),
                                   ACT.Copy).then_inc(read[b], 1)

            act.dma_start(ident[:], c_ident).then_inc(consts_in, 16)
            act.dma_start(cos[:], c_cos.rearrange("(n p) d -> p n d", p=P)).then_inc(consts_in, 16)
            act.dma_start(sin[:], c_sin.rearrange("(n p) d -> p n d", p=P)).then_inc(consts_in, 16)
            act.dma_start(window[:], c_window).then_inc(consts_in, 16)
            act.wait_ge(x_in_sem, 16)
            act.wait_ge(fixed_ok, 4)

            with act.Fori(0, DEPTH) as l:
                one = bass.ds(l, 1)
                for i, g in enumerate((norm1_g, norm2_g)):
                    act.dma_start(rows64[8 * i:8 * i + 8, :], g[one, :].rearrange("a (k c) -> (a k) c", c=P)
                                  ).then_inc(params_in, 16)
                act.dma_start(rows64[16:56, :], ml_conv_w[one].rearrange("a w (k c) -> (a w k) c", c=P)
                              ).then_inc(params_in, 16)
                act.dma_start(rows64[56:64, :], ml_conv_b[one, :].rearrange("a (k c) -> (a k) c", c=P)
                              ).then_inc(params_in, 16)
                act.dma_start(lg_raw, ret_decay_logit[one].rearrange("a d h -> a (d h)").to_broadcast([P, 8])
                              ).then_inc(params_in, 16)
                for d in range(2):
                    act.dma_start(gbias[32 * d:32 * d + 4, :], ml_gate_b[one, d].rearrange(
                        "a i h -> h (a i)"), allow_slow_non_contiguous=True).then_inc(params_in, 16)
                act.dma_start(gate_w[:], w_in[one, :, MGATE:MGATE + 16].rearrange(
                    "a (k p) c -> p (a k) c", p=P)).then_inc(params_in, 16)
                act.dma_start(dist, c_dist).then_inc(params_in, 16)
                act.dma_start(region_b[:, 0:6144], na_bias[one].rearrange("a p c -> (a p) c")
                              ).then_inc(bias_in, 16)
                squares(0)
                turned_banks("norm1")
                act.wait_ge(lg_a, 1)
                steps.link(act.activation(lg_e, lg_e, ACT.Exp, scale=-1.0))
                act.activation(lg_l, lg_e, ACT.Ln, bias=1.0).then_inc(lg_b, 1)
                for u in range(UNITS):
                    g = u // 2
                    if u < 2 * G_PROJ and u % 2:
                        group(g)
                    if u >= 2 * G_UP and u < U_DOWN and u % 2:
                        c = g - G_UP
                        wait_group(act, g)
                        if c >= 2:
                            act.wait_ge(up_v_ok, c - 1)
                        act.activation(up_th[:, c % 2, :, :], pair(g)[:, :, 0:256], ACT.Tanh,
                                       scale=0.5).then_inc(up_tanh, 1)
                    if u == 4:
                        act.wait_ge(lg_c, RET_HEADS)
                        act.activation(decay[:], decay[:], ACT.Exp).then_inc(decay_ok, 1)
                    if u in (18, 22):
                        i = (u - 18) // 4
                        act.wait_ge(conv_ok, 4 * i + 4)
                        if i:
                            act.wait_ge(conv_silu, 4)
                        act.activation(tanh_buf[:, :, :].rearrange("p s c -> p (s c)"),
                                       conv_out[:, 4 * i:4 * i + 4, :].rearrange("p k t -> p (k t)"),
                                       ACT.Tanh, scale=0.5).then_inc(conv_th, 1)
                    if u == U_ML:
                        act.wait_ge(na_soft, NA_HEADS)
                        act.dma_start(norm_g, ml_norm_g[one, :].to_broadcast([P, D])).then_inc(norm_g_in, 16)
                        for s in range(2):
                            act.dma_start(gate_row[:, s, :], gate_b[one, s * N512:(s + 1) * N512].to_broadcast(
                                [P, N512])).then_inc(gate_row_in[s], 16)
                    if 2 * G_MIX <= u < 2 * G_PROJ and u % 2 and (u // 2 - G_MIX) + 2 < 6:
                        j = u // 2 - G_MIX
                        act.dma_start(gate_row[:, j % 2, :], gate_b[one, (j + 2) * N512:(j + 3) * N512
                                      ].to_broadcast([P, N512])).then_inc(gate_row_in[j % 2], 16)
                    for step in MIXER.get(u, []):
                        mixer(step)
                layer_end(act, "act")

            for n in range(NT):
                act.activation(small[:, n * D:(n + 1) * D], x[:, n, :], ACT.Square,
                               accum_out=ss[:, n:n + 1]).then_inc(fin_sq, 1)

        @block.gpsimd
        def _(pool):
            steps = Steps(pool, pool_step)
            link = steps.link

            def rsqrt(dst, src, scale):
                steps.link(pool.tensor_scalar(dst, src, scale, EPS, ALU.mult, ALU.add))
                return pool.tensor_tensor(dst, dst, half[:, 0:dst.shape[-1]], ALU.pow)

            pool.memset(half, -0.5).then_inc(fixed_ok, 1)
            pool.memset(gbias[:], 0.0).then_inc(fixed_ok, 1)
            pool.memset(mv[:, :, :, DV:DV + 1], 1.0).then_inc(fixed_ok, 1)
            pool.memset(stat[:, 0:4], 0.0).then_inc(fixed_ok, 1)
            pool.wait_ge(fixed_ok, 4)
            pool.wait_ge(consts_in, 16 * 4)

            with pool.Fori(0, DEPTH):
                link(pool.memset(gate_w64, 0.0))
                for c in (0, 2 + T):
                    pool.memset(conv_in[:, :, c:c + 2], 0.0).then_inc(pad_ok, 1)
                pool.wait_ge(sumsq, 2)
                rsqrt(rstd, ss, 1.0 / D).then_inc(rstd_ok, 1)
                pool.wait_ge(params_in, 16 * 9)
                for d in range(2):
                    pool.tensor_copy(gate_w64[:, :, :, 32 * d:32 * d + 4], gate_w[:, :, 8 * d:8 * d + 8].rearrange(
                        "p k (i h) -> p k i h", i=2)).then_inc(gate_w_ok, 1)
                pool.wait_ge(bias_in, 16)
                for i in range(4):
                    part = region_b[:, i * 1536:(i + 1) * 1536].rearrange("p (j c) -> p j c", c=GRID_W)
                    pool.tensor_tensor(part, part, window[:, :].rearrange("p (a c) -> p a c", a=1).to_broadcast(
                        [P, 24, GRID_W]), ALU.add).then_inc(bias_ok, 1)
                for h in range(ML_HEADS):
                    wait_read(pool, "ml_rows", h)
                    for d, j in ((0, 0), (0, 1), (1, 0), (1, 1)):
                        block_ = ml_e[:, d, j, j * P:(j + 1) * P]
                        s = 1 if d == 0 else -1
                        pool.affine_select(block_, block_, pattern=[[s, P]], compare_op=ALU.is_ge, fill=0.0,
                                           base=0, channel_multiplier=-s).then_inc(ml_mask, 1)
                for i, y in enumerate(("ml", "ret")):
                    pool.wait_ge(bn_ok, i + 1)
                    rsqrt(rs8, mean_var[:, :, 1], 1.0).then_inc(rs_ok, 1)
                for g in (G_PROJ + 2, G_PROJ + 3):
                    pool.wait_ge(branch_tmp, g - G_PROJ + 1)
                    cols = tok[:, :, (g % 2) * N512:(g % 2 + 1) * N512]
                    pool.tensor_tensor(cols, cols, tmp[:], ALU.add).then_inc(branch_sum, 1)
                pool.wait_ge(sumsq, 4)
                rsqrt(rstd, ss, 1.0 / D).then_inc(rstd_ok, 1)
                layer_end(pool, "pool")

            pool.wait_ge(fin_sq, 2)
            pool.tensor_scalar(rstd, ss, 1.0 / D, EPS, ALU.mult, ALU.add).then_inc(fin_step, 1)
            pool.wait_ge(fin_step, 1)
            pool.tensor_tensor(rstd, rstd, half[:, 0:NT], ALU.pow).then_inc(fin_rs, 1)

        @block.vector
        def _(dve):
            steps = Steps(dve, dve_step)
            link = steps.link

            def turned_banks(name):
                dst = rot_T if name == "rot" else turned[:, {"norm1": 0, "ml": 0, "merged": 0}.get(name, 1), :, :]
                for b in range(2, 4):
                    wait_filled(dve, "turn", name, b)
                    if name in ("norm1", "norm2"):
                        for j in range(2):
                            k = 2 * b + j
                            col = k + (8 if name == "norm2" else 0)
                            ins = dve.tensor_scalar(dst[:, k, :], mix[:, b, j * T:(j + 1) * T],
                                                    cols64[:, col:col + 1], None, ALU.mult)
                    else:
                        ins = dve.tensor_scalar(dst[:, 2 * b:2 * b + 2, :], mix[:, b, :].rearrange(
                            "p (k t) -> p k t", k=2), 0.5 if name == "merged" else 1.0, None, ALU.mult)
                    ins.then_inc(read[b], 1)

            def scale_x(count):
                dve.wait_ge(rstd_ok, count)
                for n in range(NT):
                    dve.tensor_scalar(tok[:, n, :], x[:, n, :], rstd[:, n:n + 1], None, ALU.mult).then_inc(xs_ok, 1)

            def log_sigmoid(dst, raw, l):
                link(dve.scalar_tensor_tensor(dst, raw, 0.0, l, ALU.min, ALU.subtract))

            def gates():
                b = USES[("gate",)][0]
                wait_filled(dve, "gate")
                link(dve.tensor_scalar(g_f, mix[0:64, b, T:2 * T], gbias[:, 1:2], None, ALU.add))
                dve.tensor_scalar(g_i, mix[0:64, b, 0:T], gbias[:, 0:1], None, ALU.add).then_inc(read[b], 1)
                dve.scalar_tensor_tensor(g_e, g_f, -1.0, g_f, ALU.mult, ALU.max).then_inc(g_abs, 1)
                link(dve.memset(g_one, 1.0))
                dve.wait_ge(g_ln, 1)
                log_sigmoid(g_f, g_f, g_l)
                for r, way in ((slice(0, 32), 1), (slice(32, 64), -1)):
                    link(dve.tensor_tensor_scan(g_b[r, ::way], g_f[r, ::way], g_one[r, :], 0.0, ALU.add, ALU.mult))
                link(dve.tensor_tensor(g_a, g_i, g_b, ALU.subtract))
                for r, way in ((slice(0, 32), 1), (slice(32, 64), -1)):
                    link(dve.tensor_tensor_scan(g_m[r, ::way], g_a[r, ::way], g_a[r, ::way], LOWEST,
                                                ALU.max, ALU.max))
                link(dve.tensor_scalar(g_nm, g_m, -1.0, None, ALU.mult))
                dve.tensor_tensor(g_mt, g_b, g_m, ALU.add).then_inc(g_rows, 1)

            def na_scores(h):
                b = USES[("na_scores", h)][0]
                wait_filled(dve, "na_scores", h)
                if h == 0:
                    dve.wait_ge(bias_ok, 4)
                if h >= 2:
                    wait_filled(dve, "na_turn", h - 2)
                for n in range(NT):
                    first = 2 * (NT - 1 - n)
                    ins = dve.scalar_tensor_tensor(
                        na_p[:, h % 2, n, :], mix[:, b, n * T:(n + 1) * T], NA_SCALE,
                        bias[:, h, first:first + ROWS, :].rearrange("p j c -> p (j c)"), ALU.mult, ALU.add)
                    if n == NT - 1:
                        ins.then_inc(read[b], 1)
                wait_read(dve, "na_scores", h)
                dve.tensor_reduce(na_max[:, h % 2, :], na_p[:, h % 2, :, :], AX_X, ALU.max,
                                  negate=True).then_inc(na_soft, 1)

            def na_normalise(i):
                dve.wait_ge(na_exp, 8 * i + 8)
                s = na_sum[:, :, 8 * i:8 * i + 8]
                link(dve.reciprocal(s, s))
                for n in range(NT):
                    b = USES[("na_values", i, n)][0]
                    wait_filled(dve, "na_values", i, n)
                    dve.tensor_tensor(y_na[:, n, i * N512:(i + 1) * N512].rearrange("p (h d) -> p h d", d=NA_DH),
                                      mix[:, b, :].rearrange("p (h d) -> p h d", d=NA_DH),
                                      na_sum[:, n, 8 * i:8 * i + 8].rearrange("p (h a) -> p h a", a=1).to_broadcast(
                                          [P, 8, NA_DH]), ALU.mult).then_inc(read[b], 1)

            def conv(i):
                tap = lambda w: cols64[:, 16 + 8 * w + i:17 + 8 * w + i]
                if i % 4 == 0:
                    wait_group_read(dve, 6 + i // 4)
                link(dve.tensor_scalar(conv_out[:, i, :], conv_in[:, i, 0:T], tap(0), cols64[:, 56 + i:57 + i],
                                       ALU.mult, ALU.add))
                for w in range(1, CONV_W):
                    ins = dve.scalar_tensor_tensor(conv_out[:, i, :], conv_in[:, i, w:w + T], tap(w),
                                                   conv_out[:, i, :], ALU.mult, ALU.add)
                    if w < CONV_W - 1:
                        link(ins)
                ins.then_inc(conv_ok, 1)

            def silu(i):
                dve.wait_ge(conv_th, i + 1)
                part = conv_out[:, 4 * i:4 * i + 4, :].rearrange("p k t -> p (k t)")
                dve.scalar_tensor_tensor(part, tanh_buf[:, :, :].rearrange("p s c -> p (s c)"), 1.0, part,
                                         ALU.add, ALU.mult).then_inc(conv_silu, 4)

            def rotary(g, n):
                i = g - 10
                wait_group(dve, g)
                if (g, n) == (10, 0):
                    dve.wait_ge(lg_c, RET_HEADS)
                src = pair(g)[:, n, :].rearrange("p (h d) -> p h d", d=DK)
                by = [w[:, n, :].rearrange("p (a d) -> p a d", a=1).to_broadcast([P, RET_HEADS, DK])
                      for w in (cos, sin)]
                xc, xs = (tmp[:, j, :].rearrange("p (h d) -> p h d", d=DK) for j in range(2))
                dve.tensor_tensor(xc, src, by[0], ALU.mult)
                ins = dve.tensor_tensor(xs, src, by[1], ALU.mult)
                if n == NT - 1:
                    ins.then_inc(acc_read[g % 2], 1)
                    wait_group_read(dve, g)
                else:
                    link(ins)
                dst = rot[:, n, i, :, :]
                link(dve.tensor_tensor(dst[:, :, 0:64], xc[:, :, 0:64], xs[:, :, 64:128], ALU.subtract))
                ins = dve.tensor_tensor(dst[:, :, 64:128], xc[:, :, 64:128], xs[:, :, 0:64], ALU.add)
                ins.then_inc(rot_ok, 1)
                dve.wait_ge(rot_ok, 2 * i + n + 1)

            def ml_weights(h):
                b = USES[("ml_scores", h)][0]
                wait_filled(dve, "ml_scores", h)
                dve.wait_ge(ml_mask, 4 * h + 4)
                for d, j, t0, t1 in ((0, 0, 0, T), (0, 1, P, T), (1, 0, 0, P), (1, 1, 0, T)):
                    ins = dve.scalar_tensor_tensor(ml_w[:, d, j, t0:t1], mix[:, b, j * T + t0:j * T + t1],
                                                   QK_SCALE / 4, ml_e[:, d, j, t0:t1], ALU.mult, ALU.mult)
                    if j == 1:
                        ins.then_inc(ml_wt, 1)
                dve.wait_ge(ml_wt, 2 * h + 2)
                dve.sem_inc(read[b], 1)

            def ml_out(h, d):
                for n in range(NT):
                    wait_filled(dve, "ml_values", h, d, n)
                r = 32 * d + h
                link(dve.tensor_tensor(rden[:, d, :], mix[:, 2:4, DV], emt[:, :, r], ALU.max))
                link(dve.scalar_tensor_tensor(den[:, d, :], mix[:, 2:4, DV], -1.0, rden[:, d, :],
                                              ALU.mult, ALU.max))
                link(dve.reciprocal(rden[:, d, :], den[:, d, :]))
                for n in range(NT):
                    b = USES[("ml_values", h, d, n)][0]
                    dst = h_ml[:, n, h * DV:(h + 1) * DV]
                    if d == 0:
                        ins = dve.tensor_scalar(dst, mix[:, b, 0:DV], rden[:, d, n:n + 1], None, ALU.mult)
                    else:
                        ins = dve.scalar_tensor_tensor(dst, mix[:, b, 0:DV], rden[:, d, n:n + 1], dst,
                                                       ALU.mult, ALU.add)
                    ins.then_inc(read[b], 1)

            def head_norm(i, y, factor, other):
                for n in range(NT):
                    for h in range(4):
                        ins = dve.bn_stats(bn[:, 4 * n + h, :], y[:, n, h * DV:(h + 1) * DV])
                link(ins)
                for k in range(8):
                    ins = dve.bn_aggr(mean_var[:, k, :], bn[:, k, :])
                ins.then_inc(bn_ok, 1)
                dve.wait_ge(rs_ok, i + 1)
                for n in range(NT):
                    for h in range(4):
                        k, part = 4 * n + h, y[:, n, h * DV:(h + 1) * DV]
                        ins = dve.tensor_scalar(part, part, mean_var[:, k, 0:1], rs8[:, k:k + 1],
                                                ALU.subtract, ALU.mult)
                link(ins)
                dve.scalar_tensor_tensor(y, y, factor, other, ALU.mult, ALU.mult).then_inc(y_ok, 1)

            def group(g):
                part = IN_GROUPS[g][0]
                cols = slice((g % 2) * N512, (g % 2 + 1) * N512)
                if part == "rg":
                    dve.wait_ge(rg_th, g - 14 + 1)
                    dve.scalar_tensor_tensor(rgs[:, :, cols], tanh_buf[:], 1.0, pair(g), ALU.add,
                                             ALU.mult).then_inc(acc_read[g % 2], 1)
                elif part == "mo":
                    if g == 16:
                        dve.wait_ge(norm_g_in, 16)
                    wait_group_read(dve, g)
                    ins = dve.scalar_tensor_tensor(
                        mog[:, :, cols], mog[:, :, cols], 1.0,
                        norm_g[:, cols].rearrange("p (a c) -> p a c", a=1).to_broadcast([P, NT, N512]),
                        ALU.add, ALU.mult)
                    link(ins)
                elif part == "mix":
                    j = g - G_MIX
                    wait_group(dve, g)
                    dve.wait_ge(gate_row_in[j % 2], 16 * (j // 2 + 1))
                    dve.tensor_tensor(mixg[:, :, j * N512:(j + 1) * N512], pair(g),
                                      gate_row[:, j % 2:j % 2 + 1, :].to_broadcast([P, NT, N512]),
                                      ALU.add).then_inc(acc_read[g % 2], 1)

            def project(g):
                i = (g - G_PROJ) // 2
                c0 = GATE_OF[BRANCHES[i]] * D + (g % 2) * N512
                gate = mixg[:, :, c0:c0 + N512]
                cols = tok[:, :, (g % 2) * N512:(g % 2 + 1) * N512]
                wait_group(dve, g)
                dve.wait_ge(mix_th, 6)
                if g > G_PROJ + 2 and i == 1 or g == G_PROJ + 4:
                    dve.wait_ge(branch_sum, 1 if i == 1 else 2)
                dst = cols if i == 0 else tmp[:]
                ins = dve.scalar_tensor_tensor(dst, gate, 1.0, pair(g), ALU.add, ALU.mult)
                ins.then_inc(acc_read[g % 2], 1)
                wait_group_read(dve, g)
                if i < 2:
                    dve.sem_inc(branch_tmp, 1)
                else:
                    dve.tensor_tensor(cols, cols, tmp[:], ALU.add).then_inc(merged_ok, 1)
                    dve.wait_ge(merged_ok, g - G_PROJ - 3)

            def mixer(step):
                what, i = step[0], step[1] if len(step) > 1 else None
                if what == "gate":
                    gates()
                elif what == "na_scores":
                    na_scores(i)
                elif what == "na_values" and i % 8 == 7:
                    na_normalise(i // 8)
                elif what == "ml_scores":
                    ml_weights(i)
                elif what == "ml_values":
                    ml_out(i, step[2])
                    if (i, step[2]) == (ML_HEADS - 1, 1):
                        for n in range(NT):
                            wait_read(dve, "ml_values", i, 1, n)
                elif what == "ret_scores":
                    b = USES[("ret_scores", i)][0]
                    wait_filled(dve, "ret_scores", i)
                    if i == 0:
                        dve.wait_ge(decay_ok, 1)
                    dve.scalar_tensor_tensor(ret_p[:, i % 2, :, :], mix[:, b, :].rearrange("p (j t) -> p j t", j=NT),
                                             QK_SCALE, decay[:, i, :, :], ALU.mult, ALU.mult).then_inc(ret_wt, 1)
                    dve.wait_ge(ret_wt, i + 1)
                    dve.sem_inc(read[b], 1)
                elif what == "turn":
                    if i == "norm2":
                        scale_x(2)
                    turned_banks(i)

            dve.wait_ge(consts_in, 16 * 4)
            dve.wait_ge(x_in_sem, 16)
            dve.wait_ge(fixed_ok, 4)

            with dve.Fori(0, DEPTH):
                scale_x(1)
                wait_filled(dve, "params")
                dve.tensor_copy(cols64[:], mix[:, 0, 0:64]).then_inc(read[0], 1)
                dve.wait_ge(params_in, 16 * 9)
                dve.scalar_tensor_tensor(lg_e, lg_raw, -1.0, lg_raw, ALU.mult, ALU.max).then_inc(lg_a, 1)
                wait_read(dve, "params")
                turned_banks("norm1")
                dve.wait_ge(lg_b, 1)
                log_sigmoid(lg, lg_raw, lg_l)
                for h in range(RET_HEADS):
                    part = decay[:, h, :, :]
                    link(dve.tensor_scalar(part, dist[:, 1:2, :].rearrange("p a (j t) -> p (a j) t", j=NT),
                                           lg[:, RET_HEADS + h:RET_HEADS + h + 1], None, ALU.mult))
                    ins = dve.scalar_tensor_tensor(part, dist[:, 0:1, :].rearrange("p a (j t) -> p (a j) t", j=NT),
                                                   lg[:, h:h + 1], part, ALU.mult, ALU.add)
                    ins.then_inc(lg_c, 1)
                for u in range(UNITS):
                    g = u // 2
                    if u < 2 * G_PROJ and u % 2:
                        group(g)
                    if 2 * G_PROJ <= u < 2 * G_OUT and u % 2:
                        project(g)
                    if 2 * G_OUT <= u < 2 * G_UP and u % 2:
                        wait_group(dve, g)
                        cols = x[:, :, (g % 2) * N512:(g % 2 + 1) * N512]
                        dve.tensor_tensor(cols, cols, pair(g), ALU.add).then_inc(acc_read[g % 2], 1)
                        wait_group_read(dve, g)
                        dve.sem_inc(x_ok, 1)
                    if 2 * G_UP <= u < U_DOWN and u % 2:
                        c = g - G_UP
                        dve.wait_ge(up_tanh, c + 1)
                        if c >= 2:
                            wait_filled(dve, "up_turn", c - 2)
                        link(dve.scalar_tensor_tensor(up_s, up_th[:, c % 2, :, :], 1.0, pair(g)[:, :, 0:256],
                                                      ALU.add, ALU.mult))
                        ins = dve.scalar_tensor_tensor(up_v[:, c % 2, :, :], up_s, 0.5, pair(g)[:, :, 256:512],
                                                       ALU.mult, ALU.mult)
                        ins.then_inc(up_v_ok, 1)
                        dve.wait_ge(up_v_ok, c + 1)
                        dve.sem_inc(acc_read[g % 2], 1)
                    if 14 <= u < 22:
                        conv(u - 14)
                    if u in (18, 22):
                        silu((u - 18) // 4)
                    if 22 <= u < 26:
                        rotary(10 + (u - 22) // 2, u % 2)
                    for step in MIXER.get(u, []):
                        mixer(step)
                    if u == 37 + 1:
                        head_norm(0, h_ml, 0.5, mog)
                    if u == U_RET + 1 + RET_HEADS:
                        for h in range(RET_HEADS):
                            wait_read(dve, "ret_values", h)
                        head_norm(1, o_ret, 0.5, rgs)
                wait_group(dve, G_DOWN)
                for n in range(NT):
                    link(dve.tensor_tensor(x[:, n, :].rearrange("p (b c) -> p b c", b=2),
                                           x[:, n, :].rearrange("p (b c) -> p b c", b=2),
                                           acc[:, 2 * n:2 * n + 2, :], ALU.add))
                layer_end(dve, "dve")

            dve.wait_ge(fin_rs, 1)
            dve.wait_ge(final_g_in, 16)
            for n in range(NT):
                dve.scalar_tensor_tensor(tok[:, n, :], x[:, n, :], rstd[:, n:n + 1],
                                         ring[:, 0, 0:2, :].rearrange("p k c -> p (k c)"), ALU.mult,
                                         ALU.mult).then_inc(fin_y, 1)


def shape_constants():
    ident = np.eye(P, dtype=np.float32)
    half = DK // 2
    inv_freq = np.float32(10000.0) ** (-np.arange(half, dtype=np.float32) / half)
    angle = np.arange(T, dtype=np.float32)[:, None] * inv_freq.astype(np.float32)[None, :]
    cos = np.tile(np.cos(angle), (1, 2)).astype(np.float32)
    sin = np.tile(np.sin(angle), (1, 2)).astype(np.float32)
    m = np.arange(T).reshape(NT, P).T[:, :, None]
    n = np.arange(T)[None, None, :]
    dist = np.stack([np.maximum(n - m, 0), np.maximum(m - n, 0)], 1).astype(np.float32).reshape(P, 2, NT * T)
    col = np.arange(GRID_W)
    first = np.clip(col - WIN_COLS // 2, 0, GRID_W - WIN_COLS)
    inside = (col[None, :] >= first[:, None]) & (col[None, :] < first[:, None] + WIN_COLS)
    window = np.tile(np.where(inside, 0.0, -1.0e30), (2, 1)).astype(np.float32)
    return {"c_ident": ident, "c_cos": cos, "c_sin": sin, "c_dist": dist, "c_window": window}


def lay_out_bias(rpb):
    r, qc = np.arange(P) // GRID_W, np.arange(P) % GRID_W
    rows = np.arange(1, 7)[None, :] - r[:, None] - 3 + WIN_ROWS - 1
    rel = np.clip(np.arange(GRID_W)[None, :] - qc[:, None] + WIN_COLS - 1, 0, 2 * WIN_COLS - 2)
    picked = rpb[:, :, rows[:, :, None], rel[:, None, :]]
    return np.ascontiguousarray(picked.transpose(0, 2, 1, 3, 4)).reshape(rpb.shape[0], P, NA_HEADS * 6 * GRID_W)


_INS = ["x", "norm1_g", "w_in", "gate_b", "ret_decay_logit", "na_rpb", "ml_conv_w", "ml_conv_b", "ml_gate_b",
        "ml_norm_g", "w_ret_o", "w_na_o", "w_ml_o", "w_out", "norm2_g", "w_ffn_up", "w_ffn_down", "final_g"]


def kernel(**inputs):
    import concourse.bacc as bacc
    from concourse.bass_utils import run_bass_kernel_spmd

    nc = bacc.Bacc("TRN2", target_bir_lowering=False, num_devices=1)
    laid_out = {n: np.ascontiguousarray(inputs[n]) for n in _INS}
    laid_out["na_rpb"] = lay_out_bias(laid_out["na_rpb"])
    laid_out.update(shape_constants())
    arrays, args = {}, []
    for name, a in laid_out.items():
        arrays[f"in_{name}"] = a
        args.append(nc.dram_tensor(f"in_{name}", a.shape, mybir.dt.from_np(a.dtype), kind="ExternalInput").ap())
    args.append(nc.dram_tensor("out_0", (1, T, D), F32, kind="ExternalOutput").ap())
    trunk(nc, *args)
    r = run_bass_kernel_spmd(nc, [arrays], core_ids=[0])
    return r.results[0]["out_0"]
```

```python
from contextlib import ExitStack

import numpy as np
import concourse.bass as bass
from concourse import mybir

F32 = mybir.dt.float32
F32R = mybir.dt.float32r
ALU = mybir.AluOpType
ACT = mybir.ActivationFunctionType
AX_X = mybir.AxisListType.X

P = 128
T = 256
NT = T // P
D = 1024
KD = D // P
DEPTH = 2
GRID_W = 64
ROWS = T // GRID_W
WIN_ROWS, WIN_COLS = 8, 16
RET_HEADS, NA_HEADS, ML_HEADS = 4, 16, 4
DK, DV, NA_DH = 128, 256, 64
CONV_W = 5
FF = 2816
EPS = 1e-6
QK_SCALE = float(DK) ** -0.5
NA_SCALE = float(NA_DH) ** -0.5
LOWEST = -3.0e38

RQ, RK, RV, RG, NQ, NK, NV, MQ, MK, MV, MO, MGATE, MIX = np.cumsum(
    [0, 512, 512, 1024, 1024, 1024, 1024, 1024, 512, 512, 1024, 1024, 16]).tolist()

N512 = 512
UK = 2
UPG = KD // UK
RAW = 4
SPLIT = 3

IN_GROUPS = ([("nq", NQ), ("nq", NQ + N512), ("nk", NK), ("nk", NK + N512), ("nv", NV), ("nv", NV + N512),
              ("mq", MQ), ("mk", MK), ("mv", MV), ("mv", MV + N512), ("rq", RQ), ("rk", RK),
              ("rv", RV), ("rv", RV + N512)]
             + [("mix", MIX + j * N512) for j in range(6)]
             + [("mo", MO), ("mo", MO + N512), ("rg", RG), ("rg", RG + N512)])
FEATURE_MAJOR = ("nq", "nk", "mq", "mk")
G_ML, G_MV, G_ROT, G_RV, G_MIX, G_MO, G_RG = 6, 8, 10, 12, 14, 20, 22
G_PROJ = len(IN_GROUPS)
BRANCHES = ("na", "ml", "ret")
G_OUT = G_PROJ + 2 * len(BRANCHES)
GROUPS = G_OUT + 2
GATE_OF = {"ret": 0, "na": 1, "ml": 2}
N_UP = FF // 256

UNITS = [("w", g, i) for g in range(GROUPS) for i in range(UPG)]
for c in range(N_UP + 1):
    UNITS += [("up", c, i) for i in range(UPG) if c < N_UP] + [("down", c - 1, i) for i in range(2) if c]
AT = {unit: v for v, unit in enumerate(UNITS)}


def last_of(g):
    return AT[("w", g, UPG - 1)]


S_NA = 2 * 6
S_ML = S_NA + NA_HEADS + 2
S_RET = S_ML + 9


def mixer_schedule():
    after = {}

    def put(slot, *step):
        after.setdefault(2 * slot + 1, []).append(step)

    put(1, "gate")
    put(3, "gate_rows")
    put(7, "gate_turn")
    for h in range(NA_HEADS):
        put(S_NA + h, "na_scores", h)
    for h in range(NA_HEADS):
        put(S_NA + h + 1, "na_turn", h)
        put(S_NA + h + 2, "na_values", h)
    for h in range(ML_HEADS):
        put(S_ML + 2 * h, "ml_scores", h)
        put(S_ML + 2 * h + 1, "ml_values", h, 0)
        put(S_ML + 2 * h + 2, "ml_values", h, 1)
    put(S_RET, "turn", "rot")
    for h in range(RET_HEADS):
        put(S_RET + 1 + h, "ret_scores", h)
        put(S_RET + 2 + h, "ret_values", h)
    put(2 * G_PROJ + 1, "turn", "ml")
    put(2 * G_PROJ + 4, "turn", "ret")
    put(2 * G_OUT - 1, "turn", "merged")
    put(2 * GROUPS - 1, "turn", "norm2")
    for c in range(N_UP):
        v = AT[("up", c + 1, 0)] if c < N_UP - 1 else AT[("down", c - 1, 1)]
        after.setdefault(v, []).append(("up_turn", c))
    for v in after:
        after[v].sort(key=lambda s: s[0] in ("na_scores", "ml_scores", "ret_scores"))
    return after


MIXER = mixer_schedule()


def bank_uses():
    count, uses = [0] * 4, {}

    def use(bank, *name):
        count[bank] += 1
        uses[name] = (bank, count[bank])

    def turn(name):
        for b in range(4):
            use(b, "turn", name, b)

    turn("norm1")
    for v, (kind, c, k) in enumerate(UNITS):
        if kind == "up" and k == 0:
            use(0, "up", c, 0)
            use(1, "up", c, 1)
        for step in MIXER.get(v, []):
            what, i = step[0], step[1] if len(step) > 1 else None
            if what in ("gate", "gate_rows"):
                use(0, what)
            elif what == "gate_turn":
                use(1, "gate_turn")
            elif what == "na_scores":
                use(0, "na_scores", i)
            elif what == "na_turn":
                use(1, "na_turn", i)
            elif what == "na_values" and i % 2 == 0:
                use(2 + i // 2 % 2, "na_values", i // 2)
            elif what == "ml_scores":
                use(0, "ml_scores", i)
                use(1, "ml_rows", i)
            elif what == "ml_values":
                use(2, "ml_values", i, step[2], 0)
                use(3, "ml_values", i, step[2], 1)
            elif what == "ret_scores":
                use(i % 2, "ret_scores", i)
            elif what == "ret_values":
                use(2 + i % 2, "ret_values", i)
            elif what == "turn":
                turn(i)
            elif what == "up_turn":
                use(2 + i % 2, "up_turn", i)
    return uses


USES = bank_uses()
N_COLS = 72
COL_NORM1, COL_NORM2, COL_ML, COL_CONV_W, COL_CONV_B = 0, 8, 16, 24, 64
COLUMN = {"norm1": COL_NORM1, "norm2": COL_NORM2, "ml": COL_ML}
BUFFER = {"norm1": 0, "na": 1, "ml": 0, "ret": 1, "merged": 0, "norm2": 1}


def trunk(nc, x_in, norm1_g, w_in, gate_b, ret_decay_logit, na_bias, ml_conv_w, ml_conv_b, ml_gate_b,
          ml_norm_g, w_ret_o, w_na_o, w_ml_o, w_out, norm2_g, w_ffn_up, w_ffn_down, final_g,
          c_ident, c_cos, c_sin, c_dist, c_window, c_spread, out):
    ctx = ExitStack()
    with ctx:
        def sb(name, shape, dtype=F32):
            return ctx.enter_context(nc.sbuf_tensor(name, shape, dtype))

        names = []

        def sem(name):
            s = ctx.enter_context(nc.semaphore(name))
            names.append((name, s))
            return s

        raw = sb("raw", [P, RAW, UK, N512])
        w_hi = sb("w_hi", [P, SPLIT, UK, N512], F32R)
        w_lo = sb("w_lo", [P, SPLIT, UK, N512], F32R)
        x = sb("x", [P, NT, D])
        turned_hi = sb("turned_hi", [P, 2, KD, T], F32R)
        turned_lo = sb("turned_lo", [P, 2, KD, T], F32R)
        up_hi = sb("up_hi", [P, 2, 2, T], F32R)
        up_lo = sb("up_lo", [P, 2, 2, T], F32R)
        gate_hi = sb("gate_hi", [P, KD, 16], F32R)
        gate_lo = sb("gate_lo", [P, KD, 16], F32R)
        tok = sb("tok", [P, NT, D])
        region_a = sb("region_a", [P, 6144])
        region_b = sb("region_b", [P, 6144])
        gate_row = sb("gate_row", [P, 2, N512])
        conv_in = sb("conv_in", [P, 8, T + CONV_W - 1])
        conv_out = sb("conv_out", [P, 8, T])
        mv = sb("mv", [P, NT, ML_HEADS, DV + 1])
        rot = sb("rot", [P, NT, 2, RET_HEADS, DK])
        rv = sb("rv", [P, NT, D])
        small = sb("small", [P, 2048])
        wide = sb("wide", [P, NT, N512])
        ident = sb("ident", [P, P])
        cos = sb("cos", [P, NT, DK])
        sin = sb("sin", [P, NT, DK])
        window = sb("window", [P, GRID_W])
        spread = sb("spread", [16, 2, 64])
        cols_all = sb("cols_all", [P, DEPTH * N_COLS])
        cols = sb("cols", [P, N_COLS])
        gate_w_all = sb("gate_w_all", [P, DEPTH * KD * 16])
        gbias_all = sb("gbias_all", [64, DEPTH * 2])
        gbias = sb("gbias", [64, 2])
        lg_all = sb("lg_all", [P, DEPTH * 8])
        acol = sb("acol", [P, NT, 64])
        emt = sb("emt", [P, NT, 64])
        stat = sb("stat", [P, 108])

        nqT = region_a[:, 0:2048].rearrange("p (k t) -> p k t", k=8)
        nkT = region_a[:, 2048:4096].rearrange("p (k t) -> p k t", k=8)
        nv = region_a[:, 4096:6144].rearrange("p (n c) -> p n c", n=NT)
        mixg = region_a[:, 0:6144].rearrange("p (n c) -> p n c", n=NT)
        bias = region_b[:, 0:6144].rearrange("p (h j c) -> p h j c", h=NA_HEADS, j=6)
        rgs = region_b[:, 0:2048].rearrange("p (n c) -> p n c", n=NT)
        decay = region_b[:, 2048:4096].rearrange("p (h j t) -> p h j t", h=RET_HEADS, j=NT)
        rot_T = region_b[:, 4096:6144].rearrange("p (k t) -> p k t", k=8)
        wide_flat = wide[:, :, :].rearrange("p s c -> p (s c)")
        dist = wide[:, :, :].rearrange("p s (j t) -> p s j t", j=NT)
        up_th = wide[:, :, :].rearrange("p s (n c) -> p s n c", n=NT)
        h_ml = conv_in[:, :, :].rearrange("p k c -> p (k c)")[:, 0:2048].rearrange("p (n c) -> p n c", n=NT)
        o_ret = rot[:, :, :, :, :].rearrange("p n a h d -> p n (a h d)")
        na_p = small[:, 0:1024].rearrange("p (s n c) -> p s n c", s=2, n=NT)
        na_pT = small[:, 1024:2048].rearrange("p (s n c) -> p s n c", s=2, n=NT)
        ml_e = small[:, 0:1024].rearrange("p (d j t) -> p d j t", d=2, j=NT)
        ml_w = small[:, 1024:2048].rearrange("p (d j t) -> p d j t", d=2, j=NT)
        ret_p = small[:, 0:1024].rearrange("p (s j t) -> p s j t", s=2, j=NT)
        up_s = small[:, 0:512].rearrange("p (n c) -> p n c", n=NT)
        up_v = small[:, 512:1536].rearrange("p (s n c) -> p s n c", s=2, n=NT)
        rows = small[0:N_COLS, 0:DEPTH * P].rearrange("p (l c) -> p l c", l=DEPTH)
        gw = tok[0:64, :, :].rearrange("p n c -> p (n c)").rearrange("p (s t) -> p s t", s=8)
        g_i, g_f, g_e, g_l, g_b, g_a, g_m, g_mt = (gw[:, i, :] for i in range(8))
        g_nm, g_one, g_raw = g_e, g_m, g_mt[0:16, :]
        ss, rstd = stat[:, 0:2], stat[:, 2:4]
        lg_raw, lg_e, lg_l = (small[:, 1024 + 16 * i:1040 + 16 * i] for i in range(3))
        na_max = stat[:, 4:8].rearrange("p (s n) -> p s n", s=2)
        na_sum = stat[:, 8:12].rearrange("p (s n) -> p s n", s=2)
        den = stat[:, 12:16].rearrange("p (d n) -> p d n", d=2)
        rden = stat[:, 16:20].rearrange("p (d n) -> p d n", d=2)
        bn = stat[:, 20:68].rearrange("p (g s) -> p g s", g=8)
        mean_var = stat[:, 68:84].rearrange("p (g s) -> p g s", g=8)
        rs8 = stat[:, 84:92]
        lg = stat[:, 100:108]
        half = stat[:, 92:100]

        acc = ctx.enter_context(nc.psum_tensor("acc", [P, 4, N512], F32))
        mix = ctx.enter_context(nc.psum_tensor("mix", [P, 4, N512], F32))

        unit_in = [sem(f"unit_in{i}") for i in range(RAW)]
        hi_ok, lo_ok = sem("hi_ok"), sem("lo_ok")
        unit_used = sem("unit_used")
        acc_read = [sem("acc_read0"), sem("acc_read1")]
        filled = [sem(f"filled{b}") for b in range(4)]
        read = [sem(f"read{b}") for b in range(4)]
        turn_hi = sem("turn_hi")
        bias_in, dist_in = sem("bias_in"), sem("dist_in")
        gate_row_in = [sem("gate_row_in0"), sem("gate_row_in1")]
        cols_ok = sem("cols_ok")
        sumsq = sem("sumsq")
        rstd_ok = sem("rstd_ok")
        xs_ok = sem("xs_ok")
        gate_hi_ok, gate_lo_ok = sem("gate_hi_ok"), sem("gate_lo_ok")
        decay_arg, decay_ok = sem("decay_arg"), sem("decay_ok")
        g_abs, g_ln, g_rows = sem("g_abs"), sem("g_ln"), sem("g_rows")
        bias_ok = sem("bias_ok")
        na_soft = sem("na_soft")
        na_exp = sem("na_exp")
        na_prob = sem("na_prob")
        conv_ok, conv_th, conv_silu = sem("conv_ok"), sem("conv_th"), sem("conv_silu")
        rot_ok = sem("rot_ok")
        ml_exp, ml_mask, ml_wt = sem("ml_exp"), sem("ml_mask"), sem("ml_wt")
        bn_ok = sem("bn_ok")
        rs_ok = sem("rs_ok")
        y_ok = sem("y_ok")
        ret_wt = sem("ret_wt")
        mo_th, rg_th = sem("mo_th"), sem("rg_th")
        mix_th = sem("mix_th")
        branch_sum = sem("branch_sum")
        x_ok = sem("x_ok")
        up_tanh, up_v_ok = sem("up_tanh"), sem("up_v_ok")
        dve_step, act_step, pool_step = sem("dve_step"), sem("act_step"), sem("pool_step")
        pad_ok = sem("pad_ok")
        arrived = sem("arrived")
        layer_sems = list(names)
        consts_in, params_in, x_in_sem, out_sem = sem("consts_in"), sem("params_in"), sem("x_in"), sem("out_sem")
        fixed_ok = sem("fixed_ok")
        pre_turn, pre_cols, pre_abs, pre_ln, pre_lg = (
            sem("pre_turn"), sem("pre_cols"), sem("pre_abs"), sem("pre_ln"), sem("pre_lg"))
        fin_sq, fin_rs, fin_step, fin_y = sem("fin_sq"), sem("fin_rs"), sem("fin_step"), sem("fin_y")
        final_g_in = sem("final_g_in")
        go = {e: sem(f"go_{e}") for e in ("act", "dve", "pe", "pool")}

        block = ctx.enter_context(nc.Block())

        def wait_unit(eng, v):
            eng.wait_ge(unit_used, v + 1)

        def wait_group(eng, g):
            wait_unit(eng, last_of(g))

        def wait_group_read(eng, g):
            eng.wait_ge(acc_read[g % 2], g // 2 + 1)

        def wait_filled(eng, *name):
            bank, n = USES[name]
            eng.wait_ge(filled[bank], n)

        def wait_read(eng, *name):
            bank, n = USES[name]
            eng.wait_ge(read[bank], n)

        def pair(g):
            return acc[:, 2 * (g % 2):2 * (g % 2) + 2, :]

        def pair_fm(g):
            return pair(g).rearrange("p b (k t) -> p (b k) t", t=T)

        def layer_end(eng, key):
            eng.drain().then_inc(arrived, 1)
            eng.wait_ge(go[key], 1)
            eng.sem_clear(go[key])

        class Steps:

            def __init__(self, eng, semaphore):
                self.eng, self.semaphore, self.n = eng, semaphore, 0

            def link(self, ins):
                self.n += 1
                ins.then_inc(self.semaphore, 1)
                self.eng.wait_ge(self.semaphore, self.n)

        @block.sync
        def _(sp):
            sp.dma_start(x[:], x_in.rearrange("b (n p) c -> p (b n) c", p=P)).then_inc(x_in_sem, 16)

            def source(l, v):
                kind, g, i = UNITS[v]
                one, rows_ = bass.ds(l, 1), slice(i * UK * P, (i + 1) * UK * P)
                if kind == "down":
                    r = (2 * g + i) * P
                    return [w_ffn_down[one, r:r + P, :].rearrange("a p (k c) -> p (a k) c", k=2)]
                if kind == "up":
                    return [w_ffn_up[one, rows_, s:s + 256].rearrange("a (k p) c -> p (a k) c", p=P)
                            for s in (g * 256, FF + g * 256)]
                if g < G_PROJ:
                    w, col = w_in, IN_GROUPS[g][1]
                elif g < G_OUT:
                    w = {"na": w_na_o, "ml": w_ml_o, "ret": w_ret_o}[BRANCHES[(g - G_PROJ) // 2]]
                    col = g % 2 * N512
                else:
                    w, col = w_out, g % 2 * N512
                return [w[one, rows_, col:col + N512].rearrange("a (k p) c -> p (a k) c", p=P)]

            with sp.Fori(0, DEPTH) as l:
                for v in range(len(UNITS)):
                    slot = v % RAW
                    if v >= RAW:
                        sp.wait_ge(lo_ok, v - RAW + 1)
                    parts = source(l, v)
                    width = N512 // len(parts)
                    for i, src in enumerate(parts):
                        sp.dma_start(raw[:, slot, :, width * i:width * (i + 1)], src).then_inc(unit_in[slot], 16)
                sp.wait_ge(arrived, 4)
                for _, s in layer_sems:
                    sp.sem_clear(s)
                for e in go.values():
                    sp.sem_inc(e, 1)
            sp.dma_start(raw[:, 0, :, :], final_g.partition_broadcast(P).rearrange(
                "p (k c) -> p k c", k=2)).then_inc(final_g_in, 16)
            for n in range(NT):
                sp.wait_ge(fin_y, n + 1)
                sp.dma_start(out[0, n * P:(n + 1) * P, :], tok[:, n, :]).then_inc(out_sem, 16)
            sp.wait_ge(out_sem, 16 * NT)

        def unit_in_count(v):
            return sum(32 if UNITS[w][0] == "up" else 16 for w in range(v % RAW, v + 1, RAW))

        @block.tensor
        def _(pe):
            def begin(*name):
                bank, n = USES[name]
                if n > 1:
                    pe.wait_ge(read[bank], n - 1)
                return bank

            def turn(name, src):
                for b in range(4):
                    begin("turn", name, b)
                    if name == "merged":
                        pe.wait_ge(branch_sum, 5 + b // 2)
                    if name == "ml":
                        pe.wait_ge(y_ok, 1 + b // 2)
                    for j in range(2):
                        for n in range(NT):
                            c = (2 * b + j) * P
                            ins = pe.transpose(mix[:, b, j * T + n * P:j * T + (n + 1) * P],
                                               src[:, n, c:c + P], ident[:])
                    ins.then_inc(filled[b], 1)

            def products(dst, left_hi, left_lo, right_hi, right_lo, first, last, **kw):
                pe.matmul(dst, left_hi, right_hi, start=first, stop=False, **kw)
                pe.matmul(dst, left_hi, right_lo, start=False, stop=False, **kw)
                return pe.matmul(dst, left_lo, right_hi, start=False, stop=last, **kw)

            def mixer(step):
                what, h = step[0], step[1] if len(step) > 1 else None
                if what == "gate":
                    b = begin("gate")
                    pe.wait_ge(gate_lo_ok, 1)
                    for k in range(KD):
                        ins = products(mix[0:16, b, 0:T], gate_hi[:, k, :], gate_lo[:, k, :],
                                       turned_hi[:, 0, k, :], turned_lo[:, 0, k, :], k == 0, k == KD - 1)
                    ins.then_inc(filled[b], 1)
                elif what == "gate_rows":
                    wait_read(pe, "gate")
                    b = begin("gate_rows")
                    for i in range(2):
                        ins = pe.matmul(mix[0:64, b, i * T:(i + 1) * T], spread[:, i, :], g_raw,
                                        start=True, stop=True)
                    ins.then_inc(filled[b], 1)
                elif what == "gate_turn":
                    b = begin("gate_turn")
                    pe.wait_ge(g_rows, 1)
                    for i, src in enumerate((g_a, g_mt)):
                        for n in range(NT):
                            o = (i * NT + n) * 64
                            ins = pe.transpose(mix[:, b, o:o + 64], src[:, n * P:(n + 1) * P],
                                               ident[0:64, 0:64])
                    ins.then_inc(filled[b], 1)
                elif what == "na_scores":
                    b = begin("na_scores", h)
                    if h == 0:
                        for g in range(4):
                            wait_group_read(pe, g)
                    r = NA_DH * (h % 2)
                    for n in range(NT):
                        ins = pe.matmul(mix[:, b, n * T:(n + 1) * T],
                                        nqT[r:r + NA_DH, h // 2, n * P:(n + 1) * P],
                                        nkT[r:r + NA_DH, h // 2, :], start=True, stop=True)
                    ins.then_inc(filled[b], 1)
                elif what == "na_turn":
                    b = begin("na_turn", h)
                    pe.wait_ge(na_prob, h + 1)
                    for k in range(NT):
                        for n in range(NT):
                            ins = pe.transpose(mix[:, b, k * T + n * P:k * T + (n + 1) * P],
                                               na_p[:, h % 2, n, k * P:(k + 1) * P], ident[:])
                    ins.then_inc(filled[b], 1)
                elif what == "na_values":
                    b = USES[("na_values", h // 2)][0]
                    if h % 2 == 0:
                        begin("na_values", h // 2)
                    if h == 0:
                        wait_group_read(pe, 4)
                        wait_group_read(pe, 5)
                    wait_read(pe, "na_turn", h)
                    r = NA_DH * (h % 2)
                    for k in range(NT):
                        ins = pe.matmul(mix[r:r + NA_DH, b, 0:T], nv[:, k, h * NA_DH:(h + 1) * NA_DH],
                                        na_pT[:, h % 2, k, :], start=(k == 0), stop=(k == NT - 1))
                    if h % 2:
                        ins.then_inc(filled[b], 1)
                elif what == "ml_scores":
                    b = begin("ml_scores", h)
                    if h == 0:
                        pe.wait_ge(conv_silu, 2)
                    for j in range(NT):
                        ins = pe.matmul(mix[:, b, j * T:(j + 1) * T],
                                        conv_out[:, ML_HEADS + h, j * P:(j + 1) * P],
                                        conv_out[:, h, :], start=True, stop=True)
                    ins.then_inc(filled[b], 1)
                    b = begin("ml_rows", h)
                    for d in range(2):
                        r = 32 * d + h
                        ins = pe.matmul(mix[:, b, d * T:(d + 1) * T],
                                        ident[0:64, r:r + 1].to_broadcast([64, P]), g_nm,
                                        start=True, stop=True)
                    ins.then_inc(filled[b], 1)
                elif what == "ml_values":
                    d = step[2]
                    if (h, d) == (0, 0):
                        wait_group_read(pe, G_MV)
                        wait_group_read(pe, G_MV + 1)
                    pe.wait_ge(ml_wt, 2 * h + d + 1)
                    for n in range(NT):
                        b = begin("ml_values", h, d, n)
                        js = range(0, n + 1) if d == 0 else range(n, NT)
                        for j in js:
                            ins = pe.matmul(mix[:, b, 0:DV + 1], ml_w[:, d, j, n * P:(n + 1) * P],
                                            mv[:, j, h, :], start=(j == js[0]), stop=(j == js[-1]))
                        ins.then_inc(filled[b], 1)
                elif what == "ret_scores":
                    b = begin("ret_scores", h)
                    if h == 0:
                        for i in range(4):
                            wait_read(pe, "turn", "rot", i)
                    for j in range(NT):
                        ins = pe.matmul(mix[:, b, j * T:(j + 1) * T],
                                        rot_T[:, RET_HEADS + h, j * P:(j + 1) * P],
                                        rot_T[:, h, :], start=True, stop=True)
                    ins.then_inc(filled[b], 1)
                elif what == "ret_values":
                    b = begin("ret_values", h)
                    if h == 0:
                        wait_group_read(pe, G_RV)
                        wait_group_read(pe, G_RV + 1)
                    pe.wait_ge(ret_wt, h + 1)
                    for n in range(NT):
                        for j in range(NT):
                            ins = pe.matmul(mix[:, b, n * T:(n + 1) * T], ret_p[:, h % 2, j, n * P:(n + 1) * P],
                                            rv[:, j, h * DV:(h + 1) * DV], start=(j == 0), stop=(j == NT - 1))
                    ins.then_inc(filled[b], 1)
                elif what == "turn":
                    if h == "rot":
                        pe.wait_ge(rot_ok, 4)
                    elif h == "ret":
                        pe.wait_ge(y_ok, 3)
                    elif h == "norm2":
                        pe.wait_ge(xs_ok, 4)
                    turn(h, {"rot": o_ret, "ml": h_ml, "ret": o_ret, "merged": tok, "norm2": tok}[h])
                elif what == "up_turn":
                    b = begin("up_turn", h)
                    pe.wait_ge(up_v_ok, h + 1)
                    for j in range(2):
                        for n in range(NT):
                            ins = pe.transpose(mix[:, b, j * T + n * P:j * T + (n + 1) * P],
                                               up_v[:, h % 2, n, j * P:(j + 1) * P], ident[:])
                    ins.then_inc(filled[b], 1)

            def left_of(g):
                if g < G_PROJ:
                    return "norm1"
                return BRANCHES[(g - G_PROJ) // 2] if g < G_OUT else "merged"

            pe.wait_ge(consts_in, 16 * 5)
            pe.wait_ge(params_in, 16 * 17)
            for l in range(DEPTH):
                ins = pe.transpose(mix[:, 0, l * N_COLS:(l + 1) * N_COLS], rows[:, l, :],
                                   ident[0:N_COLS, 0:N_COLS])
            ins.then_inc(pre_turn, 1)
            pe.wait_ge(pre_cols, 1)

            with pe.Fori(0, DEPTH):
                pe.wait_ge(xs_ok, 2)
                turn("norm1", tok)
                for v, (kind, g, i) in enumerate(UNITS):
                    slot = v % SPLIT
                    pe.wait_ge(lo_ok, v + 1)
                    hi, lo = w_hi[:, slot, :, :], w_lo[:, slot, :, :]
                    if kind == "w":
                        name = left_of(g)
                        buf = BUFFER[name]
                        if i == 0 and g >= 2:
                            wait_group_read(pe, g - 2)
                        if name == "na":
                            for p in range(UK * i, UK * i + UK):
                                wait_read(pe, "na_values", p)
                        else:
                            wait_read(pe, "turn", name, i)
                        for k in range(UK):
                            kk = UK * i + k
                            if g >= G_PROJ or IN_GROUPS[g][0] not in FEATURE_MAJOR:
                                for n in range(NT):
                                    c = slice(n * P, (n + 1) * P)
                                    ins = products(pair(g)[:, n, :], turned_hi[:, buf, kk, c],
                                                   turned_lo[:, buf, kk, c], hi[:, k, :], lo[:, k, :],
                                                   kk == 0, kk == KD - 1)
                            else:
                                for j in range(4):
                                    c = slice(j * P, (j + 1) * P)
                                    ins = products(pair_fm(g)[:, j, :], hi[:, k, c], lo[:, k, c],
                                                   turned_hi[:, buf, kk, :], turned_lo[:, buf, kk, :],
                                                   kk == 0 and j % 2 == 0, kk == KD - 1,
                                                   skip_group_check=True)
                    elif kind == "up":
                        if i == 0:
                            for n in range(NT):
                                begin("up", g, n)
                        wait_read(pe, "turn", "norm2", i)
                        for k in range(UK):
                            kk = UK * i + k
                            for n in range(NT):
                                c = slice(n * P, (n + 1) * P)
                                ins = products(mix[:, n, :], turned_hi[:, 1, kk, c], turned_lo[:, 1, kk, c],
                                               hi[:, k, :], lo[:, k, :], kk == 0, kk == KD - 1)
                    else:
                        if (g, i) == (0, 0):
                            wait_group_read(pe, GROUPS - 2)
                            wait_group_read(pe, GROUPS - 1)
                        wait_read(pe, "up_turn", g)
                        for n in range(NT):
                            c = slice(n * P, (n + 1) * P)
                            for j in range(2):
                                ins = products(acc[:, 2 * n + j, :], up_hi[:, g % 2, i, c], up_lo[:, g % 2, i, c],
                                               hi[:, j, :], lo[:, j, :], (g, i) == (0, 0),
                                               (g, i) == (N_UP - 1, 1))
                    ins.then_inc(unit_used, 1)
                    for step in MIXER.get(v, []):
                        mixer(step)
                layer_end(pe, "pe")

        @block.scalar
        def _(act):
            steps = Steps(act, act_step)
            split_to = [0]

            def split(end):
                while split_to[0] < min(end, len(UNITS)):
                    v = split_to[0]
                    act.wait_ge(unit_in[v % RAW], unit_in_count(v))
                    if v >= SPLIT:
                        wait_unit(act, v - SPLIT)
                    act.activation(w_hi[:, v % SPLIT, :, :], raw[:, v % RAW, :, :], ACT.Copy).then_inc(hi_ok, 1)
                    split_to[0] += 1

            def turned_banks(name):
                for b in range(4):
                    wait_filled(act, "turn", name, b)
                    src = mix[:, b, :].rearrange("p (k t) -> p k t", k=2)
                    if name == "rot":
                        act.activation(rot_T[:, 2 * b:2 * b + 2, :], src, ACT.Copy).then_inc(read[b], 1)
                        continue
                    dst = turned_hi[:, BUFFER[name], 2 * b:2 * b + 2, :]
                    if name in COLUMN:
                        if b == 0 and name == "norm1":
                            act.wait_ge(cols_ok, 1)
                        for j in range(2):
                            c = COLUMN[name] + 2 * b + j
                            ins = act.activation(dst[:, j, :], src[:, j, :], ACT.Copy, scale=cols[:, c:c + 1])
                    else:
                        ins = act.activation(dst, src, ACT.Copy, scale=0.5 if name == "merged" else 1.0)
                    ins.then_inc(turn_hi, 1)

            def squares(x_count):
                for n in range(NT):
                    if x_count:
                        act.wait_ge(x_ok, x_count)
                    junk = (wide_flat, small[:, 0:D])[n]
                    act.activation(junk, x[:, n, :], ACT.Square, accum_out=ss[:, n:n + 1]).then_inc(sumsq, 1)

            def group(g):
                part = IN_GROUPS[g][0]
                half_of = slice((g % 2) * N512, (g % 2 + 1) * N512)
                if part in ("nq", "nk"):
                    dst = (nqT if part == "nq" else nkT)[:, 4 * (g % 2):4 * (g % 2) + 4, :]
                    wait_group(act, g)
                    act.activation(dst, pair_fm(g), ACT.Copy).then_inc(acc_read[g % 2], 1)
                elif part in ("mq", "mk"):
                    k = 0 if part == "mq" else 4
                    wait_group(act, g)
                    act.wait_ge(pad_ok, 2)
                    act.activation(conv_in[:, k:k + 4, 2:2 + T], pair_fm(g), ACT.Copy).then_inc(acc_read[g % 2], 1)
                elif part in ("nv", "rv"):
                    wait_group(act, g)
                    act.activation((nv if part == "nv" else rv)[:, :, half_of], pair(g),
                                   ACT.Copy).then_inc(acc_read[g % 2], 1)
                elif part == "mv":
                    wait_group(act, g)
                    for n in range(NT):
                        ins = act.activation(mv[:, n, 2 * (g % 2):2 * (g % 2) + 2, 0:DV],
                                             pair(g)[:, n, :].rearrange("p (h d) -> p h d", h=2), ACT.Copy)
                    ins.then_inc(acc_read[g % 2], 1)
                elif part == "mo":
                    wait_group(act, g)
                    if g == G_MO:
                        act.wait_ge(decay_arg, RET_HEADS)
                    else:
                        act.wait_ge(y_ok, 1)
                    act.activation(wide[:], pair(g), ACT.Tanh, scale=0.5).then_inc(acc_read[g % 2], 1)
                elif part == "rg":
                    wait_group(act, g)
                    if g == G_RG:
                        act.wait_ge(y_ok, 2)
                    else:
                        wait_group_read(act, g - 1)
                    act.activation(wide[:], pair(g), ACT.Tanh, scale=0.5).then_inc(rg_th, 1)
                elif part == "mix":
                    j = g - G_MIX
                    wait_group_read(act, g)
                    if j + 2 < 6:
                        act.dma_start(gate_row[:, j % 2, :], gate_b[bass.ds(layer[0], 1), (j + 2) * N512:
                                      (j + 3) * N512].to_broadcast([P, N512])).then_inc(gate_row_in[j % 2], 16)
                    part = mixg[:, :, j * N512:(j + 1) * N512]
                    act.activation(part, part, ACT.Tanh, scale=0.5).then_inc(mix_th, 1)

            def mixer(step):
                what, h = step[0], step[1] if len(step) > 1 else None
                if what == "gate":
                    wait_filled(act, "gate")
                    b = USES[("gate",)][0]
                    act.activation(g_raw, mix[0:16, b, 0:T], ACT.Copy).then_inc(read[b], 1)
                elif what == "gate_rows":
                    act.wait_ge(g_abs, 1)
                    steps.link(act.activation(g_e, g_e, ACT.Exp, scale=-1.0))
                    act.activation(g_l, g_e, ACT.Ln, bias=1.0).then_inc(g_ln, 1)
                elif what == "gate_turn":
                    wait_filled(act, "gate_turn")
                    b = USES[("gate_turn",)][0]
                    act.activation(acol[:], mix[:, b, 0:2 * 64].rearrange("p (n r) -> p n r", n=NT), ACT.Copy)
                    act.activation(emt[:], mix[:, b, 2 * 64:4 * 64].rearrange("p (n r) -> p n r", n=NT),
                                   ACT.Exp, scale=-1.0).then_inc(read[b], 1)
                elif what == "na_scores":
                    act.wait_ge(na_soft, h + 1)
                    for n in range(NT):
                        ins = act.activation(na_p[:, h % 2, n, :], na_p[:, h % 2, n, :], ACT.Exp,
                                             bias=na_max[:, h % 2, n:n + 1], accum_out=na_sum[:, h % 2, n:n + 1])
                    ins.then_inc(na_exp, 1)
                elif what == "na_turn":
                    wait_filled(act, "na_turn", h)
                    b = USES[("na_turn", h)][0]
                    act.activation(na_pT[:, h % 2, :, :], mix[:, b, :].rearrange("p (k c) -> p k c", k=NT),
                                   ACT.Copy).then_inc(read[b], 1)
                elif what == "na_values" and h % 2:
                    p = h // 2
                    wait_filled(act, "na_values", p)
                    act.activation(turned_hi[:, 1, p, :], mix[:, USES[("na_values", p)][0], 0:T],
                                   ACT.Copy).then_inc(turn_hi, 1)
                elif what == "ml_scores":
                    wait_filled(act, "ml_rows", h)
                    b = USES[("ml_rows", h)][0]
                    if h == 0:
                        wait_read(act, "gate_turn")
                    else:
                        act.wait_ge(ml_wt, 2 * h)
                    for d, j, t0, t1 in ((0, 0, 0, T), (0, 1, P, T), (1, 0, 0, P), (1, 1, 0, T)):
                        r = 32 * d + h
                        ins = act.activation(ml_e[:, d, j, t0:t1], mix[:, b, d * T + t0:d * T + t1], ACT.Exp,
                                             bias=acol[:, j, r:r + 1])
                    ins.then_inc(read[b], 1)
                elif what == "ret_values":
                    wait_filled(act, "ret_values", h)
                    b = USES[("ret_values", h)][0]
                    act.activation(o_ret[:, :, h * DV:(h + 1) * DV], mix[:, b, :].rearrange(
                        "p (n c) -> p n c", n=NT), ACT.Copy).then_inc(read[b], 1)
                elif what == "turn":
                    if h == "norm2":
                        squares(2)
                    turned_banks(h)
                elif what == "up_turn":
                    wait_filled(act, "up_turn", h)
                    b = USES[("up_turn", h)][0]
                    if h >= 2:
                        wait_unit(act, AT[("down", h - 2, 1)])
                    act.activation(up_hi[:, h % 2, :, :], mix[:, b, :].rearrange("p (k t) -> p k t", k=2),
                                   ACT.Copy).then_inc(turn_hi, 1)

            act.dma_start(ident[:], c_ident).then_inc(consts_in, 16)
            for i, src in enumerate((norm1_g, norm2_g, ml_norm_g)):
                for l in range(DEPTH):
                    act.dma_start(rows[8 * i:8 * i + 8, l, :], src[l].rearrange("(k c) -> k c", c=P)
                                  ).then_inc(params_in, 16)
            for l in range(DEPTH):
                act.dma_start(rows[COL_CONV_W:COL_CONV_B, l, :], ml_conv_w[l].rearrange("w (k c) -> (w k) c", c=P)
                              ).then_inc(params_in, 16)
                act.dma_start(rows[COL_CONV_B:N_COLS, l, :], ml_conv_b[l].rearrange("(k c) -> k c", c=P)
                              ).then_inc(params_in, 16)
            act.dma_start(lg_raw, ret_decay_logit.rearrange("l d h -> (l d h)").partition_broadcast(P)
                          ).then_inc(params_in, 16)
            act.wait_ge(fixed_ok, 4)
            for l in range(DEPTH):
                act.dma_start(gate_w_all[:, l * KD * 16:(l + 1) * KD * 16].rearrange("p (k c) -> p k c", k=KD),
                              w_in[l, :, MGATE:MGATE + 16].rearrange("(k p) c -> p k c", p=P)).then_inc(params_in, 16)
                for d in range(2):
                    act.dma_start(gbias_all[32 * d:32 * d + 4, 2 * l:2 * l + 2], ml_gate_b[l, d].rearrange(
                        "i h -> h i"), allow_slow_non_contiguous=True).then_inc(params_in, 16)
            act.dma_start(cos[:], c_cos.rearrange("(n p) d -> p n d", p=P)).then_inc(consts_in, 16)
            act.dma_start(sin[:], c_sin.rearrange("(n p) d -> p n d", p=P)).then_inc(consts_in, 16)
            act.dma_start(window[:], c_window).then_inc(consts_in, 16)
            act.dma_start(spread[:], c_spread).then_inc(consts_in, 16)
            act.wait_ge(x_in_sem, 16)
            act.wait_ge(pre_abs, 1)
            act.activation(lg_e, lg_e, ACT.Exp, scale=-1.0).then_inc(pre_ln, 1)
            act.wait_ge(pre_ln, 1)
            act.activation(lg_l, lg_e, ACT.Ln, bias=1.0).then_inc(pre_ln, 1)
            act.wait_ge(pre_turn, 1)

            layer = [None]
            with act.Fori(0, DEPTH) as l:
                layer[0] = l
                squares(0)
                act.activation(gate_hi[:], gate_w_all[:, bass.ds(l * (KD * 16), KD * 16)].rearrange(
                    "p (k c) -> p k c", k=KD), ACT.Copy).then_inc(gate_hi_ok, 1)
                split(2)
                turned_banks("norm1")
                for v, (kind, g, i) in enumerate(UNITS):
                    split(v + 3)
                    slot = (v - 1) // 2 if v % 2 else None
                    if v == 3:
                        act.dma_start(region_b[:], na_bias[bass.ds(l, 1)].rearrange("a p c -> (a p) c")
                                      ).then_inc(bias_in, 16)
                        for s in range(2):
                            act.dma_start(gate_row[:, s, :], gate_b[bass.ds(l, 1), s * N512:(s + 1) * N512
                                          ].to_broadcast([P, N512])).then_inc(gate_row_in[s], 16)
                    if kind == "w" and i == UPG - 1 and g < G_PROJ:
                        group(g)
                    if kind == "up" and i == UPG - 1:
                        wait_unit(act, v)
                        if g >= 2:
                            act.wait_ge(up_v_ok, g - 1)
                        act.activation(up_th[:, g % 2, :, :], mix[:, 0:2, 0:256], ACT.Tanh,
                                       scale=0.5).then_inc(up_tanh, 1)
                    if slot in (18, 22):
                        j = (slot - 18) // 4
                        act.wait_ge(conv_ok, 4 * j + 4)
                        if j:
                            act.wait_ge(conv_silu, 1)
                        act.activation(wide_flat, conv_out[:, 4 * j:4 * j + 4, :].rearrange("p k t -> p (k t)"),
                                       ACT.Tanh, scale=0.5).then_inc(conv_th, 1)
                    if slot == 26:
                        act.wait_ge(rot_ok, 4)
                        act.dma_start(wide[:], c_dist).then_inc(dist_in, 16)
                    if slot == 32:
                        act.wait_ge(decay_arg, RET_HEADS)
                        act.activation(decay, decay, ACT.Exp).then_inc(decay_ok, 1)
                    for step in MIXER.get(v, []):
                        mixer(step)
                layer_end(act, "act")

            for n in range(NT):
                act.activation(small[:, n * D:(n + 1) * D], x[:, n, :], ACT.Square,
                               accum_out=ss[:, n:n + 1]).then_inc(fin_sq, 1)

        @block.gpsimd
        def _(pool):
            steps = Steps(pool, pool_step)

            def rsqrt(dst, src, scale):
                steps.link(pool.tensor_scalar(dst, src, scale, EPS, ALU.mult, ALU.add))
                return pool.tensor_tensor(dst, dst, half[:, 0:dst.shape[-1]], ALU.pow)

            pool.memset(half, -0.5).then_inc(fixed_ok, 1)
            pool.memset(gbias_all[:], 0.0).then_inc(fixed_ok, 1)
            pool.memset(mv[:, :, :, DV:DV + 1], 1.0).then_inc(fixed_ok, 1)
            pool.memset(stat[:, 0:4], 0.0).then_inc(fixed_ok, 1)
            pool.wait_ge(fixed_ok, 4)
            pool.wait_ge(consts_in, 16 * 5)

            with pool.Fori(0, DEPTH):
                for c in (0, 2 + T):
                    pool.memset(conv_in[:, :, c:c + 2], 0.0).then_inc(pad_ok, 1)
                pool.wait_ge(sumsq, 2)
                rsqrt(rstd, ss, 1.0 / D).then_inc(rstd_ok, 1)
                pool.wait_ge(bias_in, 16)
                for i in range(4):
                    part = region_b[:, i * 1536:(i + 1) * 1536].rearrange("p (j c) -> p j c", c=GRID_W)
                    pool.tensor_tensor(part, part, window[:, :].rearrange("p (a c) -> p a c", a=1).to_broadcast(
                        [P, 24, GRID_W]), ALU.add).then_inc(bias_ok, 1)
                for h in range(ML_HEADS):
                    wait_read(pool, "ml_rows", h)
                    for d, j in ((0, 0), (0, 1), (1, 0), (1, 1)):
                        block_ = ml_e[:, d, j, j * P:(j + 1) * P]
                        s = 1 if d == 0 else -1
                        pool.affine_select(block_, block_, pattern=[[s, P]], compare_op=ALU.is_ge, fill=0.0,
                                           base=0, channel_multiplier=-s).then_inc(ml_mask, 1)
                for i in range(2):
                    pool.wait_ge(bn_ok, i + 1)
                    rsqrt(rs8, mean_var[:, :, 1], 1.0).then_inc(rs_ok, 1)
                pool.wait_ge(sumsq, 4)
                rsqrt(rstd, ss, 1.0 / D).then_inc(rstd_ok, 1)
                layer_end(pool, "pool")

            pool.wait_ge(fin_sq, 2)
            pool.tensor_scalar(rstd, ss, 1.0 / D, EPS, ALU.mult, ALU.add).then_inc(fin_step, 1)
            pool.wait_ge(fin_step, 1)
            pool.tensor_tensor(rstd, rstd, half[:, 0:NT], ALU.pow).then_inc(fin_rs, 1)

        @block.vector
        def _(dve):
            steps = Steps(dve, dve_step)
            link = steps.link
            split_to, turned = [0], [0]

            def split(end):
                while split_to[0] < min(end, len(UNITS)):
                    v = split_to[0]
                    dve.wait_ge(hi_ok, v + 1)
                    dve.tensor_tensor(w_lo[:, v % SPLIT, :, :], raw[:, v % RAW, :, :],
                                      w_hi[:, v % SPLIT, :, :].bitcast(F32), ALU.subtract).then_inc(lo_ok, 1)
                    split_to[0] += 1

            def low_part(dst, src, scale, hi):
                turned[0] += 1
                dve.wait_ge(turn_hi, turned[0])
                return dve.scalar_tensor_tensor(dst, src, scale, hi.bitcast(F32), ALU.mult, ALU.subtract)

            def turned_banks(name):
                for b in range(4):
                    src = mix[:, b, :].rearrange("p (k t) -> p k t", k=2)
                    k = slice(2 * b, 2 * b + 2)
                    lo, hi = turned_lo[:, BUFFER[name], k, :], turned_hi[:, BUFFER[name], k, :]
                    if name in COLUMN:
                        c = COLUMN[name] + 2 * b
                        low_part(lo[:, 0, :], src[:, 0, :], cols[:, c:c + 1], hi[:, 0, :])
                        ins = dve.scalar_tensor_tensor(lo[:, 1, :], src[:, 1, :], cols[:, c + 1:c + 2],
                                                       hi[:, 1, :].bitcast(F32), ALU.mult, ALU.subtract)
                    else:
                        ins = low_part(lo, src, 0.5 if name == "merged" else 1.0, hi)
                    ins.then_inc(read[b], 1)

            def scale_x(count):
                dve.wait_ge(rstd_ok, count)
                for n in range(NT):
                    dve.tensor_scalar(tok[:, n, :], x[:, n, :], rstd[:, n:n + 1], None, ALU.mult).then_inc(xs_ok, 1)

            def gates():
                b = USES[("gate_rows",)][0]
                wait_filled(dve, "gate_rows")
                link(dve.tensor_scalar(g_f, mix[0:64, b, T:2 * T], gbias[:, 1:2], None, ALU.add))
                dve.tensor_scalar(g_i, mix[0:64, b, 0:T], gbias[:, 0:1], None, ALU.add).then_inc(read[b], 1)
                dve.scalar_tensor_tensor(g_e, g_f, -1.0, g_f, ALU.mult, ALU.max).then_inc(g_abs, 1)
                link(dve.memset(g_one, 1.0))
                dve.wait_ge(g_ln, 1)
                link(dve.scalar_tensor_tensor(g_f, g_f, 0.0, g_l, ALU.min, ALU.subtract))
                for r, way in ((slice(0, 32), 1), (slice(32, 64), -1)):
                    link(dve.tensor_tensor_scan(g_b[r, ::way], g_f[r, ::way], g_one[r, :], 0.0, ALU.add, ALU.mult))
                link(dve.tensor_tensor(g_a, g_i, g_b, ALU.subtract))
                for r, way in ((slice(0, 32), 1), (slice(32, 64), -1)):
                    link(dve.tensor_tensor_scan(g_m[r, ::way], g_a[r, ::way], g_a[r, ::way], LOWEST,
                                                ALU.max, ALU.max))
                link(dve.tensor_scalar(g_nm, g_m, -1.0, None, ALU.mult))
                dve.tensor_tensor(g_mt, g_b, g_m, ALU.add).then_inc(g_rows, 1)

            def na_scores(h):
                b = USES[("na_scores", h)][0]
                wait_filled(dve, "na_scores", h)
                if h == 0:
                    dve.wait_ge(bias_ok, 4)
                if h >= 2:
                    wait_filled(dve, "na_turn", h - 2)
                for n in range(NT):
                    first = 2 * (NT - 1 - n)
                    ins = dve.scalar_tensor_tensor(
                        na_p[:, h % 2, n, :], mix[:, b, n * T:(n + 1) * T], NA_SCALE,
                        bias[:, h, first:first + ROWS, :].rearrange("p j c -> p (j c)"), ALU.mult, ALU.add)
                ins.then_inc(read[b], 1)
                wait_read(dve, "na_scores", h)
                dve.tensor_reduce(na_max[:, h % 2, :], na_p[:, h % 2, :, :], AX_X, ALU.max,
                                  negate=True).then_inc(na_soft, 1)

            def na_probabilities(h):
                dve.wait_ge(na_exp, h + 1)
                s = na_sum[:, h % 2, :]
                link(dve.reciprocal(s, s))
                for n in range(NT):
                    ins = dve.tensor_scalar(na_p[:, h % 2, n, :], na_p[:, h % 2, n, :], na_sum[:, h % 2, n:n + 1],
                                            None, ALU.mult)
                ins.then_inc(na_prob, 1)

            def conv(i):
                def tap(w):
                    c = COL_CONV_W + 8 * w + i
                    return cols[:, c:c + 1]
                if i % 4 == 0:
                    wait_group_read(dve, G_ML + i // 4)
                link(dve.tensor_scalar(conv_out[:, i, :], conv_in[:, i, 0:T], tap(0),
                                       cols[:, COL_CONV_B + i:COL_CONV_B + i + 1], ALU.mult, ALU.add))
                for w in range(1, CONV_W):
                    ins = dve.scalar_tensor_tensor(conv_out[:, i, :], conv_in[:, i, w:w + T], tap(w),
                                                   conv_out[:, i, :], ALU.mult, ALU.add)
                    if w < CONV_W - 1:
                        link(ins)
                ins.then_inc(conv_ok, 1)

            def silu(i):
                dve.wait_ge(conv_th, i + 1)
                part = conv_out[:, 4 * i:4 * i + 4, :].rearrange("p k t -> p (k t)")
                dve.scalar_tensor_tensor(part, wide_flat, 1.0, part, ALU.add, ALU.mult).then_inc(conv_silu, 1)

            def rotary(g, n):
                i = g - G_ROT
                wait_group(dve, g)
                if (i, n) == (0, 0):
                    dve.wait_ge(conv_silu, 2)
                src = pair(g)[:, n, :].rearrange("p (h d) -> p h d", d=DK)
                by = [w[:, n, :].rearrange("p (a d) -> p a d", a=1).to_broadcast([P, RET_HEADS, DK])
                      for w in (cos, sin)]
                xc, xs = (wide[:, j, :].rearrange("p (h d) -> p h d", d=DK) for j in range(2))
                dve.tensor_tensor(xc, src, by[0], ALU.mult)
                ins = dve.tensor_tensor(xs, src, by[1], ALU.mult)
                if n == NT - 1:
                    ins.then_inc(acc_read[g % 2], 1)
                    wait_group_read(dve, g)
                else:
                    link(ins)
                dst = rot[:, n, i, :, :]
                dve.tensor_tensor(dst[:, :, 0:64], xc[:, :, 0:64], xs[:, :, 64:128], ALU.subtract)
                dve.tensor_tensor(dst[:, :, 64:128], xc[:, :, 64:128], xs[:, :, 0:64], ALU.add).then_inc(rot_ok, 1)
                dve.wait_ge(rot_ok, 2 * i + n + 1)

            def decay_exponents(h):
                if h == 0:
                    dve.wait_ge(dist_in, 16)
                link(dve.tensor_scalar(decay[:, h, :, :], dist[:, 1, :, :], lg[:, RET_HEADS + h:RET_HEADS + h + 1],
                                       None, ALU.mult))
                dve.scalar_tensor_tensor(decay[:, h, :, :], dist[:, 0, :, :], lg[:, h:h + 1], decay[:, h, :, :],
                                         ALU.mult, ALU.add).then_inc(decay_arg, 1)

            def ml_weights(h):
                b = USES[("ml_scores", h)][0]
                wait_filled(dve, "ml_scores", h)
                for d, j, t0, t1 in ((0, 0, 0, T), (0, 1, P, T), (1, 0, 0, P), (1, 1, 0, T)):
                    dve.wait_ge(ml_mask, 4 * h + 2 * d + j + 1)
                    ins = dve.scalar_tensor_tensor(ml_w[:, d, j, t0:t1], mix[:, b, j * T + t0:j * T + t1],
                                                   QK_SCALE / 4, ml_e[:, d, j, t0:t1], ALU.mult, ALU.mult)
                    if j == 1:
                        ins.then_inc(ml_wt, 1)
                dve.wait_ge(ml_wt, 2 * h + 2)
                dve.sem_inc(read[b], 1)

            def ml_out(h, d):
                for n in range(NT):
                    wait_filled(dve, "ml_values", h, d, n)
                r = 32 * d + h
                link(dve.tensor_tensor(rden[:, d, :], mix[:, 2:4, DV], emt[:, :, r], ALU.max))
                link(dve.scalar_tensor_tensor(den[:, d, :], mix[:, 2:4, DV], -1.0, rden[:, d, :],
                                              ALU.mult, ALU.max))
                link(dve.reciprocal(rden[:, d, :], den[:, d, :]))
                for n in range(NT):
                    b = USES[("ml_values", h, d, n)][0]
                    dst = h_ml[:, n, h * DV:(h + 1) * DV]
                    if d == 0:
                        ins = dve.tensor_scalar(dst, mix[:, b, 0:DV], rden[:, d, n:n + 1], None, ALU.mult)
                    else:
                        ins = dve.scalar_tensor_tensor(dst, mix[:, b, 0:DV], rden[:, d, n:n + 1], dst,
                                                       ALU.mult, ALU.add)
                    ins.then_inc(read[b], 1)

            def head_stats(y):
                for n in range(NT):
                    for h in range(4):
                        ins = dve.bn_stats(bn[:, 4 * n + h, :], y[:, n, h * DV:(h + 1) * DV])
                link(ins)
                for k in range(8):
                    ins = dve.bn_aggr(mean_var[:, k, :], bn[:, k, :])
                ins.then_inc(bn_ok, 1)

            def head_norm(i, y):
                dve.wait_ge(rs_ok, i + 1)
                for n in range(NT):
                    for h in range(4):
                        k, part = 4 * n + h, y[:, n, h * DV:(h + 1) * DV]
                        ins = dve.tensor_scalar(part, part, mean_var[:, k, 0:1], rs8[:, k:k + 1],
                                                ALU.subtract, ALU.mult)
                link(ins)

            def group(g):
                part = IN_GROUPS[g][0]
                c = slice((g % 2) * N512, (g % 2 + 1) * N512)
                if part == "rg":
                    dve.wait_ge(rg_th, g - G_RG + 1)
                    dve.scalar_tensor_tensor(rgs[:, :, c], wide[:], 1.0, pair(g), ALU.add,
                                             ALU.mult).then_inc(acc_read[g % 2], 1)
                elif part == "mo":
                    wait_group_read(dve, g)
                    dve.scalar_tensor_tensor(h_ml[:, :, c], wide[:], 1.0, h_ml[:, :, c], ALU.add,
                                             ALU.mult).then_inc(y_ok, 1)
                elif part == "mix":
                    j = g - G_MIX
                    wait_group(dve, g)
                    dve.wait_ge(gate_row_in[j % 2], 16 * (j // 2 + 1))
                    dve.tensor_tensor(mixg[:, :, j * N512:(j + 1) * N512], pair(g),
                                      gate_row[:, j % 2:j % 2 + 1, :].to_broadcast([P, NT, N512]),
                                      ALU.add).then_inc(acc_read[g % 2], 1)

            def project(g):
                i = (g - G_PROJ) // 2
                c0 = GATE_OF[BRANCHES[i]] * D + (g % 2) * N512
                total = tok[:, :, (g % 2) * N512:(g % 2 + 1) * N512]
                wait_group(dve, g)
                if g == G_PROJ:
                    dve.wait_ge(mix_th, 6)
                dve.scalar_tensor_tensor(total if i == 0 else wide[:], mixg[:, :, c0:c0 + N512], 1.0, pair(g),
                                         ALU.add, ALU.mult).then_inc(acc_read[g % 2], 1)
                wait_group_read(dve, g)
                if i:
                    dve.tensor_tensor(total, total, wide[:], ALU.add).then_inc(branch_sum, 1)
                    dve.wait_ge(branch_sum, g - G_PROJ + 1)
                else:
                    dve.sem_inc(branch_sum, 1)

            def mixer(step):
                what, i = step[0], step[1] if len(step) > 1 else None
                if what == "gate_rows":
                    gates()
                elif what == "na_scores":
                    na_scores(i)
                    na_probabilities(i)
                elif what == "na_values" and i % 2:
                    p = i // 2
                    b = USES[("na_values", p)][0]
                    low_part(turned_lo[:, 1, p, :], mix[:, b, 0:T], 1.0, turned_hi[:, 1, p, :]).then_inc(read[b], 1)
                elif what == "ml_scores":
                    ml_weights(i)
                elif what == "ml_values":
                    ml_out(i, step[2])
                elif what == "ret_scores":
                    b = USES[("ret_scores", i)][0]
                    wait_filled(dve, "ret_scores", i)
                    if i == 0:
                        dve.wait_ge(decay_ok, 1)
                    dve.scalar_tensor_tensor(ret_p[:, i % 2, :, :], mix[:, b, :].rearrange("p (j t) -> p j t", j=NT),
                                             QK_SCALE, decay[:, i, :, :], ALU.mult, ALU.mult).then_inc(ret_wt, 1)
                    dve.wait_ge(ret_wt, i + 1)
                    dve.sem_inc(read[b], 1)
                elif what == "turn" and i != "rot":
                    if i == "norm2":
                        scale_x(2)
                    turned_banks(i)
                elif what == "up_turn":
                    b = USES[("up_turn", i)][0]
                    low_part(up_lo[:, i % 2, :, :], mix[:, b, :].rearrange("p (k t) -> p k t", k=2), 1.0,
                             up_hi[:, i % 2, :, :]).then_inc(read[b], 1)

            dve.wait_ge(params_in, 16 * 17)
            dve.wait_ge(fixed_ok, 4)
            dve.scalar_tensor_tensor(lg_e, lg_raw, -1.0, lg_raw, ALU.mult, ALU.max).then_inc(pre_abs, 1)
            dve.wait_ge(pre_turn, 1)
            dve.tensor_copy(cols_all[:], mix[:, 0, 0:DEPTH * N_COLS]).then_inc(pre_cols, 1)
            dve.wait_ge(pre_cols, 1)
            for l in range(DEPTH):
                part = cols_all[:, l * N_COLS + COL_ML:l * N_COLS + COL_ML + 8]
                dve.tensor_scalar(part, part, 0.5, None, ALU.mult).then_inc(pre_cols, 1)
            dve.wait_ge(pre_ln, 2)
            dve.scalar_tensor_tensor(lg_all[:], lg_raw, 0.0, lg_l, ALU.min, ALU.subtract).then_inc(pre_lg, 1)
            dve.wait_ge(pre_lg, 1)
            dve.wait_ge(pre_cols, 3)
            dve.wait_ge(consts_in, 16 * 5)
            dve.wait_ge(x_in_sem, 16)

            with dve.Fori(0, DEPTH) as l:
                dve.tensor_copy(cols[:], cols_all[:, bass.ds(l * N_COLS, N_COLS)]).then_inc(cols_ok, 1)
                dve.tensor_copy(gbias[:], gbias_all[:, bass.ds(l * 2, 2)])
                link(dve.tensor_copy(lg, lg_all[:, bass.ds(l * 8, 8)]))
                scale_x(1)
                dve.wait_ge(gate_hi_ok, 1)
                dve.tensor_tensor(gate_lo[:], gate_w_all[:, bass.ds(l * (KD * 16), KD * 16)].rearrange(
                    "p (k c) -> p k c", k=KD), gate_hi[:].bitcast(F32), ALU.subtract).then_inc(gate_lo_ok, 1)
                split(2)
                turned_banks("norm1")
                for v, (kind, g, i) in enumerate(UNITS):
                    split(v + 3)
                    slot = (v - 1) // 2 if v % 2 else -1
                    if kind == "w" and i == UPG - 1:
                        if g < G_PROJ:
                            group(g)
                        elif g < G_OUT:
                            project(g)
                        else:
                            wait_group(dve, g)
                            part = x[:, :, (g % 2) * N512:(g % 2 + 1) * N512]
                            dve.tensor_tensor(part, part, pair(g), ALU.add).then_inc(acc_read[g % 2], 1)
                            wait_group_read(dve, g)
                            dve.sem_inc(x_ok, 1)
                    if kind == "up" and i == UPG - 1:
                        dve.wait_ge(up_tanh, g + 1)
                        if g >= 2:
                            wait_filled(dve, "up_turn", g - 2)
                        link(dve.scalar_tensor_tensor(up_s, up_th[:, g % 2, :, :], 1.0, mix[:, 0:2, 0:256],
                                                      ALU.add, ALU.mult))
                        dve.scalar_tensor_tensor(up_v[:, g % 2, :, :], up_s, 0.5, mix[:, 0:2, 256:512],
                                                 ALU.mult, ALU.mult).then_inc(up_v_ok, 1)
                        dve.wait_ge(up_v_ok, g + 1)
                        dve.sem_inc(read[0], 1)
                        dve.sem_inc(read[1], 1)
                    if 14 <= slot < 22:
                        conv(slot - 14)
                    if slot in (18, 22):
                        silu((slot - 18) // 4)
                    if 22 <= slot < 26:
                        rotary(G_ROT + (slot - 22) // 2, slot % 2)
                    if 28 <= slot < 32:
                        decay_exponents(slot - 28)
                    for step in MIXER.get(v, []):
                        mixer(step)
                    if slot == S_ML + 2 * ML_HEADS:
                        for n in range(NT):
                            wait_read(dve, "ml_values", ML_HEADS - 1, 1, n)
                        head_stats(h_ml)
                    if slot == S_ML + 2 * ML_HEADS + 1:
                        head_norm(0, h_ml)
                    if slot == S_RET + 1 + RET_HEADS:
                        for h in range(RET_HEADS):
                            wait_read(dve, "ret_values", h)
                        head_stats(o_ret)
                    if slot == S_RET + 2 + RET_HEADS:
                        head_norm(1, o_ret)
                    if v == last_of(G_RG + 1):
                        wait_group_read(dve, G_RG)
                        wait_group_read(dve, G_RG + 1)
                        dve.scalar_tensor_tensor(o_ret, o_ret, 0.5, rgs, ALU.mult, ALU.mult).then_inc(y_ok, 1)
                wait_unit(dve, len(UNITS) - 1)
                for n in range(NT):
                    part = x[:, n, :].rearrange("p (b c) -> p b c", b=2)
                    link(dve.tensor_tensor(part, part, acc[:, 2 * n:2 * n + 2, :], ALU.add))
                layer_end(dve, "dve")

            dve.wait_ge(fin_rs, 1)
            dve.wait_ge(final_g_in, 16)
            for n in range(NT):
                dve.scalar_tensor_tensor(tok[:, n, :], x[:, n, :], rstd[:, n:n + 1],
                                         raw[:, 0, :, :].rearrange("p k c -> p (k c)"), ALU.mult,
                                         ALU.mult).then_inc(fin_y, 1)


def shape_constants():
    ident = np.eye(P, dtype=np.float32)
    half = DK // 2
    inv_freq = np.float32(10000.0) ** (-np.arange(half, dtype=np.float32) / half)
    angle = np.arange(T, dtype=np.float32)[:, None] * inv_freq.astype(np.float32)[None, :]
    cos = np.tile(np.cos(angle), (1, 2)).astype(np.float32)
    sin = np.tile(np.sin(angle), (1, 2)).astype(np.float32)
    m = np.arange(T).reshape(NT, P).T[:, :, None]
    n = np.arange(T)[None, None, :]
    dist = np.stack([np.maximum(n - m, 0), np.maximum(m - n, 0)], 1).astype(np.float32).reshape(P, 2, NT * T)
    col = np.arange(GRID_W)
    first = np.clip(col - WIN_COLS // 2, 0, GRID_W - WIN_COLS)
    inside = (col[None, :] >= first[:, None]) & (col[None, :] < first[:, None] + WIN_COLS)
    window = np.tile(np.where(inside, 0.0, -1.0e30), (2, 1)).astype(np.float32)
    spread = np.zeros((16, 2, 64), np.float32)
    for d in range(2):
        for i in range(2):
            for h in range(ML_HEADS):
                spread[8 * d + 4 * i + h, i, 32 * d + h] = 1.0
    return {"c_ident": ident, "c_cos": cos, "c_sin": sin, "c_dist": dist, "c_window": window, "c_spread": spread}


def lay_out_bias(rpb):
    r, qc = np.arange(P) // GRID_W, np.arange(P) % GRID_W
    rows = np.arange(1, 7)[None, :] - r[:, None] - 3 + WIN_ROWS - 1
    rel = np.clip(np.arange(GRID_W)[None, :] - qc[:, None] + WIN_COLS - 1, 0, 2 * WIN_COLS - 2)
    picked = rpb[:, :, rows[:, :, None], rel[:, None, :]]
    return np.ascontiguousarray(picked.transpose(0, 2, 1, 3, 4)).reshape(rpb.shape[0], P, NA_HEADS * 6 * GRID_W)


_INS = ["x", "norm1_g", "w_in", "gate_b", "ret_decay_logit", "na_rpb", "ml_conv_w", "ml_conv_b", "ml_gate_b",
        "ml_norm_g", "w_ret_o", "w_na_o", "w_ml_o", "w_out", "norm2_g", "w_ffn_up", "w_ffn_down", "final_g"]


def kernel(**inputs):
    import concourse.bacc as bacc
    from concourse.bass_utils import run_bass_kernel_spmd

    nc = bacc.Bacc("TRN2", target_bir_lowering=False, num_devices=1)
    laid_out = {n: np.ascontiguousarray(inputs[n]) for n in _INS}
    laid_out["na_rpb"] = lay_out_bias(laid_out["na_rpb"])
    laid_out.update(shape_constants())
    arrays, args = {}, []
    for name, a in laid_out.items():
        arrays[f"in_{name}"] = a
        args.append(nc.dram_tensor(f"in_{name}", a.shape, mybir.dt.from_np(a.dtype), kind="ExternalInput").ap())
    args.append(nc.dram_tensor("out_0", (1, T, D), F32, kind="ExternalOutput").ap())
    trunk(nc, *args)
    r = run_bass_kernel_spmd(nc, [arrays], core_ids=[0])
    return r.results[0]["out_0"]
```

```python
from contextlib import ExitStack

import numpy as np
import concourse.bass as bass
from concourse import mybir

F32 = mybir.dt.float32
F32R = mybir.dt.float32r
ALU = mybir.AluOpType
ACT = mybir.ActivationFunctionType
AX_X = mybir.AxisListType.X

P = 128
T = 256
NT = T // P
D = 1024
KD = D // P
DEPTH = 2
GRID_W = 64
ROWS = T // GRID_W
WIN_ROWS, WIN_COLS = 8, 16
RET_HEADS, NA_HEADS, ML_HEADS = 4, 16, 4
DK, DV, NA_DH = 128, 256, 64
CONV_W = 5
FF = 2816
EPS = 1e-6
QK_SCALE = float(DK) ** -0.5
NA_SCALE = float(NA_DH) ** -0.5
LOWEST = -3.0e38

RQ, RK, RV, RG, NQ, NK, NV, MQ, MK, MV, MO, MGATE, MIX = np.cumsum(
    [0, 512, 512, 1024, 1024, 1024, 1024, 1024, 512, 512, 1024, 1024, 16]).tolist()

N512 = 512
UK = 2
UPG = KD // UK
RAW = 4
SPLIT = 3
WARM_UP = 3
HEAD = 2

IN_GROUPS = ([("nq", NQ), ("nq", NQ + N512), ("nk", NK), ("nk", NK + N512), ("nv", NV), ("nv", NV + N512),
              ("mq", MQ), ("mk", MK), ("mv", MV), ("mv", MV + N512), ("rq", RQ), ("rk", RK),
              ("rv", RV), ("rv", RV + N512)]
             + [("mix", MIX + j * N512) for j in range(6)]
             + [("mo", MO), ("mo", MO + N512), ("rg", RG), ("rg", RG + N512)])
FEATURE_MAJOR = ("nq", "nk", "mq", "mk")
G_ML, G_MV, G_ROT, G_RV, G_MIX, G_MO, G_RG = 6, 8, 10, 12, 14, 20, 22
G_PROJ = len(IN_GROUPS)
BRANCHES = ("na", "ml", "ret")
G_OUT = G_PROJ + 2 * len(BRANCHES)
GROUPS = G_OUT + 2
GATE_OF = {"ret": 0, "na": 1, "ml": 2}
N_UP = FF // 256

UNITS = [("w", g, i) for g in range(GROUPS) for i in range(UPG)]
for c in range(N_UP + 1):
    UNITS += [("up", c, i) for i in range(UPG) if c < N_UP] + [("down", c - 1, i) for i in range(2) if c]
AT = {unit: v for v, unit in enumerate(UNITS)}


def last_of(g):
    return AT[("w", g, UPG - 1)]


S_NA = 2 * 6
S_ML = S_NA + NA_HEADS + 3
S_RET = S_ML + 9

V_CONV = 4 * G_ML + 4
V_SILU = (V_CONV + 9, V_CONV + 16)
V_ROTARY = (V_CONV + 17, V_CONV + 18, V_CONV + 20, V_CONV + 22)


def mixer_schedule():
    after = {}

    def put(slot, *step):
        after.setdefault(2 * slot + 1, []).append(step)

    put(1, "gate")
    put(3, "gate_rows")
    after.setdefault(8, []).append(("gate_logs",))
    put(4, "gate_sums")
    put(5, "gate_maxima")
    put(7, "gate_turn")
    for h in range(NA_HEADS):
        put(S_NA + h, "na_scores", h)
        after.setdefault(2 * (S_NA + h) + 2, []).append(("na_exp", h))
    for h in range(NA_HEADS):
        put(S_NA + h + 1, "na_prob", h)
        if h % 2 == 0 and h:
            put(S_NA + h + 2, "na_values", h // 2 - 1)
        put(S_NA + h + 2, "na_turn", h)
    put(S_NA + NA_HEADS + 2, "na_values", NA_HEADS // 2 - 1)
    for h in range(ML_HEADS):
        put(S_ML + 2 * h, "ml_scores", h)
        put(S_ML + 2 * h + 1, "ml_values", h, 0)
        put(S_ML + 2 * h + 2, "ml_values", h, 1)
    put(S_RET, "turn", "rot", 0)
    put(S_RET, "turn", "rot", 1)
    for h in range(RET_HEADS):
        put(S_RET + 1 + h, "ret_scores", h)
        put(S_RET + 2 + h, "ret_values", h)
    for half in range(2):
        put(2 * G_PROJ + 1, "turn", "ml", half)
        put(2 * G_PROJ + 4, "turn", "ret", half)
    for name, g, v in (("merged", G_OUT, AT[("w", G_OUT, 0)]), ("norm2", GROUPS, AT[("up", 0, 0)])):
        after.setdefault(last_of(g - 2) + 2, []).append(("turn", name, 0))
        after.setdefault(v, []).append(("turn", name, 1))
    for c in range(N_UP):
        v = AT[("up", c + 1, 0)] if c < N_UP - 1 else AT[("down", c - 1, 0)]
        after.setdefault(v, []).append(("up_turn", c))
    for v in after:
        after[v].sort(key=lambda s: s[0] in ("na_scores", "ml_scores", "ret_scores"))
    return after


MIXER = mixer_schedule()


def up_banks(c):
    return (0, 1) if c % 2 == 0 else (2, 3)


def bank_uses():
    count, fills, uses = [0] * 4, [0] * 4, {}

    def use(bank, *name):
        count[bank] += 1
        fills[bank] += name[0] != "up"
        uses[name] = (bank, count[bank], fills[bank])

    def turn(name, half):
        for b in (2 * half, 2 * half + 1):
            use(b, "turn", name, b)

    turn("norm1", 0)
    turn("norm1", 1)
    for v, (kind, c, k) in enumerate(UNITS):
        if kind == "up" and k == 0:
            for n in range(NT):
                use(up_banks(c)[n], "up", c, n)
        for step in MIXER.get(v, []):
            what, i = step[0], step[1] if len(step) > 1 else None
            if what in ("gate", "gate_rows"):
                use(0, what)
            elif what == "gate_turn":
                use(1, "gate_turn")
            elif what == "na_scores":
                use(0, "na_scores", i)
            elif what == "na_turn":
                use(1, "na_turn", i)
            elif what == "na_values":
                use(2 + i % 2, "na_values", i)
            elif what == "ml_scores":
                use(0, "ml_scores", i)
                use(1, "ml_rows", i)
            elif what == "ml_values":
                use(2, "ml_values", i, step[2], 0)
                use(3, "ml_values", i, step[2], 1)
            elif what == "ret_scores":
                use(i % 2, "ret_scores", i)
            elif what == "ret_values":
                use(2 + i % 2, "ret_values", i)
            elif what == "turn":
                turn(i, step[2])
            elif what == "up_turn":
                use(up_banks(i)[0], "up_turn", i)
    return uses


USES = bank_uses()

N_COLS = 72
COL_NORM1, COL_NORM2, COL_ML, COL_CONV_W, COL_CONV_B = 0, 8, 16, 24, 64
COLUMN = {"norm1": COL_NORM1, "norm2": COL_NORM2, "ml": COL_ML}
BUFFER = {"norm1": 0, "na": 1, "ml": 0, "ret": 1, "merged": 0, "norm2": 1}


def trunk(nc, x_in, norm1_g, w_in, gate_b, ret_decay_logit, na_bias, ml_conv_w, ml_conv_b, ml_gate_b,
          ml_norm_g, w_ret_o, w_na_o, w_ml_o, w_out, norm2_g, w_ffn_up, w_ffn_down, final_g,
          c_ident, c_cos, c_sin, c_dist, c_window, c_spread, out):
    ctx = ExitStack()
    with ctx:
        def sb(name, shape, dtype=F32):
            return ctx.enter_context(nc.sbuf_tensor(name, shape, dtype))

        sems = []

        def sem(name):
            sems.append(ctx.enter_context(nc.semaphore(name)))
            return sems[-1]

        raw = sb("raw", [P, RAW, UK, N512])
        w_hi = sb("w_hi", [P, SPLIT, UK, N512], F32R)
        w_lo = sb("w_lo", [P, SPLIT, UK, N512], F32R)
        x = sb("x", [P, NT, D])
        turned_hi = sb("turned_hi", [P, 2, KD, T], F32R)
        turned_lo = sb("turned_lo", [P, 2, KD, T], F32R)
        up_hi = sb("up_hi", [P, 2, 2, T], F32R)
        up_lo = sb("up_lo", [P, 2, 2, T], F32R)
        gate_w = sb("gate_w", [P, KD, 32], F32R)
        tok = sb("tok", [P, NT, D])
        region_a = sb("region_a", [P, 6144])
        region_b = sb("region_b", [P, 6144])
        gate_row = sb("gate_row", [P, 2, N512])
        conv_in = sb("conv_in", [P, 8, T + CONV_W - 1])
        conv_out = sb("conv_out", [P, 8, T])
        mv = sb("mv", [P, NT, ML_HEADS, DV + 1])
        rot = sb("rot", [P, NT, 2, RET_HEADS, DK])
        rv = sb("rv", [P, NT, D])
        small = sb("small", [P, 2048])
        wide = sb("wide", [P, NT, N512])
        ident = sb("ident", [P, P])
        cos = sb("cos", [P, NT, DK])
        sin = sb("sin", [P, NT, DK])
        window = sb("window", [P, GRID_W])
        spread = sb("spread", [32, 2, 64])
        cols_all = sb("cols_all", [P, DEPTH * N_COLS])
        cols = sb("cols", [P, N_COLS])
        gate_w_all = sb("gate_w_all", [P, DEPTH * KD * 16])
        gbias_all = sb("gbias_all", [64, DEPTH * 2])
        gbias = sb("gbias", [64, 2])
        lg_logits = sb("lg_logits", [P, DEPTH * 8])
        acol = sb("acol", [P, NT, 64])
        emt = sb("emt", [P, NT, 64])
        stat = sb("stat", [P, 116])

        nqT = region_a[:, 0:2048].rearrange("p (k t) -> p k t", k=8)
        nkT = region_a[:, 2048:4096].rearrange("p (k t) -> p k t", k=8)
        nv = region_a[:, 4096:6144].rearrange("p (n c) -> p n c", n=NT)
        mixg = region_a[:, 0:6144].rearrange("p (n c) -> p n c", n=NT)
        bias = region_b[:, 0:6144].rearrange("p (h j c) -> p h j c", h=NA_HEADS, j=6)
        rgs = region_b[:, 0:2048].rearrange("p (n c) -> p n c", n=NT)
        decay = region_b[:, 2048:4096].rearrange("p (h j t) -> p h j t", h=RET_HEADS, j=NT)
        rot_T = region_b[:, 4096:6144].rearrange("p (k t) -> p k t", k=8)
        wide_flat = wide[:, :, :].rearrange("p s c -> p (s c)")
        dist = wide[:, :, :].rearrange("p s (j t) -> p s j t", j=NT)
        up_th = wide[:, :, :].rearrange("p s (n c) -> p s n c", n=NT)
        h_ml = conv_in[:, :, :].rearrange("p k c -> p (k c)")[:, 0:2048].rearrange("p (n c) -> p n c", n=NT)
        o_ret = rot[:, :, :, :, :].rearrange("p n a h d -> p n (a h d)")
        na_p = small[:, 0:1024].rearrange("p (s n c) -> p s n c", s=2, n=NT)
        na_pT = small[:, 1024:2048].rearrange("p (s n c) -> p s n c", s=2, n=NT)
        ml_e = small[:, 0:1024].rearrange("p (d j t) -> p d j t", d=2, j=NT)
        ml_w = small[:, 1024:2048].rearrange("p (d j t) -> p d j t", d=2, j=NT)
        ret_p = small[:, 0:1024].rearrange("p (s j t) -> p s j t", s=2, j=NT)
        up_s = small[:, 0:512].rearrange("p (n c) -> p n c", n=NT)
        up_v = small[:, 512:1536].rearrange("p (s n c) -> p s n c", s=2, n=NT)
        rows = small[0:N_COLS, 0:DEPTH * P].rearrange("p (l c) -> p l c", l=DEPTH)
        zeros = small[:, 1024:1024 + N512]
        gw = tok[0:64, :, :].rearrange("p n c -> p (n c)").rearrange("p (s t) -> p s t", s=8)
        g_i, g_f, g_e, g_l, g_b, g_a, g_m, g_mt = (gw[:, i, :] for i in range(8))
        g_nm, g_one, g_raw = g_e, g_m, g_mt[0:32, :]
        lg_e, lg_l = emt[:, 0, 0:8], emt[:, 0, 8:16]
        ss, rstd = stat[:, 0:2], stat[:, 2:4]
        na_max = stat[:, 4:8].rearrange("p (s n) -> p s n", s=2)
        na_sum = stat[:, 8:12].rearrange("p (s n) -> p s n", s=2)
        den = stat[:, 12:16].rearrange("p (d n) -> p d n", d=2)
        rden = stat[:, 16:20].rearrange("p (d n) -> p d n", d=2)
        bn = stat[:, 20:68].rearrange("p (g s) -> p g s", g=8)
        mean_var = stat[:, 68:84].rearrange("p (g s) -> p g s", g=8)
        rs8 = stat[:, 84:92]
        half = stat[:, 92:100]
        lg = stat[:, 100:108]
        half_rstd, half_rstd2 = stat[:, 108:110], stat[:, 110:112]
        ms = stat[:, 112:116].rearrange("p (n b) -> p n b", n=NT)

        acc = ctx.enter_context(nc.psum_tensor("acc", [P, 4, N512], F32))
        mix = ctx.enter_context(nc.psum_tensor("mix", [P, 4, N512], F32))

        acc_read = [sem("acc_read0"), sem("acc_read1")]
        bias_in, dist_in = sem("bias_in"), sem("dist_in")
        gate_row_in = [sem("gate_row_in0"), sem("gate_row_in1")]
        cols_ok = sem("cols_ok")
        gate_hi_ok, gate_lo_ok = sem("gate_hi_ok"), sem("gate_lo_ok")
        decay_arg, decay_ok = sem("decay_arg"), sem("decay_ok")
        g_abs, g_ln, g_rows = sem("g_abs"), sem("g_ln"), sem("g_rows")
        bias_ok = sem("bias_ok")
        na_soft = sem("na_soft")
        na_exp = sem("na_exp")
        na_prob = sem("na_prob")
        pad_ok = sem("pad_ok")
        conv_tap, conv_th, conv_silu = sem("conv_tap"), sem("conv_th"), sem("conv_silu")
        rot_ok = sem("rot_ok")
        ml_mask, ml_wt = sem("ml_mask"), sem("ml_wt")
        bn_ok = sem("bn_ok")
        rs_ok = sem("rs_ok")
        y_ok = sem("y_ok")
        ret_wt = sem("ret_wt")
        rg_th, mix_th = sem("rg_th"), sem("mix_th")
        branch_sum = sem("branch_sum")
        mixer_sems = list(sems)
        unit_in = [sem(f"unit_in{i}") for i in range(RAW)]
        hi_ok, lo_ok = sem("hi_ok"), sem("lo_ok")
        unit_used = sem("unit_used")
        filled = [sem(f"filled{b}") for b in range(4)]
        read = [sem(f"read{b}") for b in range(4)]
        turn_hi = sem("turn_hi")
        sumsq = sem("sumsq")
        half_rstd_ok = sem("half_rstd_ok")
        x_ok = sem("x_ok")
        up_tanh, up_v_ok = sem("up_tanh"), sem("up_v_ok")
        dve_step, act_step, pool_step = sem("dve_step"), sem("act_step"), sem("pool_step")
        arrived = sem("arrived")
        layer_sems = [s for s in sems[len(mixer_sems):] if s not in unit_in[:HEAD]]
        slot_reset = sem("slot_reset")
        bank_done = sem("bank_done")
        x_next = sem("x_next")
        next_sq = sem("next_sq")
        next_step = sem("next_step")
        next_rstd = sem("next_rstd")
        xs_ok = sem("xs_ok")
        x_landed = [sem("x_landed0"), sem("x_landed1")]
        rows_in, params_in, consts_in = sem("rows_in"), sem("params_in"), sem("consts_in")
        out_sem = sem("out_sem")
        fixed_ok = sem("fixed_ok")
        pre_turn, pre_cols = sem("pre_turn"), sem("pre_cols")
        fin_y = sem("fin_y")
        final_g_in = sem("final_g_in")
        go = {e: sem(f"go_{e}") for e in ("act", "dve", "pe", "pool")}

        block = ctx.enter_context(nc.Block())

        def last_in_slot(v):
            return max(w for w in range(len(UNITS)) if w % RAW == v % RAW)

        def wait_unit(eng, v):
            eng.wait_ge(unit_used, v + 1)

        def wait_group(eng, g):
            wait_unit(eng, last_of(g))

        def wait_group_read(eng, g):
            eng.wait_ge(acc_read[g % 2], g // 2 + 1)

        def wait_filled(eng, *name):
            bank, _, n = USES[name]
            eng.wait_ge(filled[bank], n)

        def wait_read(eng, *name):
            bank, n, _ = USES[name]
            eng.wait_ge(read[bank], n)

        def pair(g):
            return acc[:, 2 * (g % 2):2 * (g % 2) + 2, :]

        def pair_fm(g):
            return pair(g).rearrange("p b (k t) -> p (b k) t", t=T)

        def arrive(eng):
            eng.drain().then_inc(arrived, 1)

        def next_layer(eng, key):
            eng.wait_ge(go[key], 1)
            eng.sem_clear(go[key])

        class Steps:

            def __init__(self, eng, semaphore):
                self.eng, self.semaphore, self.n = eng, semaphore, 0

            def link(self, ins):
                self.n += 1
                ins.then_inc(self.semaphore, 1)
                self.eng.wait_ge(self.semaphore, self.n)

        @block.sync
        def _(sp):
            for n in range(NT):
                sp.dma_start(x[:, n, :], x_in[0, n * P:(n + 1) * P, :]).then_inc(x_landed[n], 16)
            sp.dma_start(ident[:], c_ident).then_inc(rows_in, 16)
            for i, src in enumerate((norm1_g, norm2_g, ml_norm_g)):
                sp.dma_start(rows[8 * i:8 * i + 8, :, :], src.rearrange("l (k c) -> k l c", c=P)).then_inc(rows_in, 16)
            sp.dma_start(rows[COL_CONV_W:COL_CONV_B, :, :], ml_conv_w.rearrange("l w (k c) -> (w k) l c", c=P)
                         ).then_inc(rows_in, 16)
            sp.dma_start(rows[COL_CONV_B:N_COLS, :, :], ml_conv_b.rearrange("l (k c) -> k l c", c=P)
                         ).then_inc(rows_in, 16)

            def source(l, v):
                kind, g, i = UNITS[v]
                one, rows_ = bass.ds(l, 1), slice(i * UK * P, (i + 1) * UK * P)
                if kind == "down":
                    r = (2 * g + i) * P
                    return [w_ffn_down[one, r:r + P, :].rearrange("a p (k c) -> p (a k) c", k=2)]
                if kind == "up":
                    return [w_ffn_up[one, rows_, s:s + 256].rearrange("a (k p) c -> p (a k) c", p=P)
                            for s in (g * 256, FF + g * 256)]
                if g < G_PROJ:
                    w, col = w_in, IN_GROUPS[g][1]
                elif g < G_OUT:
                    w = {"na": w_na_o, "ml": w_ml_o, "ret": w_ret_o}[BRANCHES[(g - G_PROJ) // 2]]
                    col = g % 2 * N512
                else:
                    w, col = w_out, g % 2 * N512
                return [w[one, rows_, col:col + N512].rearrange("a (k p) c -> p (a k) c", p=P)]

            def load(l, v):
                parts = source(l, v)
                width = N512 // len(parts)
                for i, src in enumerate(parts):
                    sp.dma_start(raw[:, v % RAW, :, width * i:width * (i + 1)], src).then_inc(unit_in[v % RAW], 16)

            for v in range(HEAD):
                load(0, v)
            sp.wait_ge(fixed_ok, 5)
            for l in range(DEPTH):
                sp.dma_start(gate_w_all[:, l * KD * 16:(l + 1) * KD * 16].rearrange("p (k c) -> p k c", k=KD),
                              w_in[l, :, MGATE:MGATE + 16].rearrange("(k p) c -> p k c", p=P)).then_inc(params_in, 16)
                for d in range(2):
                    sp.dma_start(gbias_all[32 * d:32 * d + 4, 2 * l:2 * l + 2], ml_gate_b[l, d].rearrange(
                        "i h -> h i"), allow_slow_non_contiguous=True).then_inc(params_in, 16)
            sp.dma_start(lg_logits[:], ret_decay_logit.rearrange("l d h -> (l d h)").partition_broadcast(P)
                          ).then_inc(params_in, 16)
            sp.dma_start(spread[:], c_spread).then_inc(consts_in, 16)
            sp.dma_start(window[:], c_window).then_inc(consts_in, 16)
            sp.dma_start(cos[:], c_cos.rearrange("(n p) d -> p n d", p=P)).then_inc(consts_in, 16)
            sp.dma_start(sin[:], c_sin.rearrange("(n p) d -> p n d", p=P)).then_inc(consts_in, 16)

            with sp.Fori(0, DEPTH) as l:
                for v in range(HEAD, len(UNITS)):
                    if v >= RAW:
                        sp.wait_ge(lo_ok, v - RAW + 1)
                    load(l, v)
                    if v == AT[("up", 5, 0)]:
                        for s in mixer_sems:
                            sp.sem_clear(s)
                for v in range(HEAD):
                    sp.wait_ge(slot_reset, v + 1)
                    sp.wait_ge(lo_ok, last_in_slot(v) + 1)
                    load((l + 1) % DEPTH, v)
                sp.sem_clear(slot_reset)
                sp.wait_ge(lo_ok, last_in_slot(RAW - 1) + 1)
                sp.dma_start(raw[:, RAW - 1, :, :], final_g.partition_broadcast(P).rearrange(
                    "p (k c) -> p k c", k=2)).then_inc(final_g_in, 16)
                sp.wait_ge(final_g_in, 16)
                sp.sem_clear(final_g_in)
                sp.wait_ge(arrived, 4)
                for s in layer_sems:
                    sp.sem_clear(s)
                for e in go.values():
                    sp.sem_inc(e, 1)
            for i in range(2 * NT):
                sp.wait_ge(fin_y, i + 1)
                n, c = i // 2, slice(i % 2 * N512, (i % 2 + 1) * N512)
                sp.dma_start(out[0, n * P:(n + 1) * P, c], tok[:, n, c]).then_inc(out_sem, 16)
            sp.wait_ge(out_sem, 16 * 2 * NT)
            for v in range(HEAD):
                sp.wait_ge(unit_in[v], 16)

        def unit_in_count(v):
            return sum(32 if UNITS[w][0] == "up" else 16 for w in range(v % RAW, v + 1, RAW))

        @block.tensor
        def _(pe):
            def begin(*name):
                bank, n, _ = USES[name]
                if n > 1:
                    pe.wait_ge(read[bank], n - 1)
                return bank

            def turn(name, src, half):
                for b in (2 * half, 2 * half + 1):
                    begin("turn", name, b)
                    if name == "merged":
                        pe.wait_ge(branch_sum, 5 + half)
                    if name == "norm2":
                        pe.wait_ge(x_ok, 1 + half)
                    if name == "ml":
                        pe.wait_ge(y_ok, 1 + half)
                    for j in range(2):
                        for n in range(NT):
                            c = (2 * b + j) * P
                            ins = pe.transpose(mix[:, b, j * T + n * P:j * T + (n + 1) * P],
                                               src[:, n, c:c + P], ident[:])
                    ins.then_inc(filled[b], 1)

            def products(dst, left_hi, left_lo, right_hi, right_lo, first, last, **kw):
                pe.matmul(dst, left_hi, right_hi, start=first, stop=False, **kw)
                pe.matmul(dst, left_hi, right_lo, start=False, stop=False, **kw)
                return pe.matmul(dst, left_lo, right_hi, start=False, stop=last, **kw)

            def mixer(step):
                what, h = step[0], step[1] if len(step) > 1 else None
                if what == "gate":
                    b = begin("gate")
                    pe.wait_ge(gate_lo_ok, 1)
                    for k in range(KD):
                        pe.matmul(mix[0:32, b, 0:T], gate_w[:, k, :], turned_hi[:, 0, k, :],
                                  start=(k == 0), stop=(k == KD - 1), skip_group_check=True)
                        ins = pe.matmul(mix[0:16, b, 0:T], gate_w[:, k, 0:16], turned_lo[:, 0, k, :],
                                        start=False, stop=(k == KD - 1), skip_group_check=True)
                    ins.then_inc(filled[b], 1)
                elif what == "gate_rows":
                    wait_read(pe, "gate")
                    pe.wait_ge(consts_in, 16 * 4)
                    b = begin("gate_rows")
                    for i in range(2):
                        ins = pe.matmul(mix[0:64, b, i * T:(i + 1) * T], spread[:, i, :], g_raw,
                                        start=True, stop=True)
                    ins.then_inc(filled[b], 1)
                elif what == "gate_turn":
                    b = begin("gate_turn")
                    pe.wait_ge(g_rows, 1)
                    for i, src in enumerate((g_a, g_mt)):
                        for n in range(NT):
                            o = (i * NT + n) * 64
                            ins = pe.transpose(mix[:, b, o:o + 64], src[:, n * P:(n + 1) * P],
                                               ident[0:64, 0:64])
                    ins.then_inc(filled[b], 1)
                elif what == "na_scores":
                    b = begin("na_scores", h)
                    if h == 0:
                        for g in range(4):
                            wait_group_read(pe, g)
                    r = NA_DH * (h % 2)
                    for n in range(NT):
                        ins = pe.matmul(mix[:, b, n * T:(n + 1) * T],
                                        nqT[r:r + NA_DH, h // 2, n * P:(n + 1) * P],
                                        nkT[r:r + NA_DH, h // 2, :], start=True, stop=True)
                    ins.then_inc(filled[b], 1)
                elif what == "na_turn":
                    b = begin("na_turn", h)
                    pe.wait_ge(na_prob, h + 1)
                    for k in range(NT):
                        for n in range(NT):
                            ins = pe.transpose(mix[:, b, k * T + n * P:k * T + (n + 1) * P],
                                               na_p[:, h % 2, n, k * P:(k + 1) * P], ident[:])
                    ins.then_inc(filled[b], 1)
                elif what == "na_values":
                    b = begin("na_values", h)
                    if h == 0:
                        wait_group_read(pe, 4)
                        wait_group_read(pe, 5)
                    wait_read(pe, "na_turn", 2 * h + 1)
                    for k in range(NT):
                        for r in range(2):
                            head = 2 * h + r
                            ins = pe.matmul(mix[r * NA_DH:(r + 1) * NA_DH, b, 0:T],
                                            nv[:, k, head * NA_DH:(head + 1) * NA_DH],
                                            na_pT[:, r, k, :], start=(k == 0), stop=(k == NT - 1))
                    ins.then_inc(filled[b], 1)
                elif what == "ml_scores":
                    b = begin("ml_scores", h)
                    if h == 0:
                        pe.wait_ge(conv_silu, 2)
                    for j in range(NT):
                        ins = pe.matmul(mix[:, b, j * T:(j + 1) * T],
                                        conv_out[:, ML_HEADS + h, j * P:(j + 1) * P],
                                        conv_out[:, h, :], start=True, stop=True)
                    ins.then_inc(filled[b], 1)
                    b = begin("ml_rows", h)
                    for d in range(2):
                        r = 32 * d + h
                        ins = pe.matmul(mix[:, b, d * T:(d + 1) * T],
                                        ident[0:64, r:r + 1].to_broadcast([64, P]), g_nm,
                                        start=True, stop=True)
                    ins.then_inc(filled[b], 1)
                elif what == "ml_values":
                    d = step[2]
                    if (h, d) == (0, 0):
                        wait_group_read(pe, G_MV)
                        wait_group_read(pe, G_MV + 1)
                    pe.wait_ge(ml_wt, 2 * h + d + 1)
                    for n in range(NT):
                        b = begin("ml_values", h, d, n)
                        js = range(0, n + 1) if d == 0 else range(n, NT)
                        for j in js:
                            ins = pe.matmul(mix[:, b, 0:DV + 1], ml_w[:, d, j, n * P:(n + 1) * P],
                                            mv[:, j, h, :], start=(j == js[0]), stop=(j == js[-1]))
                        ins.then_inc(filled[b], 1)
                elif what == "ret_scores":
                    b = begin("ret_scores", h)
                    if h == 0:
                        for i in range(4):
                            wait_read(pe, "turn", "rot", i)
                    for j in range(NT):
                        ins = pe.matmul(mix[:, b, j * T:(j + 1) * T],
                                        rot_T[:, RET_HEADS + h, j * P:(j + 1) * P],
                                        rot_T[:, h, :], start=True, stop=True)
                    ins.then_inc(filled[b], 1)
                elif what == "ret_values":
                    b = begin("ret_values", h)
                    if h == 0:
                        wait_group_read(pe, G_RV)
                        wait_group_read(pe, G_RV + 1)
                    pe.wait_ge(ret_wt, h + 1)
                    for n in range(NT):
                        for j in range(NT):
                            ins = pe.matmul(mix[:, b, n * T:(n + 1) * T], ret_p[:, h % 2, j, n * P:(n + 1) * P],
                                            rv[:, j, h * DV:(h + 1) * DV], start=(j == 0), stop=(j == NT - 1))
                    ins.then_inc(filled[b], 1)
                elif what == "turn":
                    if h == "rot":
                        pe.wait_ge(rot_ok, 4)
                    elif h == "ret":
                        pe.wait_ge(y_ok, 4)
                    turn(h, {"rot": o_ret, "ml": h_ml, "ret": o_ret, "merged": tok, "norm2": x}[h], step[2])
                elif what == "up_turn":
                    b = begin("up_turn", h)
                    pe.wait_ge(up_v_ok, h + 1)
                    for j in range(2):
                        for n in range(NT):
                            ins = pe.transpose(mix[:, b, j * T + n * P:j * T + (n + 1) * P],
                                               up_v[:, h % 2, n, j * P:(j + 1) * P], ident[:])
                    ins.then_inc(filled[b], 1)

            def left_of(g):
                if g < G_PROJ:
                    return "norm1"
                return BRANCHES[(g - G_PROJ) // 2] if g < G_OUT else "merged"

            pe.wait_ge(fixed_ok, 5)
            for _ in range(WARM_UP):
                pe.matmul(mix[:, 3, :], zeros[:, 0:P], zeros, start=True, stop=True)
            pe.wait_ge(rows_in, 16 * 6)
            for l in range(DEPTH):
                ins = pe.transpose(mix[:, 0, l * N_COLS:(l + 1) * N_COLS], rows[:, l, :],
                                   ident[0:N_COLS, 0:N_COLS])
            ins.then_inc(pre_turn, 1)
            pe.wait_ge(pre_cols, 1)

            with pe.Fori(0, DEPTH):
                for b in range(4):
                    begin("turn", "norm1", b)
                for n in range(NT):
                    pe.wait_ge(xs_ok, n + 1)
                    for b in range(4):
                        for j in range(2):
                            c = (2 * b + j) * P
                            ins = pe.transpose(mix[:, b, j * T + n * P:j * T + (n + 1) * P],
                                               tok[:, n, c:c + P], ident[:])
                        if n == NT - 1:
                            ins.then_inc(filled[b], 1)
                pe.sem_clear(xs_ok)
                for v, (kind, g, i) in enumerate(UNITS):
                    slot = v % SPLIT
                    pe.wait_ge(lo_ok, v + 1)
                    hi, lo = w_hi[:, slot, :, :], w_lo[:, slot, :, :]
                    if kind == "w":
                        name = left_of(g)
                        buf = BUFFER[name]
                        if i == 0 and g >= 2:
                            wait_group_read(pe, g - 2)
                        if name == "na":
                            for p in range(UK * i, UK * i + UK):
                                wait_read(pe, "na_values", p)
                        else:
                            wait_read(pe, "turn", name, i)
                        for k in range(UK):
                            kk = UK * i + k
                            if g >= G_PROJ or IN_GROUPS[g][0] not in FEATURE_MAJOR:
                                for n in range(NT):
                                    c = slice(n * P, (n + 1) * P)
                                    ins = products(pair(g)[:, n, :], turned_hi[:, buf, kk, c],
                                                   turned_lo[:, buf, kk, c], hi[:, k, :], lo[:, k, :],
                                                   kk == 0, kk == KD - 1)
                            else:
                                for j in range(4):
                                    c = slice(j * P, (j + 1) * P)
                                    ins = products(pair_fm(g)[:, j, :], hi[:, k, c], lo[:, k, c],
                                                   turned_hi[:, buf, kk, :], turned_lo[:, buf, kk, :],
                                                   kk == 0 and j % 2 == 0, kk == KD - 1,
                                                   skip_group_check=True)
                    elif kind == "up":
                        if i == 0:
                            for n in range(NT):
                                begin("up", g, n)
                        wait_read(pe, "turn", "norm2", i)
                        for k in range(UK):
                            kk = UK * i + k
                            for n in range(NT):
                                c = slice(n * P, (n + 1) * P)
                                ins = products(mix[:, up_banks(g)[n], :], turned_hi[:, BUFFER["norm2"], kk, c],
                                               turned_lo[:, BUFFER["norm2"], kk, c], hi[:, k, :], lo[:, k, :],
                                               kk == 0, kk == KD - 1)
                    else:
                        if (g, i) == (0, 0):
                            wait_group_read(pe, GROUPS - 2)
                            wait_group_read(pe, GROUPS - 1)
                        wait_read(pe, "up_turn", g)
                        for n in range(NT):
                            c = slice(n * P, (n + 1) * P)
                            for j in range(2):
                                ins = products(acc[:, 2 * n + j, :], up_hi[:, g % 2, i, c], up_lo[:, g % 2, i, c],
                                               hi[:, j, :], lo[:, j, :], (g, i) == (0, 0),
                                               (g, i) == (N_UP - 1, 1))
                                if v == len(UNITS) - 1:
                                    ins.then_inc(bank_done, 1)
                    if v < len(UNITS) - 1:
                        ins.then_inc(unit_used, 1)
                    for step in MIXER.get(v, []):
                        mixer(step)
                arrive(pe)
                next_layer(pe, "pe")

        @block.scalar
        def _(act):
            steps = Steps(act, act_step)
            split_to = [0]

            def split(end):
                while split_to[0] < min(end, len(UNITS)):
                    v = split_to[0]
                    act.wait_ge(unit_in[v % RAW], unit_in_count(v))
                    if v >= SPLIT:
                        wait_unit(act, v - SPLIT)
                    act.activation(w_hi[:, v % SPLIT, :, :], raw[:, v % RAW, :, :], ACT.Copy).then_inc(hi_ok, 1)
                    if v in [last_in_slot(w) for w in range(HEAD)]:
                        act.sem_clear(unit_in[v % RAW])
                        act.sem_inc(slot_reset, 1)
                    split_to[0] += 1

            def turned_banks(name, half):
                for b in (2 * half, 2 * half + 1):
                    wait_filled(act, "turn", name, b)
                    src = mix[:, b, :].rearrange("p (k t) -> p k t", k=2)
                    if name == "rot":
                        act.activation(rot_T[:, 2 * b:2 * b + 2, :], src, ACT.Copy).then_inc(read[b], 1)
                        continue
                    dst = turned_hi[:, BUFFER[name], 2 * b:2 * b + 2, :]
                    if name in COLUMN:
                        if b == 0 and name == "norm1":
                            act.wait_ge(cols_ok, 1)
                        for j in range(2):
                            c = COLUMN[name] + 2 * b + j
                            ins = act.activation(dst[:, j, :], src[:, j, :], ACT.Copy, scale=cols[:, c:c + 1])
                    else:
                        ins = act.activation(dst, src, ACT.Copy, scale=0.5 if name == "merged" else 1.0)
                    ins.then_inc(turn_hi, 1)

            def squares():
                act.wait_ge(x_ok, 2)
                for n in range(NT):
                    junk = wide_flat if n == 0 else rv[:, 0, :]
                    act.activation(junk, x[:, n, :], ACT.Square, accum_out=ss[:, n:n + 1]).then_inc(sumsq, 1)

            def next_squares(first):
                for n in range(NT):
                    for b in range(2):
                        c = slice(b * N512, (b + 1) * N512)
                        if first:
                            act.wait_ge(x_landed[n], 16)
                        else:
                            act.wait_ge(x_next, 2 * n + b + 1)
                        junk = wide[:, b, :] if n == 0 else rv[:, 0, c]
                        act.activation(junk, x[:, n, c], ACT.Square, scale=D ** -0.5,
                                       accum_out=ms[:, n, b:b + 1]).then_inc(next_sq, 1)
                if not first:
                    act.sem_clear(x_next)

            def group(g, l):
                part = IN_GROUPS[g][0]
                half_of = slice((g % 2) * N512, (g % 2 + 1) * N512)
                if part in ("nq", "nk"):
                    dst = (nqT if part == "nq" else nkT)[:, 4 * (g % 2):4 * (g % 2) + 4, :]
                    wait_group(act, g)
                    act.activation(dst, pair_fm(g), ACT.Copy).then_inc(acc_read[g % 2], 1)
                elif part in ("mq", "mk"):
                    k = 0 if part == "mq" else 4
                    wait_group(act, g)
                    act.wait_ge(pad_ok, 2)
                    act.activation(conv_in[:, k:k + 4, 2:2 + T], pair_fm(g), ACT.Copy).then_inc(acc_read[g % 2], 1)
                elif part in ("nv", "rv"):
                    wait_group(act, g)
                    act.activation((nv if part == "nv" else rv)[:, :, half_of], pair(g),
                                   ACT.Copy).then_inc(acc_read[g % 2], 1)
                elif part == "mv":
                    wait_group(act, g)
                    for n in range(NT):
                        ins = act.activation(mv[:, n, 2 * (g % 2):2 * (g % 2) + 2, 0:DV],
                                             pair(g)[:, n, :].rearrange("p (h d) -> p h d", h=2), ACT.Copy)
                    ins.then_inc(acc_read[g % 2], 1)
                elif part == "mo":
                    wait_group(act, g)
                    if g == G_MO:
                        act.wait_ge(decay_arg, RET_HEADS)
                    else:
                        act.wait_ge(y_ok, 1)
                    act.activation(wide[:], pair(g), ACT.Tanh, scale=0.5).then_inc(acc_read[g % 2], 1)
                elif part == "rg":
                    wait_group(act, g)
                    if g == G_RG:
                        act.wait_ge(y_ok, 2)
                    else:
                        wait_group_read(act, g - 1)
                    act.activation(wide[:], pair(g), ACT.Tanh, scale=0.5).then_inc(rg_th, 1)
                elif part == "mix":
                    j = g - G_MIX
                    wait_group_read(act, g)
                    if j + 2 < 6:
                        act.dma_start(gate_row[:, j % 2, :], gate_b[bass.ds(l, 1), (j + 2) * N512:
                                      (j + 3) * N512].to_broadcast([P, N512])).then_inc(gate_row_in[j % 2], 16)
                    part = mixg[:, :, j * N512:(j + 1) * N512]
                    act.activation(part, part, ACT.Tanh, scale=0.5).then_inc(mix_th, 1)

            def mixer(step):
                what, h = step[0], step[1] if len(step) > 1 else None
                if what == "gate":
                    wait_filled(act, "gate")
                    b = USES[("gate",)][0]
                    act.activation(g_raw, mix[0:32, b, 0:T], ACT.Copy).then_inc(read[b], 1)
                elif what == "gate_logs":
                    act.wait_ge(g_abs, 2)
                    act.activation(g_e, g_e, ACT.Exp, scale=-1.0)
                    steps.link(act.activation(lg_e, lg_e, ACT.Exp, scale=-1.0))
                    act.activation(lg_l, lg_e, ACT.Ln, bias=1.0)
                    act.activation(g_l, g_e, ACT.Ln, bias=1.0).then_inc(g_ln, 1)
                elif what == "gate_turn":
                    wait_filled(act, "gate_turn")
                    b = USES[("gate_turn",)][0]
                    act.activation(acol[:], mix[:, b, 0:2 * 64].rearrange("p (n r) -> p n r", n=NT), ACT.Copy)
                    act.activation(emt[:], mix[:, b, 2 * 64:4 * 64].rearrange("p (n r) -> p n r", n=NT),
                                   ACT.Exp, scale=-1.0).then_inc(read[b], 1)
                elif what == "na_exp":
                    act.wait_ge(na_soft, h + 1)
                    for n in range(NT):
                        ins = act.activation(na_p[:, h % 2, n, :], na_p[:, h % 2, n, :], ACT.Exp,
                                             bias=na_max[:, h % 2, n:n + 1], accum_out=na_sum[:, h % 2, n:n + 1])
                    ins.then_inc(na_exp, 1)
                elif what == "na_turn":
                    wait_filled(act, "na_turn", h)
                    b = USES[("na_turn", h)][0]
                    act.activation(na_pT[:, h % 2, :, :], mix[:, b, :].rearrange("p (k c) -> p k c", k=NT),
                                   ACT.Copy).then_inc(read[b], 1)
                elif what == "na_values":
                    wait_filled(act, "na_values", h)
                    act.activation(turned_hi[:, 1, h, :], mix[:, USES[("na_values", h)][0], 0:T],
                                   ACT.Copy).then_inc(turn_hi, 1)
                elif what == "ml_scores":
                    wait_filled(act, "ml_rows", h)
                    b = USES[("ml_rows", h)][0]
                    if h == 0:
                        wait_read(act, "gate_turn")
                    else:
                        act.wait_ge(ml_wt, 2 * h)
                    for d, j, t0, t1 in ((0, 0, 0, T), (0, 1, P, T), (1, 0, 0, P), (1, 1, 0, T)):
                        r = 32 * d + h
                        ins = act.activation(ml_e[:, d, j, t0:t1], mix[:, b, d * T + t0:d * T + t1], ACT.Exp,
                                             bias=acol[:, j, r:r + 1])
                    ins.then_inc(read[b], 1)
                elif what == "ret_values":
                    wait_filled(act, "ret_values", h)
                    b = USES[("ret_values", h)][0]
                    act.activation(o_ret[:, :, h * DV:(h + 1) * DV], mix[:, b, :].rearrange(
                        "p (n c) -> p n c", n=NT), ACT.Copy).then_inc(read[b], 1)
                elif what == "turn":
                    turned_banks(h, step[2])
                    if (h, step[2]) == ("norm2", 1):
                        squares()
                elif what == "up_turn":
                    wait_filled(act, "up_turn", h)
                    b = USES[("up_turn", h)][0]
                    if h >= 2:
                        wait_unit(act, AT[("down", h - 2, 1)])
                    act.activation(up_hi[:, h % 2, :, :], mix[:, b, :].rearrange("p (k t) -> p k t", k=2),
                                   ACT.Copy).then_inc(turn_hi, 1)

            act.wait_ge(fixed_ok, 5)
            act.activation(rstd[:, 0:1], ss[:, 0:1], ACT.Square)
            next_squares(True)
            with act.Fori(0, DEPTH) as l:
                split(2)
                turned_banks("norm1", 0)
                turned_banks("norm1", 1)
                act.wait_ge(params_in, 16 * 7)
                act.activation(gate_w[:, :, 0:16], gate_w_all[:, bass.ds(l * (KD * 16), KD * 16)].rearrange(
                    "p (k c) -> p k c", k=KD), ACT.Copy).then_inc(gate_hi_ok, 1)
                for v, (kind, g, i) in enumerate(UNITS):
                    split(v + 3)
                    slot = (v - 1) // 2 if v % 2 else None
                    if v == 3:
                        act.dma_start(region_b[:], na_bias[bass.ds(l, 1)].rearrange("a p c -> (a p) c")
                                      ).then_inc(bias_in, 16)
                        for s in range(2):
                            act.dma_start(gate_row[:, s, :], gate_b[bass.ds(l, 1), s * N512:(s + 1) * N512
                                          ].to_broadcast([P, N512])).then_inc(gate_row_in[s], 16)
                    if kind == "w" and i == UPG - 1 and g < G_PROJ:
                        group(g, l)
                    if kind == "up" and i == UPG - 1:
                        wait_unit(act, v)
                        if g >= 2:
                            act.wait_ge(up_v_ok, g - 1)
                        if g == 0:
                            act.wait_ge(half_rstd_ok, 2)
                        for n in range(NT):
                            ins = act.activation(up_th[:, g % 2, n, :], mix[:, up_banks(g)[n], 0:256], ACT.Tanh,
                                                 scale=half_rstd[:, n:n + 1])
                        ins.then_inc(up_tanh, 1)
                    if v + 1 in V_SILU:
                        j = V_SILU.index(v + 1)
                        act.wait_ge(conv_tap, 4 * CONV_W * (j + 1))
                        if j:
                            act.wait_ge(conv_silu, 1)
                        act.activation(wide_flat, conv_out[:, 4 * j:4 * j + 4, :].rearrange("p k t -> p (k t)"),
                                       ACT.Tanh, scale=0.5).then_inc(conv_th, 1)
                    if slot == 26:
                        act.wait_ge(rot_ok, 4)
                        act.dma_start(wide[:], c_dist).then_inc(dist_in, 16)
                    if slot == 32:
                        act.wait_ge(decay_arg, RET_HEADS)
                        act.activation(decay, decay, ACT.Exp).then_inc(decay_ok, 1)
                    for step in MIXER.get(v, []):
                        mixer(step)
                arrive(act)
                next_squares(False)
                next_layer(act, "act")

        @block.gpsimd
        def _(pool):
            steps = Steps(pool, pool_step)

            def rsqrt(dst, src, scale):
                steps.link(pool.tensor_scalar(dst, src, scale, EPS, ALU.mult, ALU.add))
                return pool.tensor_tensor(dst, dst, half[:, 0:dst.shape[-1]], ALU.pow)

            def next_rsqrt():
                for n in range(NT):
                    pool.wait_ge(next_sq, 2 * n + 2)
                    pool.tensor_scalar(rstd[:, n:n + 1], ms[:, n, 0:1], ms[:, n, 1:2], EPS,
                                       ALU.add, ALU.add).then_inc(next_step, 1)
                    pool.wait_ge(next_step, n + 1)
                    pool.tensor_tensor(rstd[:, n:n + 1], rstd[:, n:n + 1], half[:, 0:1], ALU.pow).then_inc(next_rstd, 1)
                pool.sem_clear(next_sq)
                pool.sem_clear(next_step)

            pool.memset(gbias_all[:], 0.0).then_inc(fixed_ok, 1)
            pool.memset(mv[:, :, :, DV:DV + 1], 1.0).then_inc(fixed_ok, 1)
            pool.memset(ss, 0.0)
            pool.memset(stat[:, 112:116], 0.0).then_inc(fixed_ok, 1)
            pool.memset(half, -0.5).then_inc(fixed_ok, 1)
            pool.memset(zeros, 0.0).then_inc(fixed_ok, 1)
            pool.wait_ge(fixed_ok, 5)
            next_rsqrt()

            with pool.Fori(0, DEPTH):
                for c in (0, 2 + T):
                    pool.memset(conv_in[:, :, c:c + 2], 0.0).then_inc(pad_ok, 1)
                pool.wait_ge(consts_in, 16 * 4)
                pool.wait_ge(bias_in, 16)
                for i in range(4):
                    part = region_b[:, i * 1536:(i + 1) * 1536].rearrange("p (j c) -> p j c", c=GRID_W)
                    pool.tensor_tensor(part, part, window[:, :].rearrange("p (a c) -> p a c", a=1).to_broadcast(
                        [P, 24, GRID_W]), ALU.add).then_inc(bias_ok, 1)
                for h in range(ML_HEADS):
                    wait_read(pool, "ml_rows", h)
                    for d, j in ((0, 0), (0, 1), (1, 0), (1, 1)):
                        block_ = ml_e[:, d, j, j * P:(j + 1) * P]
                        s = 1 if d == 0 else -1
                        pool.affine_select(block_, block_, pattern=[[s, P]], compare_op=ALU.is_ge, fill=0.0,
                                           base=0, channel_multiplier=-s).then_inc(ml_mask, 1)
                for i in range(2):
                    pool.wait_ge(bn_ok, i + 1)
                    rsqrt(rs8, mean_var[:, :, 1], 1.0).then_inc(rs_ok, 1)
                pool.wait_ge(sumsq, 2)
                steps.link(rsqrt(rstd, ss, 1.0 / D))
                pool.tensor_scalar(half_rstd, rstd, 0.5, None, ALU.mult).then_inc(half_rstd_ok, 1)
                pool.wait_ge(half_rstd_ok, 1)
                pool.tensor_tensor(half_rstd2, half_rstd, rstd, ALU.mult).then_inc(half_rstd_ok, 1)
                arrive(pool)
                next_rsqrt()
                next_layer(pool, "pool")

        @block.vector
        def _(dve):
            steps = Steps(dve, dve_step)
            link = steps.link
            split_to, turned = [0], [0]

            def split(end):
                while split_to[0] < min(end, len(UNITS)):
                    v = split_to[0]
                    dve.wait_ge(hi_ok, v + 1)
                    dve.tensor_tensor(w_lo[:, v % SPLIT, :, :], raw[:, v % RAW, :, :],
                                      w_hi[:, v % SPLIT, :, :].bitcast(F32), ALU.subtract).then_inc(lo_ok, 1)
                    split_to[0] += 1

            def low_part(dst, src, scale, hi):
                turned[0] += 1
                dve.wait_ge(turn_hi, turned[0])
                return dve.scalar_tensor_tensor(dst, src, scale, hi.bitcast(F32), ALU.mult, ALU.subtract)

            def turned_banks(name, half):
                for b in (2 * half, 2 * half + 1):
                    src = mix[:, b, :].rearrange("p (k t) -> p k t", k=2)
                    k = slice(2 * b, 2 * b + 2)
                    lo, hi = turned_lo[:, BUFFER[name], k, :], turned_hi[:, BUFFER[name], k, :]
                    if name in COLUMN:
                        c = COLUMN[name] + 2 * b
                        low_part(lo[:, 0, :], src[:, 0, :], cols[:, c:c + 1], hi[:, 0, :])
                        ins = dve.scalar_tensor_tensor(lo[:, 1, :], src[:, 1, :], cols[:, c + 1:c + 2],
                                                       hi[:, 1, :].bitcast(F32), ALU.mult, ALU.subtract)
                    else:
                        ins = low_part(lo, src, 0.5 if name == "merged" else 1.0, hi)
                    ins.then_inc(read[b], 1)

            def normalise():
                for n in range(NT):
                    dve.wait_ge(next_rstd, n + 1)
                    dve.tensor_scalar(tok[:, n, :], x[:, n, :], rstd[:, n:n + 1], None, ALU.mult).then_inc(xs_ok, 1)
                dve.sem_clear(next_rstd)

            def gate_rows():
                b = USES[("gate_rows",)][0]
                wait_filled(dve, "gate_rows")
                link(dve.tensor_scalar(g_f, mix[0:64, b, T:2 * T], gbias[:, 1:2], None, ALU.add))
                dve.tensor_scalar(g_i, mix[0:64, b, 0:T], gbias[:, 0:1], None, ALU.add).then_inc(read[b], 1)
                dve.scalar_tensor_tensor(g_e, g_f, -1.0, g_f, ALU.mult, ALU.max).then_inc(g_abs, 1)
                dve.scalar_tensor_tensor(lg_e, lg, -1.0, lg, ALU.mult, ALU.max).then_inc(g_abs, 1)
                dve.memset(g_one, 1.0)

            def gate_sums():
                dve.wait_ge(g_ln, 1)
                link(dve.scalar_tensor_tensor(g_f, g_f, 0.0, g_l, ALU.min, ALU.subtract))
                dve.scalar_tensor_tensor(lg, lg, 0.0, lg_l, ALU.min, ALU.subtract)
                for r, way in ((slice(0, 32), 1), (slice(32, 64), -1)):
                    link(dve.tensor_tensor_scan(g_b[r, ::way], g_f[r, ::way], g_one[r, :], 0.0, ALU.add, ALU.mult))

            def gate_maxima():
                link(dve.tensor_tensor(g_a, g_i, g_b, ALU.subtract))
                for r, way in ((slice(0, 32), 1), (slice(32, 64), -1)):
                    link(dve.tensor_tensor_scan(g_m[r, ::way], g_a[r, ::way], g_a[r, ::way], LOWEST,
                                                ALU.max, ALU.max))
                link(dve.tensor_scalar(g_nm, g_m, -1.0, None, ALU.mult))
                dve.tensor_tensor(g_mt, g_b, g_m, ALU.add).then_inc(g_rows, 1)

            def na_scores(h):
                b = USES[("na_scores", h)][0]
                wait_filled(dve, "na_scores", h)
                if h == 0:
                    dve.wait_ge(bias_ok, 4)
                if h >= 2:
                    wait_filled(dve, "na_turn", h - 2)
                for n in range(NT):
                    first = 2 * (NT - 1 - n)
                    ins = dve.scalar_tensor_tensor(
                        na_p[:, h % 2, n, :], mix[:, b, n * T:(n + 1) * T], NA_SCALE,
                        bias[:, h, first:first + ROWS, :].rearrange("p j c -> p (j c)"), ALU.mult, ALU.add)
                ins.then_inc(read[b], 1)
                wait_read(dve, "na_scores", h)
                dve.tensor_reduce(na_max[:, h % 2, :], na_p[:, h % 2, :, :], AX_X, ALU.max,
                                  negate=True).then_inc(na_soft, 1)

            def na_probabilities(h):
                dve.wait_ge(na_exp, h + 1)
                s = na_sum[:, h % 2, :]
                link(dve.reciprocal(s, s))
                for n in range(NT):
                    ins = dve.tensor_scalar(na_p[:, h % 2, n, :], na_p[:, h % 2, n, :], na_sum[:, h % 2, n:n + 1],
                                            None, ALU.mult)
                ins.then_inc(na_prob, 1)

            def conv(i, taps):
                if i % 4 == 0 and taps[0] == 0:
                    wait_group_read(dve, G_ML + i // 4)
                for w in taps:
                    if w:
                        dve.wait_ge(conv_tap, 5 * i + 2 * w)
                    for k in (i, i + 1):
                        c = COL_CONV_W + 8 * w + k
                        out_, in_, tap = conv_out[:, k, :], conv_in[:, k, w:w + T], cols[:, c:c + 1]
                        if w == 0:
                            ins = dve.tensor_scalar(out_, in_, tap, cols[:, COL_CONV_B + k:COL_CONV_B + k + 1],
                                                    ALU.mult, ALU.add)
                        else:
                            ins = dve.scalar_tensor_tensor(out_, in_, tap, out_, ALU.mult, ALU.add)
                        ins.then_inc(conv_tap, 1)

            def silu(i):
                dve.wait_ge(conv_th, i + 1)
                part = conv_out[:, 4 * i:4 * i + 4, :].rearrange("p k t -> p (k t)")
                dve.scalar_tensor_tensor(part, wide_flat, 1.0, part, ALU.add, ALU.mult).then_inc(conv_silu, 1)

            def rotary(g, n):
                i = g - G_ROT
                wait_group(dve, g)
                if (i, n) == (0, 0):
                    dve.wait_ge(conv_silu, 2)
                src = pair(g)[:, n, :].rearrange("p (h d) -> p h d", d=DK)
                by = [w[:, n, :].rearrange("p (a d) -> p a d", a=1).to_broadcast([P, RET_HEADS, DK])
                      for w in (cos, sin)]
                xc, xs = (wide[:, j, :].rearrange("p (h d) -> p h d", d=DK) for j in range(2))
                dve.tensor_tensor(xc, src, by[0], ALU.mult)
                ins = dve.tensor_tensor(xs, src, by[1], ALU.mult)
                if n == NT - 1:
                    ins.then_inc(acc_read[g % 2], 1)
                    wait_group_read(dve, g)
                else:
                    link(ins)
                dst = rot[:, n, i, :, :]
                dve.tensor_tensor(dst[:, :, 0:64], xc[:, :, 0:64], xs[:, :, 64:128], ALU.subtract)
                dve.tensor_tensor(dst[:, :, 64:128], xc[:, :, 64:128], xs[:, :, 0:64], ALU.add).then_inc(rot_ok, 1)
                dve.wait_ge(rot_ok, 2 * i + n + 1)

            def decay_exponents(h):
                if h == 0:
                    dve.wait_ge(dist_in, 16)
                link(dve.tensor_scalar(decay[:, h, :, :], dist[:, 1, :, :], lg[:, RET_HEADS + h:RET_HEADS + h + 1],
                                       None, ALU.mult))
                dve.scalar_tensor_tensor(decay[:, h, :, :], dist[:, 0, :, :], lg[:, h:h + 1], decay[:, h, :, :],
                                         ALU.mult, ALU.add).then_inc(decay_arg, 1)

            def ml_weights(h):
                b = USES[("ml_scores", h)][0]
                wait_filled(dve, "ml_scores", h)
                for d, j, t0, t1 in ((0, 0, 0, T), (0, 1, P, T), (1, 0, 0, P), (1, 1, 0, T)):
                    dve.wait_ge(ml_mask, 4 * h + 2 * d + j + 1)
                    ins = dve.scalar_tensor_tensor(ml_w[:, d, j, t0:t1], mix[:, b, j * T + t0:j * T + t1],
                                                   QK_SCALE / 4, ml_e[:, d, j, t0:t1], ALU.mult, ALU.mult)
                    if j == 1:
                        ins.then_inc(ml_wt, 1)
                dve.wait_ge(ml_wt, 2 * h + 2)
                dve.sem_inc(read[b], 1)

            def ml_out(h, d):
                for n in range(NT):
                    wait_filled(dve, "ml_values", h, d, n)
                r = 32 * d + h
                link(dve.tensor_tensor(rden[:, d, :], mix[:, 2:4, DV], emt[:, :, r], ALU.max))
                link(dve.scalar_tensor_tensor(den[:, d, :], mix[:, 2:4, DV], -1.0, rden[:, d, :],
                                              ALU.mult, ALU.max))
                link(dve.reciprocal(rden[:, d, :], den[:, d, :]))
                for n in range(NT):
                    b = USES[("ml_values", h, d, n)][0]
                    dst = h_ml[:, n, h * DV:(h + 1) * DV]
                    if d == 0:
                        ins = dve.tensor_scalar(dst, mix[:, b, 0:DV], rden[:, d, n:n + 1], None, ALU.mult)
                    else:
                        ins = dve.scalar_tensor_tensor(dst, mix[:, b, 0:DV], rden[:, d, n:n + 1], dst,
                                                       ALU.mult, ALU.add)
                    ins.then_inc(read[b], 1)

            def head_stats(y, heads, last):
                for n in range(NT):
                    for h in heads:
                        ins = dve.bn_stats(bn[:, 4 * n + h, :], y[:, n, h * DV:(h + 1) * DV])
                link(ins)
                if not last:
                    return
                for k in range(8):
                    ins = dve.bn_aggr(mean_var[:, k, :], bn[:, k, :])
                ins.then_inc(bn_ok, 1)

            def head_norm(i, y, n):
                dve.wait_ge(rs_ok, i + 1)
                for h in range(4):
                    k, part = 4 * n + h, y[:, n, h * DV:(h + 1) * DV]
                    ins = dve.tensor_scalar(part, part, mean_var[:, k, 0:1], rs8[:, k:k + 1],
                                            ALU.subtract, ALU.mult)
                link(ins)

            def group(g):
                part = IN_GROUPS[g][0]
                c = slice((g % 2) * N512, (g % 2 + 1) * N512)
                if part == "rg":
                    dve.wait_ge(rg_th, g - G_RG + 1)
                    dve.scalar_tensor_tensor(rgs[:, :, c], wide[:], 1.0, pair(g), ALU.add,
                                             ALU.mult).then_inc(acc_read[g % 2], 1)
                elif part == "mo":
                    wait_group_read(dve, g)
                    dve.scalar_tensor_tensor(h_ml[:, :, c], wide[:], 1.0, h_ml[:, :, c], ALU.add,
                                             ALU.mult).then_inc(y_ok, 1)
                elif part == "mix":
                    j = g - G_MIX
                    wait_group(dve, g)
                    dve.wait_ge(gate_row_in[j % 2], 16 * (j // 2 + 1))
                    dve.tensor_tensor(mixg[:, :, j * N512:(j + 1) * N512], pair(g),
                                      gate_row[:, j % 2:j % 2 + 1, :].to_broadcast([P, NT, N512]),
                                      ALU.add).then_inc(acc_read[g % 2], 1)

            def project(g):
                i = (g - G_PROJ) // 2
                c0 = GATE_OF[BRANCHES[i]] * D + (g % 2) * N512
                total = tok[:, :, (g % 2) * N512:(g % 2 + 1) * N512]
                wait_group(dve, g)
                if g == G_PROJ:
                    dve.wait_ge(mix_th, 6)
                dve.scalar_tensor_tensor(total if i == 0 else wide[:], mixg[:, :, c0:c0 + N512], 1.0, pair(g),
                                         ALU.add, ALU.mult).then_inc(acc_read[g % 2], 1)
                wait_group_read(dve, g)
                if i:
                    dve.tensor_tensor(total, total, wide[:], ALU.add).then_inc(branch_sum, 1)
                    dve.wait_ge(branch_sum, g - G_PROJ + 1)
                else:
                    dve.sem_inc(branch_sum, 1)

            def mixer(step):
                what, i = step[0], step[1] if len(step) > 1 else None
                if what == "gate_rows":
                    gate_rows()
                elif what == "gate_sums":
                    gate_sums()
                elif what == "gate_maxima":
                    gate_maxima()
                elif what == "na_scores":
                    na_scores(i)
                elif what == "na_prob":
                    na_probabilities(i)
                elif what == "na_values":
                    b = USES[("na_values", i)][0]
                    low_part(turned_lo[:, 1, i, :], mix[:, b, 0:T], 1.0, turned_hi[:, 1, i, :]).then_inc(read[b], 1)
                elif what == "ml_scores":
                    ml_weights(i)
                elif what == "ml_values":
                    ml_out(i, step[2])
                elif what == "ret_scores":
                    b = USES[("ret_scores", i)][0]
                    wait_filled(dve, "ret_scores", i)
                    if i == 0:
                        dve.wait_ge(decay_ok, 1)
                    dve.scalar_tensor_tensor(ret_p[:, i % 2, :, :], mix[:, b, :].rearrange("p (j t) -> p j t", j=NT),
                                             QK_SCALE, decay[:, i, :, :], ALU.mult, ALU.mult).then_inc(ret_wt, 1)
                    dve.wait_ge(ret_wt, i + 1)
                    dve.sem_inc(read[b], 1)
                elif what == "turn" and i != "rot":
                    turned_banks(i, step[2])
                elif what == "up_turn":
                    b = USES[("up_turn", i)][0]
                    low_part(up_lo[:, i % 2, :, :], mix[:, b, :].rearrange("p (k t) -> p k t", k=2), 1.0,
                             up_hi[:, i % 2, :, :]).then_inc(read[b], 1)

            normalise()
            dve.wait_ge(fixed_ok, 5)
            dve.wait_ge(pre_turn, 1)
            dve.tensor_copy(cols_all[:], mix[:, 0, 0:DEPTH * N_COLS]).then_inc(pre_cols, 1)
            dve.wait_ge(pre_cols, 1)
            for l in range(DEPTH):
                part = cols_all[:, l * N_COLS + COL_ML:l * N_COLS + COL_ML + 8]
                dve.tensor_scalar(part, part, 0.5, None, ALU.mult).then_inc(pre_cols, 1)
            dve.wait_ge(pre_cols, 3)

            with dve.Fori(0, DEPTH) as l:
                dve.tensor_copy(cols[:], cols_all[:, bass.ds(l * N_COLS, N_COLS)]).then_inc(cols_ok, 1)
                split(1)
                turned_banks("norm1", 0)
                split(2)
                turned_banks("norm1", 1)
                dve.wait_ge(params_in, 16 * 7)
                dve.wait_ge(consts_in, 16 * 4)
                dve.tensor_copy(gbias[:], gbias_all[:, bass.ds(l * 2, 2)])
                link(dve.tensor_copy(lg, lg_logits[:, bass.ds(l * 8, 8)]))
                dve.wait_ge(gate_hi_ok, 1)
                dve.tensor_tensor(gate_w[:, :, 16:32], gate_w_all[:, bass.ds(l * (KD * 16), KD * 16)].rearrange(
                    "p (k c) -> p k c", k=KD), gate_w[:, :, 0:16].bitcast(F32), ALU.subtract).then_inc(gate_lo_ok, 1)
                for v, (kind, g, i) in enumerate(UNITS):
                    split(v + 3)
                    slot = (v - 1) // 2 if v % 2 else -1
                    if kind == "w" and i == UPG - 1:
                        if g < G_PROJ:
                            group(g)
                        elif g < G_OUT:
                            project(g)
                        else:
                            wait_group(dve, g)
                            part = x[:, :, (g % 2) * N512:(g % 2 + 1) * N512]
                            dve.tensor_tensor(part, part, pair(g), ALU.add).then_inc(acc_read[g % 2], 1)
                            wait_group_read(dve, g)
                            dve.sem_inc(x_ok, 1)
                    if kind == "up" and i == UPG - 1:
                        dve.wait_ge(up_tanh, g + 1)
                        if g >= 2:
                            wait_filled(dve, "up_turn", g - 2)
                        if g == 0:
                            dve.wait_ge(half_rstd_ok, 2)
                        a, b = up_banks(g)
                        link(dve.scalar_tensor_tensor(up_s, up_th[:, g % 2, :, :], 1.0, mix[:, a:b + 1, 0:256],
                                                      ALU.add, ALU.mult))
                        for n in range(NT):
                            ins = dve.scalar_tensor_tensor(up_v[:, g % 2, n, :], up_s[:, n, :], half_rstd2[:, n:n + 1],
                                                           mix[:, a + n, 256:512], ALU.mult, ALU.mult)
                        ins.then_inc(up_v_ok, 1)
                        dve.wait_ge(up_v_ok, g + 1)
                        dve.sem_inc(read[a], 1)
                        dve.sem_inc(read[b], 1)
                    if V_CONV <= v < V_CONV + 16 and v % 2 == 0:
                        j = (v - V_CONV) // 2
                        conv(j // 2 * 2, (range(3), range(3, CONV_W))[j % 2])
                    if v in V_SILU:
                        silu(V_SILU.index(v))
                    if v in V_ROTARY:
                        j = V_ROTARY.index(v)
                        rotary(G_ROT + j // 2, j % 2)
                    if 28 <= slot < 32:
                        decay_exponents(slot - 28)
                    for step in MIXER.get(v, []):
                        mixer(step)
                    after_ml, after_ret = v - (2 * (S_ML + 2 * ML_HEADS) + 1), v - (2 * (S_RET + 1 + RET_HEADS) + 1)
                    if after_ml == 0:
                        for n in range(NT):
                            wait_read(dve, "ml_values", ML_HEADS - 1, 1, n)
                        head_stats(h_ml, range(0, 2), False)
                    elif after_ml == 1:
                        head_stats(h_ml, range(2, 4), True)
                    elif after_ml in (2, 3):
                        head_norm(0, h_ml, after_ml - 2)
                    if after_ret == -2:
                        for h in range(2):
                            wait_read(dve, "ret_values", h)
                        head_stats(o_ret, range(0, 2), False)
                    elif after_ret == 0:
                        for h in range(2, RET_HEADS):
                            wait_read(dve, "ret_values", h)
                        head_stats(o_ret, range(2, 4), True)
                    elif after_ret in (2, 3):
                        head_norm(1, o_ret, after_ret - 2)
                    n = v - last_of(G_RG + 1) - 2
                    if n in range(NT):
                        wait_group_read(dve, G_RG)
                        wait_group_read(dve, G_RG + 1)
                        dve.scalar_tensor_tensor(o_ret[:, n, :], o_ret[:, n, :], 0.5, rgs[:, n, :],
                                                 ALU.mult, ALU.mult).then_inc(y_ok, 1)
                arrive(dve)
                for n in range(NT):
                    for b in range(2):
                        dve.wait_ge(bank_done, 2 * n + b + 1)
                        part = x[:, n, b * N512:(b + 1) * N512]
                        dve.tensor_tensor(part, part, acc[:, 2 * n + b, :], ALU.add).then_inc(x_next, 1)
                dve.sem_clear(bank_done)
                normalise()
                next_layer(dve, "dve")

            for n in range(NT):
                dve.wait_ge(xs_ok, n + 1)
                for b in range(2):
                    part = tok[:, n, b * N512:(b + 1) * N512]
                    dve.tensor_tensor(part, part, raw[:, RAW - 1, b, :], ALU.mult).then_inc(fin_y, 1)


def shape_constants():
    ident = np.eye(P, dtype=np.float32)
    half = DK // 2
    inv_freq = np.float32(10000.0) ** (-np.arange(half, dtype=np.float32) / half)
    angle = np.arange(T, dtype=np.float32)[:, None] * inv_freq.astype(np.float32)[None, :]
    cos = np.tile(np.cos(angle), (1, 2)).astype(np.float32)
    sin = np.tile(np.sin(angle), (1, 2)).astype(np.float32)
    m = np.arange(T).reshape(NT, P).T[:, :, None]
    n = np.arange(T)[None, None, :]
    dist = np.stack([np.maximum(n - m, 0), np.maximum(m - n, 0)], 1).astype(np.float32).reshape(P, 2, NT * T)
    col = np.arange(GRID_W)
    first = np.clip(col - WIN_COLS // 2, 0, GRID_W - WIN_COLS)
    inside = (col[None, :] >= first[:, None]) & (col[None, :] < first[:, None] + WIN_COLS)
    window = np.tile(np.where(inside, 0.0, -1.0e30), (2, 1)).astype(np.float32)
    spread = np.zeros((2, 16, 2, 64), np.float32)
    for d in range(2):
        for i in range(2):
            for h in range(ML_HEADS):
                spread[:, 8 * d + 4 * i + h, i, 32 * d + h] = 1.0
    return {"c_ident": ident, "c_cos": cos, "c_sin": sin, "c_dist": dist, "c_window": window,
            "c_spread": spread.reshape(32, 2, 64)}


def lay_out_bias(rpb):
    r, qc = np.arange(P) // GRID_W, np.arange(P) % GRID_W
    rows = np.arange(1, 7)[None, :] - r[:, None] - 3 + WIN_ROWS - 1
    rel = np.clip(np.arange(GRID_W)[None, :] - qc[:, None] + WIN_COLS - 1, 0, 2 * WIN_COLS - 2)
    picked = rpb[:, :, rows[:, :, None], rel[:, None, :]]
    return np.ascontiguousarray(picked.transpose(0, 2, 1, 3, 4)).reshape(rpb.shape[0], P, NA_HEADS * 6 * GRID_W)


_INS = ["x", "norm1_g", "w_in", "gate_b", "ret_decay_logit", "na_rpb", "ml_conv_w", "ml_conv_b", "ml_gate_b",
        "ml_norm_g", "w_ret_o", "w_na_o", "w_ml_o", "w_out", "norm2_g", "w_ffn_up", "w_ffn_down", "final_g"]


def kernel(**inputs):
    import concourse.bacc as bacc
    from concourse.bass_utils import run_bass_kernel_spmd

    nc = bacc.Bacc("TRN2", target_bir_lowering=False, num_devices=1)
    laid_out = {n: np.ascontiguousarray(inputs[n]) for n in _INS}
    laid_out["na_rpb"] = lay_out_bias(laid_out["na_rpb"])
    laid_out.update(shape_constants())
    arrays, args = {}, []
    for name, a in laid_out.items():
        arrays[f"in_{name}"] = a
        args.append(nc.dram_tensor(f"in_{name}", a.shape, mybir.dt.from_np(a.dtype), kind="ExternalInput").ap())
    args.append(nc.dram_tensor("out_0", (1, T, D), F32, kind="ExternalOutput").ap())
    trunk(nc, *args)
    r = run_bass_kernel_spmd(nc, [arrays], core_ids=[0])
    return r.results[0]["out_0"]
```
